# Optimizing a Trainium2 kernel written in Bass

```python
import jax, jax.numpy as jnp
from jax import lax
import numpy as np

D_MODEL = 1024
BATCH = 1
SEQ = 512
DEPTH = 1
DEC_BATCH = 1
DEC_SEQ = 32
PAST_LEN = 256

CHUNK = 64
N_META = 16
ROPE_THETA = 500000.0
EPS = 1e-6
QBLOCK = 128

A_HEADS = 8
A_NOPE = 64
A_ROPE = 32
A_V = 64
A_QRANK = 256
A_KVRANK = 128
A_SCALE = (A_NOPE + A_ROPE) ** -0.5

B_HEADS = 8
B_HEAD_DIM = 64
B_ROT = B_HEAD_DIM // 4
B_SCALE = B_HEAD_DIM ** -0.5
IDX_HEADS = 8
IDX_DIM = 64
IDX_ROT = IDX_DIM // 4
IDX_TOPK = 256
IDX_W_SCALE = (IDX_HEADS * IDX_DIM) ** -0.5

PEER_HEADS = 8
PEER_DKEY = 128
N_KEYS = 128
N_EXPERTS = N_KEYS * N_KEYS
PEER_TOPK = 16
PEER_BLOCK = 256

IN_SPLITS = (A_QRANK, A_KVRANK, A_ROPE, B_HEADS * B_HEAD_DIM, B_HEAD_DIM, B_HEAD_DIM,
             IDX_HEADS * IDX_DIM, IDX_HEADS, IDX_DIM, D_MODEL, D_MODEL)
IN_COLS = A_QRANK + A_KVRANK + A_ROPE + B_HEADS * B_HEAD_DIM + 2 * B_HEAD_DIM + IDX_HEADS * IDX_DIM + IDX_HEADS + IDX_DIM + 2 * D_MODEL

kernel_name = 'hybrid_mla_dsa_peer_stream_step'

def _rms(x, g):
    xf = x.astype(jnp.float32)
    y = xf * lax.rsqrt(jnp.mean(xf * xf, axis=-1, keepdims=True) + EPS)
    return (y * g.astype(jnp.float32)).astype(x.dtype)

def _rotary(x, pos, rot_dim):
    half = rot_dim // 2
    inv = ROPE_THETA ** (-jnp.arange(half, dtype=jnp.float32) * (2.0 / rot_dim))
    ang = pos.astype(jnp.float32)[:, None] * inv[None, :]
    shp = (pos.shape[0],) + (1,) * (x.ndim - 3) + (half,)
    cos = jnp.cos(ang).reshape(shp)
    sin = jnp.sin(ang).reshape(shp)
    xf = x[..., :rot_dim].astype(jnp.float32)
    x1, x2 = xf[..., :half], xf[..., half:]
    rot = jnp.concatenate([x1 * cos - x2 * sin, x2 * cos + x1 * sin], axis=-1).astype(x.dtype)
    return jnp.concatenate([rot, x[..., rot_dim:]], axis=-1)

def _query_blocks(fn, q_arrays, q_chunk):
    T = q_chunk.shape[0]
    blk = min(QBLOCK, T)
    nb = -(-T // blk)
    pad = nb * blk - T

    def to_blocks(a):
        a = jnp.pad(a, [(0, 0), (0, pad)] + [(0, 0)] * (a.ndim - 2))
        a = a.reshape((a.shape[0], nb, blk) + a.shape[2:])
        return jnp.moveaxis(a, 1, 0)

    qc = jnp.pad(q_chunk, (0, pad), mode='edge').reshape(nb, blk)
    out = lax.map(lambda args: fn(*args), tuple(to_blocks(a) for a in q_arrays) + (qc,))
    out = jnp.moveaxis(out, 0, 1)
    out = out.reshape((out.shape[0], nb * blk) + out.shape[3:])
    return out[:, :T]

def _token_mixers(h, pos, q_chunk, k_chunk, k_sel, past, w_in, a_q_norm_g, a_kv_norm_g,
                  a_w_uq, a_w_ukv, a_qk_g, b_qk_g, w_o_a, w_o_b, w_out):
    Bn, T = h.shape[0], h.shape[1]
    offs = np.cumsum(IN_SPLITS)[:-1].tolist()
    cq, ckv, kpe, bq, bk, bv, iq, iw, ik, ga, gb = jnp.split(h @ w_in, offs, axis=-1)
    cq = _rms(cq, a_q_norm_g)
    ckv = _rms(ckv, a_kv_norm_g)
    q = (cq @ a_w_uq).reshape(Bn, T, A_HEADS, A_NOPE + A_ROPE)
    qn = _rms(q[..., :A_NOPE], a_qk_g[0, :A_NOPE])
    qp = _rotary(_rms(q[..., A_NOPE:], a_qk_g[0, A_NOPE:]), pos, A_ROPE)
    kpe = _rotary(_rms(kpe, a_qk_g[1, A_NOPE:]), pos, A_ROPE)
    bq = _rotary(_rms(bq.reshape(Bn, T, B_HEADS, B_HEAD_DIM), b_qk_g[0]), pos, B_ROT)
    bk = _rotary(_rms(bk, b_qk_g[1]), pos, B_ROT)
    iq = _rotary(iq.reshape(Bn, T, IDX_HEADS, IDX_DIM), pos, IDX_ROT)
    ik = _rotary(ik, pos, IDX_ROT)
    iw = iw * IDX_W_SCALE
    new_rows = (ckv, kpe, bk, bv, ik)

    if past is None:
        lat_all, kpe_all, bk_all, bv_all, ik_all = new_rows
    else:
        lat_all, kpe_all, bk_all, bv_all, ik_all = tuple(
            jnp.concatenate([c.astype(n.dtype), n], axis=1) for c, n in zip(past, new_rows))
    S = lat_all.shape[1]
    kv = (lat_all @ a_w_ukv).reshape(Bn, S, A_HEADS, A_NOPE + A_V)
    kn = _rms(kv[..., :A_NOPE], a_qk_g[1, :A_NOPE])
    va = kv[..., A_NOPE:]

    def mla_block(qn_b, qp_b, qc):
        mask = k_chunk[None, :] <= qc[:, None]
        s = (jnp.einsum('bqhd,bshd->bhqs', qn_b, kn)
             + jnp.einsum('bqhr,bsr->bhqs', qp_b, kpe_all)).astype(jnp.float32) * A_SCALE
        p = jax.nn.softmax(jnp.where(mask, s, -jnp.inf), axis=-1).astype(va.dtype)
        return jnp.einsum('bhqs,bshd->bqhd', p, va)

    def dsa_block(bq_b, iq_b, iw_b, qc):
        blk = qc.shape[0]
        mask = k_chunk[None, :] <= qc[:, None]
        rel = jax.nn.relu(jnp.einsum('bqhd,bsd->bqhs', iq_b, ik_all).astype(jnp.float32))
        score = jnp.einsum('bqh,bqhs->bqs', iw_b.astype(jnp.float32), rel)
        _, sel = lax.top_k(jnp.where(mask, score, -jnp.inf), k_sel)
        gk = jax.vmap(lambda t, i: t[i])(bk_all, sel)
        gv = jax.vmap(lambda t, i: t[i])(bv_all, sel)
        valid = mask[jnp.arange(blk)[None, :, None], sel]
        logit = jnp.einsum('bqhd,bqkd->bqhk', bq_b, gk).astype(jnp.float32) * B_SCALE
        p = jax.nn.softmax(jnp.where(valid[:, :, None, :], logit, -jnp.inf), axis=-1).astype(gv.dtype)
        return jnp.einsum('bqhk,bqkd->bqhd', p, gv)

    o_a = _query_blocks(mla_block, (qn, qp), q_chunk).reshape(Bn, T, A_HEADS * A_V)
    o_b = _query_blocks(dsa_block, (bq, iq, iw), q_chunk).reshape(Bn, T, B_HEADS * B_HEAD_DIM)
    merged = jax.nn.sigmoid(ga) * (o_a @ w_o_a) + jax.nn.sigmoid(gb) * (o_b @ w_o_b)
    return merged @ w_out, new_rows

def _peer(h, wq, subkeys, u, v):
    shape = h.shape
    flat = h.reshape(-1, D_MODEL)
    N = flat.shape[0]
    blk = min(PEER_BLOCK, N)
    nb = -(-N // blk)
    blocks = jnp.pad(flat, ((0, nb * blk - N), (0, 0))).reshape(nb, blk, D_MODEL)
    half = PEER_DKEY // 2

    def fn(t):
        q = (t @ wq).reshape(blk, PEER_HEADS, PEER_DKEY)
        s1 = jnp.einsum('thd,hnd->thn', q[..., :half], subkeys[:, 0]).astype(jnp.float32)
        s2 = jnp.einsum('thd,hnd->thn', q[..., half:], subkeys[:, 1]).astype(jnp.float32)
        v1, i1 = lax.top_k(s1, PEER_TOPK)
        v2, i2 = lax.top_k(s2, PEER_TOPK)
        cand = (v1[..., :, None] + v2[..., None, :]).reshape(blk, PEER_HEADS, PEER_TOPK * PEER_TOPK)
        sc, pos = lax.top_k(cand, PEER_TOPK)
        e = (jnp.take_along_axis(i1, pos // PEER_TOPK, axis=-1) * N_KEYS
             + jnp.take_along_axis(i2, pos % PEER_TOPK, axis=-1))
        g = jax.nn.softmax(sc, axis=-1)
        a = jax.nn.gelu(jnp.einsum('td,thkd->thk', t, u[e]))
        return jnp.einsum('thk,thkd->td', (g * a.astype(jnp.float32)).astype(t.dtype), v[e])

    out = lax.map(fn, blocks).reshape(nb * blk, D_MODEL)[:N]
    return out.reshape(shape)

def _layer(x, pos, q_chunk, k_chunk, k_sel, past, ln1_g, w_in, a_q_norm_g, a_kv_norm_g, a_w_uq,
           a_w_ukv, a_qk_g, b_qk_g, w_o_a, w_o_b, w_out, ln2_g, peer_wq, peer_subkeys, peer_u, peer_v):
    out, rows = _token_mixers(_rms(x, ln1_g), pos, q_chunk, k_chunk, k_sel, past, w_in, a_q_norm_g,
                              a_kv_norm_g, a_w_uq, a_w_ukv, a_qk_g, b_qk_g, w_o_a, w_o_b, w_out)
    x = x + out
    x = x + _peer(_rms(x, ln2_g), peer_wq, peer_subkeys, peer_u, peer_v)
    return x, rows

def setup_inputs(seed: int = 0) -> dict:
    key = jax.random.key(seed)
    ks = jax.random.split(key, 24)
    f32 = jnp.float32
    nrm = lambda k, shp, sc: jax.random.normal(k, shp, f32) * sc
    gain = lambda k, shp: 1.0 + 0.02 * jax.random.normal(k, shp, f32)
    return {
        'x_prompt': nrm(ks[0], (BATCH, SEQ, D_MODEL), 1.0),
        'x_sample': nrm(ks[1], (DEC_BATCH, DEC_SEQ, D_MODEL), 1.0),
        'cache_a_latent': nrm(ks[2], (DEPTH, DEC_BATCH, PAST_LEN, A_KVRANK), 1.0),
        'cache_a_kpe': nrm(ks[3], (DEPTH, DEC_BATCH, PAST_LEN, A_ROPE), 1.0),
        'cache_b_k': nrm(ks[4], (DEPTH, DEC_BATCH, PAST_LEN, B_HEAD_DIM), 1.0),
        'cache_b_v': nrm(ks[5], (DEPTH, DEC_BATCH, PAST_LEN, B_HEAD_DIM), 1.0),
        'cache_b_idx_k': nrm(ks[6], (DEPTH, DEC_BATCH, PAST_LEN, IDX_DIM), 1.0),
        'meta_tokens': nrm(ks[7], (N_META, D_MODEL), 1.0),
        'ln1_g': gain(ks[8], (DEPTH, D_MODEL)),
        'w_in': nrm(ks[9], (DEPTH, D_MODEL, IN_COLS), D_MODEL ** -0.5),
        'a_q_norm_g': gain(ks[10], (DEPTH, A_QRANK)),
        'a_kv_norm_g': gain(ks[11], (DEPTH, A_KVRANK)),
        'a_w_uq': nrm(ks[12], (DEPTH, A_QRANK, A_HEADS * (A_NOPE + A_ROPE)), A_QRANK ** -0.5),
        'a_w_ukv': nrm(ks[13], (DEPTH, A_KVRANK, A_HEADS * (A_NOPE + A_V)), A_KVRANK ** -0.5),
        'a_qk_g': gain(ks[14], (DEPTH, 2, A_NOPE + A_ROPE)),
        'b_qk_g': gain(ks[15], (DEPTH, 2, B_HEAD_DIM)),
        'w_o_a': nrm(ks[16], (DEPTH, A_HEADS * A_V, D_MODEL), (A_HEADS * A_V) ** -0.5),
        'w_o_b': nrm(ks[17], (DEPTH, B_HEADS * B_HEAD_DIM, D_MODEL), (B_HEADS * B_HEAD_DIM) ** -0.5),
        'w_out': nrm(ks[18], (DEPTH, D_MODEL, D_MODEL), D_MODEL ** -0.5),
        'ln2_g': gain(ks[19], (DEPTH, D_MODEL)),
        'peer_wq': nrm(ks[20], (DEPTH, D_MODEL, PEER_HEADS * PEER_DKEY), D_MODEL ** -0.5),
        'peer_subkeys': nrm(ks[21], (DEPTH, PEER_HEADS, 2, N_KEYS, PEER_DKEY // 2), (PEER_DKEY // 2) ** -0.5),
        'peer_u': nrm(ks[22], (DEPTH, N_EXPERTS, D_MODEL), D_MODEL ** -0.5),
        'peer_v': nrm(ks[23], (DEPTH, N_EXPERTS, D_MODEL), 0.5),
    }

def reference(x_prompt, x_sample, cache_a_latent, cache_a_kpe, cache_b_k, cache_b_v, cache_b_idx_k,
              meta_tokens, ln1_g, w_in, a_q_norm_g, a_kv_norm_g, a_w_uq, a_w_ukv, a_qk_g, b_qk_g,
              w_o_a, w_o_b, w_out, ln2_g, peer_wq, peer_subkeys, peer_u, peer_v):
    Bp, Sp = x_prompt.shape[0], x_prompt.shape[1]
    Tp = N_META + Sp
    meta = jnp.broadcast_to(meta_tokens.astype(x_prompt.dtype)[None], (Bp, N_META, D_MODEL))
    xp = jnp.concatenate([meta, x_prompt], axis=1)
    pos_p = jnp.arange(Tp, dtype=jnp.int32)
    chunk_p = jnp.where(pos_p < N_META, -1, (pos_p - N_META) // CHUNK)
    k_sel_p = min(IDX_TOPK, Sp // 4)
    Ts = x_sample.shape[1]
    P = cache_a_latent.shape[2]
    xs = x_sample
    pos_s = P + jnp.arange(Ts, dtype=jnp.int32)
    q_chunk_s = jnp.ones((Ts,), jnp.int32)
    k_chunk_s = jnp.concatenate([jnp.zeros((P,), jnp.int32), jnp.ones((Ts,), jnp.int32)])
    k_sel_s = min(IDX_TOPK, (P + Ts) // 4)

    rows_p, rows_s = [], []
    for l in range(DEPTH):
        lw = (ln1_g[l], w_in[l], a_q_norm_g[l], a_kv_norm_g[l], a_w_uq[l], a_w_ukv[l], a_qk_g[l],
              b_qk_g[l], w_o_a[l], w_o_b[l], w_out[l], ln2_g[l], peer_wq[l], peer_subkeys[l],
              peer_u[l], peer_v[l])
        xp, rp = _layer(xp, pos_p, chunk_p, chunk_p, k_sel_p, None, *lw)
        past = (cache_a_latent[l], cache_a_kpe[l], cache_b_k[l], cache_b_v[l], cache_b_idx_k[l])
        xs, rs = _layer(xs, pos_s, q_chunk_s, k_chunk_s, k_sel_s, past, *lw)
        rows_p.append(rp)
        rows_s.append(rs)

    new_a_latent_p = jnp.stack([r[0] for r in rows_p])
    new_a_kpe_p = jnp.stack([r[1] for r in rows_p])
    new_b_k_p = jnp.stack([r[2] for r in rows_p])
    new_b_v_p = jnp.stack([r[3] for r in rows_p])
    new_b_idx_k_p = jnp.stack([r[4] for r in rows_p])
    new_a_latent_s = jnp.stack([r[0] for r in rows_s])
    new_a_kpe_s = jnp.stack([r[1] for r in rows_s])
    new_b_k_s = jnp.stack([r[2] for r in rows_s])
    new_b_v_s = jnp.stack([r[3] for r in rows_s])
    new_b_idx_k_s = jnp.stack([r[4] for r in rows_s])
    y_prompt = xp[:, N_META:]
    y_sample = xs
    return (y_prompt, y_sample, new_a_latent_p, new_a_kpe_p, new_b_k_p, new_b_v_p, new_b_idx_k_p,
            new_a_latent_s, new_a_kpe_s, new_b_k_s, new_b_v_s, new_b_idx_k_s)


_drawn_inputs = setup_inputs


def setup_inputs(seed=0):
    import zlib

    import numpy as np

    out = dict(_drawn_inputs(seed))
    spreads = {}
    factors = {'a_q_norm_g': 5.447, 'a_qk_g': 3.4, 'b_qk_g': 2.724}
    for name, (base, spread) in spreads.items():
        noise = np.random.default_rng([zlib.crc32(name.encode()), seed]).standard_normal(out[name].shape)
        drawn = base * np.exp(spread * noise) if base else spread * noise
        out[name] = __import__('jax').numpy.asarray(drawn.astype(out[name].dtype))
    for name, factor in factors.items():
        out[name] = (out[name] * factor).astype(out[name].dtype)
    return out
```

```python
import numpy as np
import concourse.bass as bass
from concourse import mybir

F32 = mybir.dt.float32
U32 = mybir.dt.uint32
ALU = mybir.AluOpType
ACT = mybir.ActivationFunctionType
AX_X = mybir.AxisListType.X

P = 128
D = 1024
DC = D // P
SEQ, DEC, META, PAST = 512, 32, 16, 256
TOK = SEQ + DEC + META
NQ = SEQ + DEC
NT = 5
KEYS = META + SEQ + PAST + DEC
KPROMPT = META + SEQ
KCACHE = KPROMPT
KSAMPLE = KPROMPT + PAST
CHUNK = 64
EPS = 1e-6
THETA = 500000.0

H = 8
NOPE, ROPE, AV = 64, 32, 64
AQK = NOPE + ROPE
QRANK, KVRANK = 256, 128
HD = 64
BROT = HD // 4
A_SCALE = AQK ** -0.5
B_SCALE = HD ** -0.5
IDX_SCALE = (H * HD) ** -0.5
TOPK_P = min(256, SEQ // 4)
TOPK_S = min(256, (PAST + DEC) // 4)

C_KV = QRANK
C_KPE = C_KV + KVRANK
C_B = C_KPE + ROPE
NPAIR = H + 1
C_BV = C_B + NPAIR * 2 * HD
C_IW = C_BV + HD
COLS = C_IW + H
PJ = COLS // 4
assert PJ * 4 == COLS and PJ <= 512

NKEY = 128
PH = 8
TOPE = 16
SLOTS = PH * TOPE
HALF = NQ // 2
HIDE = -1e30
NEG = -3.0e38
TAKEN = -3.3e38
SEEN = -3.2e38

GAINS = KVRANK + ROPE + NPAIR * HD + AQK + NOPE
G_KPE = KVRANK
G_B = G_KPE + ROPE
G_Q = G_B + NPAIR * HD
G_KN = G_Q + AQK
TABS = 2 * ROPE + 2 * BROT


def rows_of(t):
    return P if t < 4 else DEC + META


def queries_of(t):
    return P if t < 4 else DEC


def key_columns(t):
    if t < 4:
        return [(0, P, META + P * t)]
    if t == 4:
        return [(0, DEC, KSAMPLE), (DEC, META, 0)]
    return [(0, P, KCACHE + P * (t - 5))]


class Plan:

    def __init__(self, nc, at):
        self.nc, self.at = nc, at

    def __call__(self, name, shape, dt=F32):
        size = int(np.prod(shape[1:])) * 4
        size = (size + 31) // 32 * 32
        t = self.nc.alloc_sbuf_tensor_at(name, shape, dt, offset=self.at)
        self.at += size
        return t


BASE = 16512


class Chain:

    def __init__(self, eng):
        self.eng, self.n = eng, {}

    def __call__(self, ins, sem):
        ins.then_inc(sem, 1)
        self.n[sem.name] = self.n.get(sem.name, 0) + 1
        self.eng.wait_ge(sem, self.n[sem.name])


def mid(ap, n):
    return ap.unsqueeze(1).to_broadcast([ap.shape[0], n, ap.shape[1]])


def last(ap, n):
    return ap.unsqueeze(2).to_broadcast([ap.shape[0], ap.shape[1], n])


def project(nc, io, m, sem):
    pl = Plan(nc, m.temps)
    w_tok = pl("w_tok", [P, DC, COLS])
    x2 = [pl(f"xa{i}", [P, D]) for i in range(2)]
    xs = pl("xs", [P, D])
    pr = [pl(f"pr{i}", [P, COLS]) for i in range(2)]
    qf = pl("qf", [P, H, AQK])
    kf = pl("kf", [P, H, AQK])
    t1 = pl("t1", [P, 18 * BROT])
    t2 = pl("t2", [P, 18 * BROT])
    w_uq = pl("w_uq", [P, 2, H * AQK])
    w_ukv = pl("w_ukv", [P, H * (NOPE + AV)])
    gains = pl("gains", [P, GAINS])
    tabs = pl("tabs", [P, NT, TABS])
    latc = pl("latc", [P, PAST])
    lat = pl("lat", [P, P])
    cq = pl("cq", [P, 2, P])
    kpec = pl("kpec", [P, 2, ROPE])
    ln1 = pl("ln1", [P, DC])
    qg = pl("qg", [P, 2])
    stx = pl("stx", [P, 4])
    stp = pl("stp", [P, 3, 16])
    stq = pl("stq", [P, 3, 24])
    inv_n = pl("inv_n", [P, 16])
    assert pl.at <= m.end
    ident = m.ident

    psum = lambda name, shape: nc.psum_tensor(name, shape, F32)
    with psum("ps_x", [P, DC, P]) as ps_x, psum("ps_pj", [P, 2, 512]) as ps_pj, \
            psum("ps_tr", [P, 2, 4, P]) as ps_tr, psum("ps_mm", [P, 2, 512]) as ps_mm, nc.Block() as block:
        s_x = [sem(f"a_x{t}") for t in range(NT)]
        s_win = sem("a_win")
        s_small = sem("a_small")
        s_kpec = sem("a_kpec")
        s_step = sem("a_step")
        s_ms_x = sem("a_ms_x")
        s_rt_x = sem("a_rt_x")
        s_xs = sem("a_xs")
        s_xT = sem("a_xT")
        s_hT = sem("a_hT")
        s_proj = sem("a_proj")
        s_pr = sem("a_pr")
        s_ms_p = sem("a_ms_p")
        s_rt_p = sem("a_rt_p")
        s_norm = sem("a_norm")
        s_tr = sem("a_tr")
        s_trc = sem("a_trc")
        s_mm = sem("a_mm")
        s_mmc = sem("a_mmc")
        s_ms_q = sem("a_ms_q")
        s_rt_q = sem("a_rt_q")
        s_qk = sem("a_qk")
        s_kv = sem("a_kv")
        s_ident = sem("a_ident")
        s_out = [sem("a_out0"), sem("a_out1")]

        groups = []
        for t in range(NT):
            groups.append((t, "lat", 0))
            groups += [(t, "pair", g) for g in range(3)]
            groups += [(t, "q", 0), (t, "q", 1), (t, "k", 0), (t, "k", 1)]
        for t in (5, 6):
            groups += [(t, "k", 0), (t, "k", 1)]
        index = {g: n for n, g in enumerate(groups)}
        halves = [(t, k, j) for t in range(NT) for k in ("q", "kv") for j in range(2)]
        halves += [(t, "kv", j) for t in (5, 6) for j in range(2)]
        mm_index = {g: n for n, g in enumerate(halves)}

        def pair(buf, g):
            return buf[:, C_B + 2 * HD * g:C_B + 2 * HD * (g + 1)]

        @block.sync
        def _(sp):
            def load_x(t):
                if t < 4:
                    sp.dma_start(x2[t % 2][:, :], io.x_prompt[P * t:P * (t + 1), :]).then_inc(s_x[t], 16)
                else:
                    sp.dma_start(x2[t % 2][0:DEC, :], io.x_sample[:, :]).then_inc(s_x[t], 16)
                    sp.dma_start(x2[t % 2][DEC:DEC + META, :], io.meta_tokens[:, :]).then_inc(s_x[t], 16)

            load_x(0)
            for c in range(DC):
                sp.dma_start(w_tok[:, c, :], io.w_tok[:, c, :]).then_inc(s_win, 16)
            load_x(1)
            for t in range(NT):
                if t + 2 < NT:
                    sp.wait_ge(s_xs, t + 1)
                    load_x(t + 2)
                sp.wait_ge(s_norm, t + 1)
                buf = pr[t % 2]
                for dst, c0, n in ((0, C_KV, KVRANK), (1, C_KPE, ROPE), (2, C_B + 2 * HD * H, HD),
                                   (3, C_BV, HD), (4, C_B + 2 * HD * H + HD, HD)):
                    if t < 4:
                        sp.dma_start(io.new_p[dst][META + P * t:META + P * (t + 1), :],
                                     buf[:, c0:c0 + n]).then_inc(s_out[t % 2], 16)
                    else:
                        sp.dma_start(io.new_s[dst][:, :], buf[0:DEC, c0:c0 + n]).then_inc(s_out[0], 16)
                        sp.dma_start(io.new_p[dst][0:META, :],
                                     buf[DEC:DEC + META, c0:c0 + n]).then_inc(s_out[0], 16)
            sp.wait_ge(s_out[0], 16 * 5 * 4)
            sp.wait_ge(s_out[1], 16 * 5 * 2)

        @block.gpsimd
        def _(pool):
            nc.gpsimd.memset(ident[:, :], 0.0).then_inc(s_ident, 1)
            pool.wait_ge(s_ident, 1)
            nc.gpsimd.affine_select(out=ident[:, :], in_=ident[:, :], compare_op=ALU.not_equal, fill=1.0,
                                    base=0, pattern=[[-1, P]], channel_multiplier=1).then_inc(s_ident, 1)

        @block.scalar
        def _(act):
            act.dma_start(gains[:, :], io.gains[:, :]).then_inc(s_small, 16)
            act.dma_start(tabs[:, :, :], io.tabs[:, :, :]).then_inc(s_small, 16)
            act.dma_start(ln1[:, :], io.ln1[:, :]).then_inc(s_small, 16)
            act.dma_start(qg[:, :], io.q_gain[:, :]).then_inc(s_small, 16)
            act.dma_start(w_uq[:, :, :], io.w_uq[:, :, :]).then_inc(s_small, 16)
            act.dma_start(w_ukv[:, :], io.w_ukv[:, :]).then_inc(s_small, 16)
            act.dma_start(latc[:, :], io.lat_t[:, :]).then_inc(s_small, 16)
            act.dma_start(kpec[:, :, :], io.cache_kpe[:, :].rearrange("(a p) r -> p a r", p=P)).then_inc(s_kpec, 16)
            act.dma_start(m.bik[0:HD, KCACHE:KSAMPLE], io.bk_t[:, :]).then_inc(s_kpec, 16)
            act.dma_start(m.bik[HD:P, KCACHE:KSAMPLE], io.ik_t[:, :]).then_inc(s_kpec, 16)
            for a in range(2):
                act.dma_start(m.vb[:, 5 + a, :], io.cache_bv[P * a:P * (a + 1), :]).then_inc(s_kpec, 16)
            act.wait_ge(s_small, 16 * 7)

            def root(n_sem, r_sem, n, dst, src):
                act.wait_ge(n_sem, n)
                nc.scalar.activation(dst, src, ACT.Sqrt).then_inc(r_sem, 1)

            def proj_out(t):
                r = rows_of(t)
                for c in range(4):
                    act.wait_ge(s_proj, 4 * t + c + 1)
                    if c == 0 and t >= 2:
                        act.wait_ge(s_out[t % 2], 16 * 5 * (t // 2))
                        act.wait_ge(s_tr, index[(t - 2, "pair", 2)] + 1)
                    nc.scalar.copy(pr[t % 2][0:r, PJ * c:PJ * (c + 1)],
                                   ps_pj[0:r, c % 2, 0:PJ]).then_inc(s_pr, 1)

            def tr_out(key):
                t, kind, g = key
                n = index[key]
                r = rows_of(t) if t < NT else P
                bank = ps_tr[:, n % 2, :, :]
                act.wait_ge(s_tr, n + 1)
                if kind == "lat":
                    act.wait_ge(s_mm, mm_index[(t - 1, "kv", 1)] + 1) if t else None
                    for j in range(2):
                        nc.scalar.activation(cq[:, j, 0:r], bank[:, j, 0:r], ACT.Copy, scale=qg[:, j:j + 1])
                    nc.scalar.copy(lat[:, 0:r], bank[:, 2, 0:r]).then_inc(s_trc, 1)
                    return
                moves = []
                for r0, nr, k0 in key_columns(t):
                    if kind == "pair" and g == 2:
                        moves.append((m.bik[:, k0:k0 + nr], bank[:, 0, r0:r0 + nr]))
                    if kind == "k":
                        moves.append((m.kt[0:AQK, 4 * g:4 * g + 4, k0:k0 + nr], bank[0:AQK, :, r0:r0 + nr]))
                nq = queries_of(t)
                if kind == "pair" and g < 2:
                    moves.append((m.biq[:, 4 * g:4 * g + 4, P * t:P * t + nq], bank[:, :, 0:nq]))
                if kind == "q":
                    moves.append((m.qt[0:AQK, 4 * g:4 * g + 4, P * t:P * t + nq], bank[0:AQK, :, 0:nq]))
                for i, (dst, src) in enumerate(moves):
                    ins = nc.scalar.copy(dst, src)
                ins.then_inc(s_trc, 1)

            def mm_out(t, kind):
                r = rows_of(t) if t < NT else P
                for j in range(2):
                    act.wait_ge(s_mm, mm_index[(t, kind, j)] + 1)
                    if kind == "q":
                        if j == 0 and t:
                            act.wait_ge(s_tr, index[(t - 1, "q", 1)] + 1)
                        nc.scalar.copy(qf[0:r, 4 * j:4 * j + 4, :],
                                       ps_mm[0:r, j, 0:4 * AQK].rearrange("p (h c) -> p h c", h=4)
                                       ).then_inc(s_mmc, 1)
                    else:
                        if j == 0 and t:
                            act.wait_ge(s_tr, index[(t - 1, "k", 1)] + 1)
                        kv = ps_mm[0:r, j, :].rearrange("p (h c) -> p h c", h=4)
                        nc.scalar.copy(kf[0:r, 4 * j:4 * j + 4, 0:NOPE], kv[:, :, 0:NOPE])
                        nc.scalar.copy(m.va[0:r, t, 4 * j:4 * j + 4, :], kv[:, :, NOPE:]).then_inc(s_mmc, 1)

            root(s_ms_x, s_rt_x, 1, stx[:, 2:3], stx[:, 1:2])
            proj_out(0)
            for t in range(NT):
                root(s_ms_p, s_rt_p, t + 1, stp[:, 2, 0:12], stp[:, 1, 0:12])
                if t + 1 < NT:
                    root(s_ms_x, s_rt_x, t + 2, stx[:, 2:3], stx[:, 1:2])
                tr_out((t, "lat", 0))
                mm_out(t, "q")
                mm_out(t, "kv")
                root(s_ms_q, s_rt_q, t + 1, stq[:, 2, 0:24], stq[:, 1, 0:24])
                if t + 1 < NT:
                    proj_out(t + 1)
                for g in range(3):
                    tr_out((t, "pair", g))
                for g in range(2):
                    tr_out((t, "q", g))
                for g in range(2):
                    tr_out((t, "k", g))
            for t in (5, 6):
                mm_out(t, "kv")
                root(s_ms_q, s_rt_q, t + 1, stq[:, 2, 16:24], stq[:, 1, 16:24])
                for g in range(2):
                    tr_out((t, "k", g))
            act.wait_ge(s_kpec, 16 * 5)

        @block.vector
        def _(dve):
            step = Chain(dve)
            v = nc.vector
            for j, (n, lo, hi) in enumerate(((QRANK, 0, 1), (KVRANK, 1, 2), (ROPE, 2, 3), (HD, 3, 12))):
                v.memset(inv_n[:, lo:hi], 1.0 / n)
            for buf in (stx, stp, stq):
                step(v.memset(buf[:], 1.0), s_step)

            def x_scale(t):
                r = rows_of(t)
                dve.wait_ge(s_x[t], 16 if t < 4 else 32)
                if t:
                    dve.wait_ge(s_xT, DC * t)
                step(v.tensor_tensor_reduce(out=xs[0:r, :], in0=x2[t % 2][0:r, :], in1=x2[t % 2][0:r, :],
                                            scale=1.0, scalar=0.0, op0=ALU.mult, op1=ALU.add,
                                            accum_out=stx[0:r, 0:1]), s_step)
                v.tensor_scalar(stx[:, 1:2], stx[:, 0:1], 1.0 / D, EPS, ALU.mult, ALU.add).then_inc(s_ms_x, 1)
                dve.wait_ge(s_rt_x, t + 1)
                step(v.reciprocal(stx[:, 3:4], stx[:, 2:3]), s_step)
                step(v.tensor_scalar(xs[0:r, :], x2[t % 2][0:r, :], stx[0:r, 3:4], None, ALU.mult), s_xs)

            def hT_out(t):
                r = rows_of(t)
                for j in range(2):
                    dve.wait_ge(s_xT, DC * t + 4 * (j + 1))
                    v.tensor_tensor(m.ht[:, 4 * j:4 * j + 4, P * t:P * t + r], ps_x[:, 4 * j:4 * j + 4, 0:r],
                                    last(ln1[:, 4 * j:4 * j + 4], r), ALU.mult).then_inc(s_hT, 1)

            def rotate(x, cos, sin, n, half):
                r = x.shape[0]
                a = t1[0:r, 0:2 * n * half].rearrange("p (n k) -> p n k", n=n)
                b = t2[0:r, 0:2 * n * half].rearrange("p (n k) -> p n k", n=n)
                v.tensor_tensor(a, x, mid(cos, n), ALU.mult)
                v.tensor_tensor(b[:, :, 0:half], x[:, :, half:2 * half], mid(sin[:, 0:half], n), ALU.mult)
                step(v.tensor_tensor(b[:, :, half:2 * half], x[:, :, 0:half],
                                     mid(sin[:, half:2 * half], n), ALU.mult), s_step)
                return v.tensor_tensor(x, a, b, ALU.add)

            def p_norm(t):
                r = rows_of(t)
                buf = pr[t % 2][0:r]
                pairs = buf[:, C_B:C_BV].rearrange("p (n k) -> p n k", n=NPAIR)
                dve.wait_ge(s_pr, 4 * t + 4)
                if t == 0:
                    dve.wait_ge(s_small, 16 * 7)
                sq = xs[0:r, :]
                dve.wait_ge(s_xT, DC * (t + 1))
                v.tensor_tensor(sq[:, 0:C_B], buf[:, 0:C_B], buf[:, 0:C_B], ALU.mult)
                sqb = sq[:, C_B:C_B + NPAIR * HD].rearrange("p (n k) -> p n k", n=NPAIR)
                step(v.tensor_tensor(sqb, pairs[:, :, 0:HD], pairs[:, :, 0:HD], ALU.mult), s_step)
                v.tensor_reduce(stp[0:r, 0, 0:1], sq[:, 0:C_KV], AX_X, ALU.add)
                v.tensor_reduce(stp[0:r, 0, 1:2], sq[:, C_KV:C_KPE], AX_X, ALU.add)
                v.tensor_reduce(stp[0:r, 0, 2:3], sq[:, C_KPE:C_B], AX_X, ALU.add)
                step(v.tensor_reduce(stp[0:r, 0, 3:12], sqb, AX_X, ALU.add), s_step)
                step(v.tensor_tensor(stp[:, 1, 0:12], stp[:, 0, 0:12], inv_n[:, 0:12], ALU.mult), s_step)
                v.tensor_scalar(stp[:, 1, 0:12], stp[:, 1, 0:12], EPS, None, ALU.add).then_inc(s_ms_p, 1)
                v.tensor_copy(m.vb[0:r, t, :], buf[:, C_BV:C_IW])
                v.tensor_scalar(m.iw[0:r, t, :], buf[:, C_IW:COLS], IDX_SCALE, None, ALU.mult)
                dve.wait_ge(s_rt_p, t + 1)
                step(v.reciprocal(stp[:, 2, 0:12], stp[:, 2, 0:12]), s_step)
                rs = stp[0:r, 2, :]
                v.tensor_scalar(buf[:, 0:C_KV], buf[:, 0:C_KV], rs[:, 0:1], None, ALU.mult)
                v.scalar_tensor_tensor(out=buf[:, C_KV:C_KPE], in0=buf[:, C_KV:C_KPE], scalar=rs[:, 1:2],
                                       in1=gains[0:r, 0:G_KPE], op0=ALU.mult, op1=ALU.mult)
                v.scalar_tensor_tensor(out=buf[:, C_KPE:C_B], in0=buf[:, C_KPE:C_B], scalar=rs[:, 2:3],
                                       in1=gains[0:r, G_KPE:G_B], op0=ALU.mult, op1=ALU.mult)
                step(v.tensor_tensor(pairs[:, :, 0:HD], pairs[:, :, 0:HD], last(rs[:, 3:12], HD), ALU.mult),
                     s_step)
                step(v.tensor_tensor(pairs[:, :, 0:HD], pairs[:, :, 0:HD],
                                     gains[0:r, G_B:G_Q].rearrange("p (n k) -> p n k", n=NPAIR), ALU.mult),
                     s_step)
                tab = tabs[0:r, t, :]
                step(rotate(buf[:, C_KPE:C_B].unsqueeze(1), tab[:, 0:ROPE], tab[:, ROPE:2 * ROPE], 1, ROPE // 2),
                     s_step)
                heads = buf[:, C_B:C_BV].rearrange("p (n k) -> p n k", n=2 * NPAIR)
                step(rotate(heads[:, :, 0:BROT], tab[:, 2 * ROPE:2 * ROPE + BROT],
                            tab[:, 2 * ROPE + BROT:TABS], 2 * NPAIR, BROT // 2), s_norm)

            def qk_norm(t):
                r = rows_of(t) if t < NT else P
                new = t < NT
                sq = xs[0:r, 0:H * AQK].rearrange("p (h c) -> p h c", h=H)
                lo = 0 if new else 16
                if new:
                    dve.wait_ge(s_mmc, mm_index[(t, "q", 1)] + 1)
                    step(v.tensor_tensor(sq, qf[0:r], qf[0:r], ALU.mult), s_step)
                    v.tensor_reduce(stq[0:r, 0, 0:8], sq[:, :, 0:NOPE], AX_X, ALU.add)
                    step(v.tensor_reduce(stq[0:r, 0, 8:16], sq[:, :, NOPE:], AX_X, ALU.add), s_step)
                dve.wait_ge(s_mmc, mm_index[(t, "kv", 1)] + 1)
                step(v.tensor_tensor(sq[:, :, 0:NOPE], kf[0:r, :, 0:NOPE], kf[0:r, :, 0:NOPE], ALU.mult), s_step)
                step(v.tensor_reduce(stq[0:r, 0, 16:24], sq[:, :, 0:NOPE], AX_X, ALU.add), s_step)
                if new:
                    v.tensor_scalar(stq[:, 1, 8:16], stq[:, 0, 8:16], 1.0 / ROPE, EPS, ALU.mult, ALU.add)
                    v.tensor_scalar(stq[:, 1, 0:8], stq[:, 0, 0:8], 1.0 / NOPE, EPS, ALU.mult, ALU.add)
                step(v.tensor_scalar(stq[:, 1, 16:24], stq[:, 0, 16:24], 1.0 / NOPE, EPS, ALU.mult, ALU.add),
                     s_ms_q)
                dve.wait_ge(s_rt_q, t + 1)
                step(v.reciprocal(stq[:, 2, lo:24], stq[:, 2, lo:24]), s_step)
                rs = stq[0:r, 2, :]
                q, k = qf[0:r], kf[0:r]
                if new:
                    v.tensor_tensor(q[:, :, 0:NOPE], q[:, :, 0:NOPE], last(rs[:, 0:8], NOPE), ALU.mult)
                    v.tensor_tensor(q[:, :, NOPE:], q[:, :, NOPE:], last(rs[:, 8:16], ROPE), ALU.mult)
                step(v.tensor_tensor(k[:, :, 0:NOPE], k[:, :, 0:NOPE], last(rs[:, 16:24], NOPE), ALU.mult), s_step)
                if new:
                    v.tensor_tensor(q, q, mid(gains[0:r, G_Q:G_KN], H), ALU.mult)
                kpe = pr[t % 2][0:r, C_KPE:C_B] if new else kpec[:, t - 5, :]
                if t == 5:
                    dve.wait_ge(s_kpec, 16 * 5)
                v.tensor_copy(k[:, :, NOPE:], mid(kpe, H))
                step(v.tensor_tensor(k[:, :, 0:NOPE], k[:, :, 0:NOPE], mid(gains[0:r, G_KN:GAINS], H), ALU.mult),
                     s_step)
                if new:
                    tab = tabs[0:r, t, :]
                    rotate(q[:, :, NOPE:], tab[:, 0:ROPE], tab[:, ROPE:2 * ROPE], H, ROPE // 2).then_inc(s_qk, 1)
                else:
                    v.tensor_copy(stx[:, 0:1], stx[:, 1:2]).then_inc(s_qk, 1)

            x_scale(0)
            hT_out(0)
            for t in range(NT):
                p_norm(t)
                if t + 1 < NT:
                    x_scale(t + 1)
                    hT_out(t + 1)
                qk_norm(t)
            for t in (5, 6):
                qk_norm(t)

        @block.tensor
        def _(pe):
            def x_transposes(t):
                r = rows_of(t)
                pe.wait_ge(s_xs, t + 1)
                if t:
                    pe.wait_ge(s_hT, 2 * t)
                for c in range(DC):
                    nc.tensor.transpose(ps_x[:, c, 0:r], xs[0:r, P * c:P * (c + 1)],
                                        ident[0:r, 0:r]).then_inc(s_xT, 1)

            def projection(t):
                r = rows_of(t)
                pe.wait_ge(s_hT, 2 * t + 2)
                if t == 0:
                    pe.wait_ge(s_win, 16 * DC)
                for c in range(4):
                    if 4 * t + c >= 2:
                        pe.wait_ge(s_pr, 4 * t + c - 1)
                    for k in range(DC):
                        ins = nc.tensor.matmul(ps_pj[0:r, c % 2, 0:PJ], m.ht[:, k, P * t:P * t + r],
                                               w_tok[:, k, PJ * c:PJ * (c + 1)], start=(k == 0), stop=(k == DC - 1))
                    ins.then_inc(s_proj, 1)

            def turn(key):
                t, kind, g = key
                n = index[key]
                r = rows_of(t) if t < NT else P
                buf = pr[t % 2][0:r]
                if n >= 2:
                    pe.wait_ge(s_trc, n - 1)
                if kind == "lat":
                    pe.wait_ge(s_norm, t + 1)
                    srcs = [buf[:, 0:P], buf[:, P:2 * P], buf[:, C_KV:C_KPE]]
                elif kind == "pair":
                    srcs = [pair(buf, i) for i in (range(4 * g, 4 * g + 4) if g < 2 else [H])]
                else:
                    pe.wait_ge(s_qk, t + 1)
                    src = qf if kind == "q" else kf
                    srcs = [src[0:r, i, :] for i in range(4 * g, 4 * g + 4)]
                for j, s in enumerate(srcs):
                    ins = nc.tensor.transpose(ps_tr[0:s.shape[1], n % 2, j, 0:r], s, ident[0:r, 0:r])
                ins.then_inc(s_tr, 1)

            def up(t, kind):
                r = rows_of(t) if t < NT else P
                for j in range(2):
                    n = mm_index[(t, kind, j)]
                    if n >= 2:
                        pe.wait_ge(s_mmc, n - 1)
                    if kind == "q":
                        for k in range(2):
                            ins = nc.tensor.matmul(ps_mm[0:r, j, 0:4 * AQK], cq[:, k, 0:r],
                                                   w_uq[:, k, 4 * AQK * j:4 * AQK * (j + 1)],
                                                   start=(k == 0), stop=(k == 1))
                    else:
                        left = lat[:, 0:r] if t < NT else latc[:, P * (t - 5):P * (t - 4)]
                        ins = nc.tensor.matmul(ps_mm[0:r, j, :], left, w_ukv[:, 512 * j:512 * (j + 1)],
                                               start=True, stop=True)
                    ins.then_inc(s_mm, 1)

            pe.wait_ge(s_ident, 2)
            x_transposes(0)
            projection(0)
            for t in range(NT):
                turn((t, "lat", 0))
                pe.wait_ge(s_trc, index[(t, "lat", 0)] + 1)
                if t == 0:
                    pe.wait_ge(s_small, 16 * 7)
                up(t, "q")
                up(t, "kv")
                if t + 1 < NT:
                    x_transposes(t + 1)
                    projection(t + 1)
                for g in range(3):
                    turn((t, "pair", g))
                for kind in ("q", "k"):
                    for g in range(2):
                        turn((t, kind, g))
            for t in (5, 6):
                up(t, "kv")
                for g in range(2):
                    turn((t, "k", g))


def attend(nc, io, m, sem):
    pl = Plan(nc, m.temps)
    m.oab = pl("oab", [P, NT, 2, H * AV])
    m.after_attend = pl.at
    vm = pl("vm", [META, H * AV + HD])
    biasA = pl("biasA", [P, KPROMPT])
    biasB = pl("biasB", [P, KPROMPT])
    score = pl("score", [P, KPROMPT])
    rel = [pl(f"rel{i}", [P, KPROMPT]) for i in range(2)]
    logit = [pl(f"logit{i}", [P, KPROMPT]) for i in range(2)]
    prob = [pl(f"prob{i}", [P, KPROMPT]) for i in range(2)]
    probT = [pl(f"probT{i}", [P, NT, P]) for i in range(2)]
    best = pl("best", [P, 8])
    mx = pl("mx", [P, 2, 2])
    total = pl("total", [P, 2, 2, H])
    inv = pl("inv", [P, H])
    assert pl.at <= m.end
    ident = m.ident

    units = [(t, kind, h) for t in range(NT) for kind in ("index", "mla", "dsa") for h in range(H)]
    N = len(units)
    number = {u: n for n, u in enumerate(units)}
    att = [n for n, u in enumerate(units) if u[1] != "index"]
    att_no = {n: i for i, n in enumerate(att)}
    idx_no = {n: i for i, n in enumerate(n for n, u in enumerate(units) if u[1] == "index")}
    LAG = 3

    def keys(t):
        return (0, META + P * (t + 1)) if t < 4 else (KPROMPT, PAST + DEC)

    def blocks(t):
        if t < 4:
            return [(META + P * j, P, j) for j in range(t + 1)] + [(0, META, None)]
        return [(0, P, 5), (P, P, 6), (PAST, DEC, 4)]

    def value(kind, h, r, j):
        if kind == "mla":
            return m.va[0:r, j, h, :] if j is not None else vm[0:r, AV * h:AV * (h + 1)]
        return m.vb[0:r, j, :] if j is not None else vm[0:r, H * AV:]

    def halves(buf, t):
        q, nk = queries_of(t), keys(t)[1]
        return buf[0:q, 0:nk].rearrange("p (a k) -> p a k", a=2)

    psum = lambda name, shape: nc.psum_tensor(name, shape, F32)
    with psum("ps_sc", [P, 2, 2, 512]) as ps_sc, psum("ps_pt", [P, 8, P]) as ps_pt, \
            psum("ps_o", [P, 2, 512]) as ps_o, nc.Block() as block:
        s_vm = sem("b_vm")
        s_step = sem("b_step")
        s_score = sem("b_score")
        s_rel = sem("b_rel")
        s_acc = sem("b_acc")
        s_logit = sem("b_logit")
        s_max = sem("b_max")
        s_prob = sem("b_prob")
        s_pt = sem("b_pt")
        s_ptc = sem("b_ptc")
        s_pv = sem("b_pv")
        s_o = sem("b_o")

        @block.sync
        def _(sp):
            sp.dma_start(vm[:, 0:H * AV], m.va[DEC:DEC + META, 4, :, :].rearrange("p h c -> p (h c)")).then_inc(s_vm, 16)
            sp.dma_start(vm[:, H * AV:], m.vb[DEC:DEC + META, 4, :]).then_inc(s_vm, 16)

        def wait_consumed(eng, n):
            if n in idx_no:
                eng.wait_ge(s_rel, idx_no[n] + 1)
            else:
                eng.wait_ge(s_logit, att_no[n] + 1)

        @block.tensor
        def _(pe):
            def scores(n):
                t, kind, h = units[n]
                q = queries_of(t)
                k0, nk = keys(t)
                if n >= 2:
                    wait_consumed(pe, n - 2)
                if kind == "mla":
                    left, right = m.qt[0:AQK, h, P * t:P * t + q], m.kt[0:AQK, h, k0:k0 + nk]
                elif kind == "dsa":
                    left, right = m.biq[0:HD, h, P * t:P * t + q], m.bik[0:HD, k0:k0 + nk]
                else:
                    left, right = m.biq[HD:P, h, P * t:P * t + q], m.bik[HD:P, k0:k0 + nk]
                for a in range(2):
                    ins = nc.tensor.matmul(ps_sc[0:q, n % 2, a, 0:nk // 2], left,
                                           right[:, nk // 2 * a:nk // 2 * (a + 1)], start=True, stop=True)
                ins.then_inc(s_score, 1)

            def turn(n):
                t, kind, h = units[n]
                q, i = queries_of(t), att_no[n]
                pe.wait_ge(s_prob, i + 1)
                if i:
                    pe.wait_ge(s_ptc, i)
                for j, (c, r, _) in enumerate(blocks(t)):
                    ins = nc.tensor.transpose(ps_pt[0:r, j, 0:q], prob[i % 2][0:q, c:c + r], ident[0:q, 0:q])
                ins.then_inc(s_pt, 1)

            def values(n):
                t, kind, h = units[n]
                q, i = queries_of(t), att_no[n]
                x = 0 if kind == "mla" else 1
                pe.wait_ge(s_ptc, i + 1)
                if h == 0 and t:
                    pe.wait_ge(s_o, 2 * t - 1 + x)
                if i == 0:
                    pe.wait_ge(s_vm, 32)
                bl = blocks(t)
                for j, (c, r, v) in enumerate(bl):
                    ins = nc.tensor.matmul(ps_o[0:q, x, AV * h:AV * (h + 1)], probT[i % 2][0:r, j, 0:q],
                                           value(kind, h, r, v), start=(j == 0), stop=(j == len(bl) - 1))
                ins.then_inc(s_pv, 1)

            for n in range(N + 2):
                if n < N:
                    scores(n)
                if n >= 2 and n - 2 in att_no:
                    values(n - 2)
                if 1 <= n <= N and n - 1 in att_no:
                    turn(n - 1)

        @block.scalar
        def _(act):
            def unit(n):
                t, kind, h = units[n]
                q = queries_of(t)
                if kind == "index":
                    i = idx_no[n]
                    act.wait_ge(s_score, n + 1)
                    if i >= 2:
                        act.wait_ge(s_acc, i - 1)
                    nc.scalar.activation(halves(rel[i % 2], t), ps_sc[0:q, n % 2, :, 0:keys(t)[1] // 2],
                                         ACT.Relu).then_inc(s_rel, 1)
                    return
                i, x = att_no[n], 0 if kind == "mla" else 1
                act.wait_ge(s_max, i + 1)
                if i >= 2:
                    act.wait_ge(s_pt, i - 1)
                if h == 0 and t >= 2:
                    act.wait_ge(s_o, 2 * (t - 2) + 1 + x)
                nk = keys(t)[1]
                nc.scalar.activation(prob[i % 2][0:q, 0:nk], logit[i % 2][0:q, 0:nk], ACT.Exp,
                                     bias=mx[0:q, i % 2, 1:2], scale=A_SCALE if x == 0 else B_SCALE,
                                     accum_out=total[0:q, t % 2, x, h:h + 1]).then_inc(s_prob, 1)

            def turned(n):
                t, kind, h = units[n]
                q, i = queries_of(t), att_no[n]
                act.wait_ge(s_pt, i + 1)
                if i >= 2:
                    act.wait_ge(s_pv, i - 1)
                bl = blocks(t)
                full = sum(r == P for _, r, _ in bl)
                nc.scalar.copy(probT[i % 2][:, 0:full, 0:q], ps_pt[:, 0:full, 0:q])
                r = bl[-1][1]
                nc.scalar.copy(probT[i % 2][0:r, full, 0:q], ps_pt[0:r, full, 0:q]).then_inc(s_ptc, 1)

            for n in range(N + 1):
                if n < N:
                    unit(n)
                if n >= 1 and n - 1 in att_no:
                    turned(n - 1)

        @block.vector
        def _(dve):
            step = Chain(dve)
            v = nc.vector

            def index_unit(n):
                t, _, h = units[n]
                q, nk = queries_of(t), keys(t)[1]
                i = idx_no[n]
                dve.wait_ge(s_rel, i + 1)
                w = m.iw[0:q, t, h:h + 1]
                if h == 0:
                    step(v.tensor_scalar(score[0:q, 0:nk], rel[i % 2][0:q, 0:nk], w, None, ALU.mult), s_acc)
                else:
                    step(v.scalar_tensor_tensor(out=score[0:q, 0:nk], in0=rel[i % 2][0:q, 0:nk], scalar=w,
                                                in1=score[0:q, 0:nk], op0=ALU.mult, op1=ALU.add), s_acc)

            def select(t):
                q, nk = queries_of(t), keys(t)[1]
                sc = score[0:q, 0:nk]
                if t < 4:
                    step(v.memset(score[0:CHUNK, nk - CHUNK:nk], NEG), s_step)
                for _ in range((TOPK_P if t < 4 else TOPK_S) // 8):
                    step(v.max(best[0:q, :], sc), s_step)
                    step(v.match_replace(sc, best[0:q, :], sc, TAKEN), s_step)
                step(v.tensor_scalar(biasB[0:q, 0:nk], sc, SEEN, HIDE, ALU.is_gt, ALU.mult), s_step)
                if t < 4:
                    step(v.tensor_tensor(biasB[0:q, 0:nk], biasB[0:q, 0:nk], biasA[0:q, KPROMPT - nk:], ALU.add),
                         s_step)

            def logits(n):
                t, kind, h = units[n]
                q, nk = queries_of(t), keys(t)[1]
                i = att_no[n]
                if kind == "dsa":
                    bias = halves(biasB, t)
                elif t < 4:
                    bias = biasA[0:q, KPROMPT - nk:].rearrange("p (a k) -> p a k", a=2)
                else:
                    bias = halves(biasA, t)
                dve.wait_ge(s_score, n + 1)
                if i >= 2:
                    dve.wait_ge(s_prob, i - 1)
                step(v.tensor_tensor_reduce(out=halves(logit[i % 2], t), in0=ps_sc[0:q, n % 2, :, 0:nk // 2],
                                            in1=bias, scale=1.0, scalar=NEG, op0=ALU.add, op1=ALU.max,
                                            accum_out=mx[0:q, i % 2, 0:1]), s_logit)
                v.tensor_scalar(mx[0:q, i % 2, 1:2], mx[0:q, i % 2, 0:1],
                                -(A_SCALE if kind == "mla" else B_SCALE), None, ALU.mult).then_inc(s_max, 1)

            def normalise(n):
                t, kind, _ = units[n]
                q, x = queries_of(t), 0 if kind == "mla" else 1
                dve.wait_ge(s_pv, att_no[n] + 1)
                step(v.reciprocal(inv[0:q, :], total[0:q, t % 2, x, :]), s_step)
                step(v.tensor_tensor(m.oab[0:q, t, x, :].rearrange("p (h c) -> p h c", h=H),
                                     ps_o[0:q, x, :].rearrange("p (h c) -> p h c", h=H),
                                     last(inv[0:q, :], AV), ALU.mult), s_o)

            step(v.memset(biasA[:, :], 0.0), s_step)
            step(v.memset(biasA[0:CHUNK, KPROMPT - CHUNK:], HIDE), s_step)
            for n in range(N + LAG):
                if n < N:
                    t, kind, h = units[n]
                    if kind == "index":
                        index_unit(n)
                        if h == H - 1:
                            select(t)
                    else:
                        logits(n)
                k = n - LAG
                if k >= 0 and units[k][1] != "index" and units[k][2] == H - 1:
                    normalise(k)


def merge(nc, io, m, sem):
    lo = Plan(nc, m.keep)
    m.x = lo("x", [P, NT, D])
    m.h2t = lo("h2t", [P, DC, NQ])
    mt = lo("mt", [P, DC, NQ])
    m.after_merge = lo.at
    assert lo.at <= m.temps
    pl = Plan(nc, m.after_attend)
    ot = pl("ot", [P, 2, 4, NQ])
    wo = pl("wo", [P, 2, 4, 512])
    wg = [pl(f"wg{i}", [P, 2, DC, P]) for i in range(2)]
    w_out = pl("w_out", [P, DC, 512])
    sg = pl("sg", [P, 2, 2, HALF])
    part = pl("part", [P, 2, HALF])
    xs = pl("xs2", [P, D])
    st = pl("st2", [P, 4])
    ln2 = pl("ln2", [P, DC])
    assert pl.at <= m.end, pl.at
    ident = m.ident

    with nc.psum_tensor("ps_m", [P, 8, 512], F32) as ps, nc.Block() as block:
        s_x = sem("c_x")
        s_wo = [sem("c_wo0"), sem("c_wo1")]
        s_wout = [sem("c_wout0"), sem("c_wout1")]
        s_wg = [sem("c_wg0"), sem("c_wg1")]
        s_ln = sem("c_ln")
        s_ot = sem("c_ot")
        s_otc = sem("c_otc")
        s_z = sem("c_z")
        s_sig = sem("c_sig")
        s_mt = sem("c_mt")
        s_y = sem("c_y")
        s_step = sem("c_step")
        s_res = sem("c_res")
        s_ms = sem("c_ms")
        s_rt = sem("c_rt")
        s_xs = sem("c_xs")
        s_hT = sem("c_hT")
        s_h2 = sem("c_h2")

        @block.sync
        def _(sp):
            def load_gate(j):
                for x in range(2):
                    sp.dma_start(wg[j % 2][:, x, :, :], io.w_gate[x * DC + j, :, :, :]).then_inc(s_wg[j % 2], 16)

            load_gate(0)
            for x in range(2):
                sp.dma_start(wo[:, x, :, :], io.w_o[0, x, :, :, :]).then_inc(s_wo[0], 16)
            load_gate(1)
            sp.dma_start(m.x[:, 0:4, :], io.x_prompt[:, :].rearrange("(t p) d -> p t d", p=P)).then_inc(s_x, 16)
            sp.dma_start(m.x[0:DEC, 4, :], io.x_sample[:, :]).then_inc(s_x, 16)
            sp.dma_start(ln2[:, :], io.ln2[:, :]).then_inc(s_ln, 16)
            sp.dma_start(w_out[:, :, :], io.w_out[0, :, :, :]).then_inc(s_wout[0], 16)
            for j in range(2, DC):
                sp.wait_ge(s_z, 2 * (j - 1))
                load_gate(j)
                if j == 5:
                    sp.wait_ge(s_z, 2 * 4)
                    for x in range(2):
                        sp.dma_start(wo[:, x, :, :], io.w_o[1, x, :, :, :]).then_inc(s_wo[1], 16)
            sp.wait_ge(s_y, NT)
            sp.dma_start(w_out[:, :, :], io.w_out[1, :, :, :]).then_inc(s_wout[1], 16)

        @block.tensor
        def _(pe):
            for t in range(NT):
                q = queries_of(t)
                for x in range(2):
                    n = 2 * t + x
                    if n >= 8:
                        pe.wait_ge(s_otc, n - 7)
                    for c in range(4):
                        ins = nc.tensor.transpose(ps[:, n % 8, P * c:P * c + q], m.oab[0:q, t, x, P * c:P * (c + 1)],
                                                  ident[0:q, 0:q])
                    ins.then_inc(s_ot, 1)
            pe.wait_ge(s_otc, 2 * NT)
            for j in range(DC):
                pe.wait_ge(s_wg[j % 2], 32 * (j // 2 + 1))
                pe.wait_ge(s_wo[j // 4], 32)
                for hf in range(2):
                    n = 2 * j + hf
                    b = 4 * (n % 2)
                    if n >= 2:
                        pe.wait_ge(s_mt, n - 1)
                    cols = slice(HALF * hf, HALF * (hf + 1))
                    for x in range(2):
                        for k in range(DC):
                            nc.tensor.matmul(ps[:, b + x, 0:HALF], wg[j % 2][:, x, k, :], m.ht[:, k, cols],
                                             start=(k == 0), stop=(k == DC - 1))
                    for x in range(2):
                        for k in range(4):
                            ins = nc.tensor.matmul(ps[:, b + 2 + x, 0:HALF],
                                                   wo[:, x, k, P * (j % 4):P * (j % 4 + 1)], ot[:, x, k, cols],
                                                   start=(k == 0), stop=(k == 3))
                    ins.then_inc(s_z, 1)
            pe.wait_ge(s_mt, 2 * DC)
            for c in range(2):
                pe.wait_ge(s_wout[c], 16)
                for t in range(NT):
                    q = queries_of(t)
                    n = NT * c + t
                    if n >= 8:
                        pe.wait_ge(s_res, n - 7)
                    for k in range(DC):
                        ins = nc.tensor.matmul(ps[0:q, n % 8, :], mt[:, k, P * t:P * t + q], w_out[:, k, :],
                                               start=(k == 0), stop=(k == DC - 1))
                    ins.then_inc(s_y, 1)
            pe.wait_ge(s_res, 2 * NT)
            for t in range(NT):
                q = queries_of(t)
                pe.wait_ge(s_xs, t + 1)
                for c in range(DC):
                    n = 2 * t + c // 4
                    if c % 4 == 0 and n >= 8:
                        pe.wait_ge(s_h2, n - 7)
                    ins = nc.tensor.transpose(ps[:, n % 8, P * (c % 4):P * (c % 4) + q],
                                              xs[0:q, P * c:P * (c + 1)], ident[0:q, 0:q])
                    if c % 4 == 3:
                        ins.then_inc(s_hT, 1)

        @block.scalar
        def _(act):
            for n in range(2 * NT):
                t, x = n // 2, n % 2
                q = queries_of(t)
                act.wait_ge(s_ot, n + 1)
                nc.scalar.copy(ot[:, x, :, P * t:P * t + q],
                               ps[:, n % 8, :].rearrange("p (c k) -> p c k", c=4)[:, :, 0:q]).then_inc(s_otc, 1)
            for n in range(2 * DC):
                act.wait_ge(s_z, n + 1)
                if n >= 2:
                    act.wait_ge(s_mt, n - 1)
                nc.scalar.activation(sg[:, n % 2, :, :], ps[:, 4 * (n % 2):4 * (n % 2) + 2, 0:HALF],
                                     ACT.Sigmoid).then_inc(s_sig, 1)
            for t in range(NT):
                act.wait_ge(s_ms, t + 1)
                nc.scalar.activation(st[:, 2:3], st[:, 1:2], ACT.Sqrt).then_inc(s_rt, 1)

        @block.vector
        def _(dve):
            step = Chain(dve)
            v = nc.vector
            step(v.memset(st[:, :], 1.0), s_step)
            for n in range(2 * DC):
                j, hf = n // 2, n % 2
                dve.wait_ge(s_sig, n + 1)
                step(v.tensor_tensor(part[:, :, :], sg[:, n % 2, :, :], ps[:, 4 * (n % 2) + 2:4 * (n % 2) + 4, 0:HALF],
                                     ALU.mult), s_step)
                step(v.tensor_tensor(mt[:, j, HALF * hf:HALF * (hf + 1)], part[:, 0, :], part[:, 1, :], ALU.add),
                     s_mt)
            dve.wait_ge(s_x, 32)
            dve.wait_ge(s_ln, 16)
            for n in range(2 * NT):
                t, c = n % NT, n // NT
                q = queries_of(t)
                dve.wait_ge(s_y, n + 1)
                step(v.tensor_tensor(m.x[0:q, t, 512 * c:512 * (c + 1)], ps[0:q, n % 8, :],
                                     m.x[0:q, t, 512 * c:512 * (c + 1)], ALU.add), s_res)
            for t in range(NT):
                q = queries_of(t)
                if t:
                    dve.wait_ge(s_hT, 2 * t)
                step(v.tensor_tensor_reduce(out=xs[0:q, :], in0=m.x[0:q, t, :], in1=m.x[0:q, t, :], scale=1.0,
                                            scalar=0.0, op0=ALU.mult, op1=ALU.add, accum_out=st[0:q, 0:1]), s_step)
                v.tensor_scalar(st[:, 1:2], st[:, 0:1], 1.0 / D, EPS, ALU.mult, ALU.add).then_inc(s_ms, 1)
                dve.wait_ge(s_rt, t + 1)
                step(v.reciprocal(st[:, 3:4], st[:, 2:3]), s_step)
                step(v.tensor_scalar(xs[0:q, :], m.x[0:q, t, :], st[0:q, 3:4], None, ALU.mult), s_xs)
                for j in range(2):
                    n = 2 * t + j
                    dve.wait_ge(s_hT, n + 1)
                    v.tensor_tensor(m.h2t[:, 4 * j:4 * j + 4, P * t:P * t + q],
                                    ps[:, n % 8, :].rearrange("p (c k) -> p c k", c=4)[:, :, 0:q],
                                    last(ln2[:, 4 * j:4 * j + 4], q), ALU.mult).then_inc(s_h2, 1)


def retrieve(nc, io, m, sem):
    lo = Plan(nc, m.after_x)
    m.slots = lo("slots", [P, 3, NQ])
    m.after_slots = lo.at
    pl = Plan(nc, m.after_slots)
    wq = [pl(f"wq{i}", [P, DC, P]) for i in range(3)]
    keyb = pl("keyb", [P, PH, 2, NKEY])
    qh = pl("qh", [P, PH, NQ])
    sc = [pl(f"sc{i}", [P, PH, 2, NKEY]) for i in range(2)]
    work = pl("work", [P, NKEY * 2])
    val = pl("val", [P, PH, 2, TOPE])
    ind = pl("ind", [P, PH, 2, TOPE], U32)
    cand = pl("cand", [P, PH, TOPE * TOPE])
    top = pl("top", [P, PH, TOPE])
    pos = pl("pos", [P, PH, TOPE], U32)
    posb = pl("posb", [P, 2, SLOTS], U32)
    posf = pl("posf", [P, 2, SLOTS])
    indf = pl("indf", [P, PH, 2, TOPE])
    hot = pl("hot", [P, SLOTS, TOPE])
    num = pl("num", [P, TOPE])
    pick = [pl(f"pick{i}", [P, 3, SLOTS]) for i in range(2)]
    ssum = pl("ssum", [P, 2, PH])
    assert pl.at <= m.end, pl.at
    ident = m.ident

    with nc.psum_tensor("ps_r", [P, 8, 512], F32) as ps, nc.Block() as block:
        s_wq = [sem(f"d_wq{i}") for i in range(3)]
        s_key = sem("d_key")
        s_zero = sem("d_zero")
        s_num = sem("d_num")
        s_q = sem("d_q")
        s_qc = sem("d_qc")
        s_s = sem("d_s")
        s_sc = sem("d_sc")
        s_used = sem("d_used")
        s_step = sem("d_step")
        s_shift = sem("d_shift")
        s_exp = sem("d_exp")
        s_pick = sem("d_pick")
        s_turn = sem("d_turn")
        s_slot = sem("d_slot")

        @block.sync
        def _(sp):
            for h in range(PH):
                if h >= 3:
                    sp.wait_ge(s_q, h - 2)
                sp.dma_start(wq[h % 3][:, :, :], io.peer_wq[h, :, :, :]).then_inc(s_wq[h % 3], 16)

        @block.gpsimd
        def _(pool):
            nc.gpsimd.memset(keyb[:, :, :, :], 0.0).then_inc(s_zero, 1)
            nc.gpsimd.iota(num[:, :], [[1, TOPE]], base=0, channel_multiplier=0,
                           allow_small_or_imprecise_dtypes=True).then_inc(s_num, 1)
            pool.wait_ge(s_zero, 1)
            for a in range(2):
                pool.dma_start(keyb[HD * a:HD * (a + 1), :, a, :], io.subkeys[a, :, :, :]).then_inc(s_key, 16)

        @block.tensor
        def _(pe):
            for h in range(PH):
                pe.wait_ge(s_wq[h % 3], 16 * (h // 3 + 1))
                if h >= 2:
                    pe.wait_ge(s_qc, h - 1)
                for hf in range(2):
                    for k in range(DC):
                        ins = nc.tensor.matmul(ps[:, 4 + 2 * (h % 2) + hf, 0:HALF], wq[h % 3][:, k, :],
                                               m.h2t[:, k, HALF * hf:HALF * (hf + 1)],
                                               start=(k == 0), stop=(k == DC - 1))
                ins.then_inc(s_q, 1)
            pe.wait_ge(s_qc, PH)
            pe.wait_ge(s_key, 32)

            def scores(t):
                q = queries_of(t)
                for g in range(4):
                    n = 4 * t + g
                    if n >= 4:
                        pe.wait_ge(s_sc, n - 3)
                    for i in range(2):
                        ins = nc.tensor.matmul(ps[0:q, g, 2 * NKEY * i:2 * NKEY * (i + 1)],
                                               qh[:, 2 * g + i, P * t:P * t + q],
                                               keyb[:, 2 * g + i, :, :].rearrange("p a k -> p (a k)"),
                                               start=True, stop=True)
                    ins.then_inc(s_s, 1)

            def turn(t):
                q = queries_of(t)
                pe.wait_ge(s_pick, t + 1)
                if t >= 2:
                    pe.wait_ge(s_slot, t - 1)
                for i in range(3):
                    ins = nc.tensor.transpose(ps[:, 4 + t % 2, P * i:P * i + q], pick[t % 2][0:q, i, :], ident[0:q, 0:q])
                ins.then_inc(s_turn, 1)

            scores(0)
            for t in range(NT):
                if t + 1 < NT:
                    scores(t + 1)
                turn(t)

        @block.scalar
        def _(act):
            for h in range(PH):
                act.wait_ge(s_q, h + 1)
                nc.scalar.copy(qh[:, h, :].rearrange("p (a k) -> p a k", a=2),
                               ps[:, 4 + 2 * (h % 2):6 + 2 * (h % 2), 0:HALF]).then_inc(s_qc, 1)

            def copy_scores(t):
                q = queries_of(t)
                if t >= 2:
                    act.wait_ge(s_used, t - 1)
                for g in range(4):
                    act.wait_ge(s_s, 4 * t + g + 1)
                    nc.scalar.copy(sc[t % 2][0:q, 2 * g:2 * g + 2, :, :].rearrange("p h a k -> p (h a k)"),
                                   ps[0:q, g, :]).then_inc(s_sc, 1)

            copy_scores(0)
            for t in range(NT):
                q = queries_of(t)
                if t + 1 < NT:
                    copy_scores(t + 1)
                act.wait_ge(s_shift, t + 1)
                nc.scalar.activation(top[0:q, :, :], top[0:q, :, :], ACT.Exp).then_inc(s_exp, 1)
                act.wait_ge(s_turn, t + 1)
                nc.scalar.copy(m.slots[:, :, P * t:P * t + q],
                               ps[:, 4 + t % 2, 0:3 * P].rearrange("p (i k) -> p i k", i=3)[:, :, 0:q]
                               ).then_inc(s_slot, 1)

        @block.vector
        def _(dve):
            step = Chain(dve)
            v = nc.vector

            def top16(values, where, src, scratch):
                step(v.max(values[:, 0:8], src), s_step)
                v.max_index(where[:, 0:8], values[:, 0:8], src)
                step(v.match_replace(scratch, values[:, 0:8], src, TAKEN), s_step)
                step(v.max(values[:, 8:16], scratch), s_step)
                return v.max_index(where[:, 8:16], values[:, 8:16], scratch)

            dve.wait_ge(s_num, 1)
            for t in range(NT):
                q = queries_of(t)
                dve.wait_ge(s_sc, 4 * t + 4)
                for h in range(PH):
                    for a in range(2):
                        ins = top16(val[0:q, h, a, :], ind[0:q, h, a, :], sc[t % 2][0:q, h, a, :],
                                    work[0:q, NKEY * a:NKEY * (a + 1)])
                step(ins, s_used)
                c4 = cand[0:q].rearrange("p h (i j) -> p h i j", i=TOPE)
                step(v.tensor_tensor(c4, val[0:q, :, 0, :].unsqueeze(3).to_broadcast([q, PH, TOPE, TOPE]),
                                     val[0:q, :, 1, :].unsqueeze(2).to_broadcast([q, PH, TOPE, TOPE]), ALU.add),
                     s_step)
                for h in range(PH):
                    ins = top16(top[0:q, h, :], pos[0:q, h, :], cand[0:q, h, :], work[0:q, :])
                step(ins, s_step)
                v.tensor_copy(ssum[0:q, 0, :], top[0:q, :, 0])
                step(v.tensor_scalar(posb[0:q, 0, :], pos[0:q].rearrange("p h k -> p (h k)"), 4, None,
                                     ALU.logical_shift_right), s_step)
                v.tensor_tensor(top[0:q], top[0:q], last(ssum[0:q, 0, :], TOPE), ALU.subtract).then_inc(s_shift, 1)
                step(v.tensor_scalar(posb[0:q, 1, :], pos[0:q].rearrange("p h k -> p (h k)"), TOPE - 1, None,
                                     ALU.bitwise_and), s_step)
                v.tensor_copy(posf[0:q], posb[0:q])
                step(v.tensor_copy(indf[0:q], ind[0:q]), s_step)
                if t >= 2:
                    dve.wait_ge(s_turn, t - 1)
                out = pick[t % 2]
                hot4 = hot[0:q].rearrange("p (h i) j -> p h i j", h=PH)
                for a in range(2):
                    step(v.tensor_tensor(hot[0:q], last(posf[0:q, a, :], TOPE), mid(num[0:q, :], SLOTS),
                                         ALU.is_equal), s_step)
                    step(v.tensor_tensor(hot4, hot4, indf[0:q, :, a, :].unsqueeze(2).to_broadcast([q, PH, TOPE, TOPE]),
                                         ALU.mult), s_step)
                    step(v.tensor_reduce(out[0:q, a, :], hot[0:q], AX_X, ALU.add), s_step)
                dve.wait_ge(s_exp, t + 1)
                step(v.tensor_reduce(ssum[0:q, 0, :], top[0:q], AX_X, ALU.add), s_step)
                step(v.reciprocal(ssum[0:q, 1, :], ssum[0:q, 0, :]), s_step)
                step(v.tensor_tensor(out[0:q, 2, :].rearrange("p (h k) -> p h k", h=PH), top[0:q],
                                     last(ssum[0:q, 1, :], TOPE), ALU.mult), s_pick)


TB = 32
NB = NQ // TB
GT = 4
GPB = TB // GT
RING = 4
assert NB * TB == NQ and NB % 2 == 1


def spread(nc, io, m, sem):
    pl = Plan(nc, m.after_slots)
    left = pl("left", [P, RING, GT, NKEY])
    right = pl("right", [P, RING, GT, NKEY])
    stage = [pl(f"stage{i}", [P, NKEY, TB]) for i in range(2)]
    number = pl("number", [P, NKEY])
    assert pl.at <= m.end, pl.at
    first_key, second_key, gate = (m.slots[:, i, :] for i in range(3))

    with nc.psum_tensor("ps_s", [P, GPB, GT, NKEY], F32) as ps, nc.Block() as block:
        s_num = sem("e_num")
        s_left = sem("e_left")
        s_right = sem("e_right")
        s_prod = sem("e_prod")
        s_out = sem("e_out")
        s_store = [sem("e_store0"), sem("e_store1")]

        def all_blocks(eng, body):
            for b in range(3):
                body(b, b % 2, b == 0)
            with eng.Fori(0, (NB - 3) // 2) as i:
                body(i * 2 + 3, 1, False)
                body(i * 2 + 4, 0, False)

        def free(eng, b, k, peeled):
            if not peeled or k >= RING:
                eng.wait_ge(s_prod, b * GPB + (k - RING + 1))

        @block.gpsimd
        def _(pool):
            nc.gpsimd.iota(number[:, :], [[1, NKEY]], base=0, channel_multiplier=0,
                           allow_small_or_imprecise_dtypes=True).then_inc(s_num, 1)

        @block.vector
        def _(dve):
            dve.wait_ge(s_num, 1)

            def body(b, par, peeled):
                for k in range(GPB):
                    free(dve, b, k, peeled)
                    for j in range(GT):
                        tok = bass.ds(b * TB + (GT * k + j), 1)
                        ins = nc.vector.tensor_scalar(left[:, k % RING, j, :], number[:, :], first_key[:, tok],
                                                      gate[:, tok], ALU.is_equal, ALU.mult)
                    ins.then_inc(s_left, 1)
                    for j in range(GT):
                        tok = bass.ds(b * TB + (GT * k + j), 1)
                        ins = nc.vector.tensor_scalar(right[:, k % RING, j, :], number[:, :],
                                                      second_key[:, tok], None, ALU.is_equal)
                    ins.then_inc(s_right, 1)

            all_blocks(dve, body)

        @block.tensor
        def _(pe):
            def body(b, par, peeled):
                for k in range(GPB):
                    pe.wait_ge(s_left, b * GPB + (k + 1))
                    pe.wait_ge(s_right, b * GPB + (k + 1))
                    if not peeled:
                        pe.wait_ge(s_out, b * GPB + (k - GPB + 1))
                    for j in range(GT):
                        ins = nc.tensor.matmul(ps[:, k, j, :], left[:, k % RING, j, :], right[:, k % RING, j, :],
                                               start=True, stop=True)
                    ins.then_inc(s_prod, 1)

            all_blocks(pe, body)

        @block.scalar
        def _(act):
            def body(b, par, peeled):
                if not isinstance(b, int) or b >= 2:
                    act.wait_ge(s_store[par], (b - par) * 8 if par else b * 8)
                for k in range(GPB):
                    act.wait_ge(s_prod, b * GPB + (k + 1))
                    nc.scalar.copy(stage[par][:, :, GT * k:GT * (k + 1)],
                                   ps[:, k, :, :].rearrange("p t i -> p i t")).then_inc(s_out, 1)

            all_blocks(act, body)

        @block.sync
        def _(sp):
            def body(b, par, peeled):
                sp.wait_ge(s_out, b * GPB + GPB)
                dst = io.dense[b] if isinstance(b, int) else io.dense[bass.ds(b, 1)].squeeze(0)
                sp.dma_start(dst, stage[par][:, :, :]).then_inc(s_store[par], 16)

            all_blocks(sp, body)
            sp.wait_ge(s_store[0], 16 * (NB // 2 + 1))
            sp.wait_ge(s_store[1], 16 * (NB // 2))


EG = 4
STEPS = NKEY // EG
HB = (NB // 2 + 1, NB // 2)
HT = (HB[0] * TB, HB[1] * TB)
HOFF = (0, HT[0])
AU = 2 * EG
BU = 2 * DC


def experts(nc, io, m, sem):
    pl = Plan(nc, m.after_x)
    m.acc = pl("acc", [P, DC, NQ])
    u = pl("u", [P, 2, EG, DC, P])
    vv = pl("v", [P, 2, EG, D])
    gt = pl("gt", [P, 2, NB, EG, TB])
    w = pl("w", [P, 2, EG, NQ])
    gl = pl("gl", [P, 4, HT[0]])
    assert pl.at <= m.end, pl.at

    with nc.psum_tensor("ps_a", [P, 4, 512], F32) as ps_a, nc.psum_tensor("ps_b", [P, 4, 512], F32) as ps_b, \
            nc.Block() as block:
        s_u = [sem("f_u0"), sem("f_u1")]
        s_v = [sem("f_v0"), sem("f_v1")]
        s_g = [sem("f_g0"), sem("f_g1")]
        s_a = sem("f_a")
        s_gelu = sem("f_gelu")
        s_w = sem("f_w")
        s_b = sem("f_b")
        s_add = sem("f_add")

        def landed(eng, s_pair, s, par, n):
            eng.wait_ge(s_pair[par], (s - par) * (8 * n) + 16 * n)

        @block.sync
        def _(sp):
            def load(s, par, peeled):
                if not peeled:
                    sp.wait_ge(s_a, s * AU - AU)
                for e in range(EG):
                    src = io.peer_u[bass.ds(s * EG + e, 1)].squeeze(0)
                    sp.dma_start(u[:, par, e, :, :], src).then_inc(s_u[par], 16)
                if not peeled:
                    sp.wait_ge(s_w, s * AU - AU)
                sp.dma_start(gt[:, par, :, :, :].rearrange("p b e t -> p b (e t)"),
                             io.dense[:, :, bass.ds(s * EG, EG), :].rearrange("b p e t -> p b (e t)")
                             ).then_inc(s_g[par], 16)
                if not peeled:
                    sp.wait_ge(s_b, s * BU - BU)
                sp.dma_start(vv[:, par, :, :], io.peer_v[:, bass.ds(s * EG, EG), :]).then_inc(s_v[par], 16)

            load(0, 0, True)
            load(1, 1, True)
            with sp.Fori(0, STEPS // 2 - 1) as i:
                load(i * 2 + 2, 0, False)
                load(i * 2 + 3, 1, False)

        def steps(eng, first, both, second):
            first(0, 0, True)
            with eng.Fori(0, STEPS // 2 - 1) as i:
                first(i * 2 + 1, 1, False)
                second(i * 2, 0, both)
                first(i * 2 + 2, 0, False)
                second(i * 2 + 1, 1, False)
            first(STEPS - 1, 1, False)
            second(STEPS - 2, 0, False)
            second(STEPS - 1, 1, False)

        @block.tensor
        def _(pe):
            def products_u(s, par, peeled):
                landed(pe, s_u, s, par, EG)
                for e in range(EG):
                    for hf in range(2):
                        a = 2 * e + hf
                        if not peeled or a >= 4:
                            pe.wait_ge(s_gelu, s * AU + (a - 3))
                        for k in range(DC):
                            ins = nc.tensor.matmul(ps_a[:, a % 4, 0:HT[hf]], u[:, par, e, k, :],
                                                   m.h2t[:, k, HOFF[hf]:HOFF[hf] + HT[hf]],
                                                   start=(k == 0), stop=(k == DC - 1))
                        ins.then_inc(s_a, 1)

            def products_v(s, par, _):
                landed(pe, s_v, s, par, 1)
                pe.wait_ge(s_w, s * AU + AU)
                for c in range(DC):
                    for hf in range(2):
                        n = 2 * c + hf
                        pe.wait_ge(s_add, s * BU + max(n - 3, 0) + 1)
                        for e in range(EG):
                            ins = nc.tensor.matmul(ps_b[:, n % 4, 0:HT[hf]], vv[:, par, e, P * c:P * (c + 1)],
                                                   w[:, par, e, HOFF[hf]:HOFF[hf] + HT[hf]],
                                                   start=(e == 0), stop=(e == EG - 1))
                        ins.then_inc(s_b, 1)

            steps(pe, products_u, False, products_v)

        @block.scalar
        def _(act):
            def gelu(s, peeled):
                for a in range(AU):
                    act.wait_ge(s_a, s * AU + (a + 1))
                    if not peeled or a >= 4:
                        act.wait_ge(s_w, s * AU + (a - 3))
                    hf = a % 2
                    nc.scalar.activation(gl[:, a % 4, 0:HT[hf]], ps_a[:, a % 4, 0:HT[hf]],
                                         ACT.Gelu_apprx_tanh).then_inc(s_gelu, 1)

            gelu(0, True)
            with act.Fori(1, STEPS) as s:
                gelu(s, False)

        @block.vector
        def _(dve):
            nc.vector.memset(m.acc[:, :, :], 0.0).then_inc(s_add, 1)
            dve.wait_ge(s_add, 1)

            def weights(s, par, peeled):
                landed(dve, s_g, s, par, 1)
                if not peeled:
                    dve.wait_ge(s_b, (s - 1) * BU)
                for a in range(AU):
                    e, hf = a // 2, a % 2
                    dve.wait_ge(s_gelu, s * AU + (a + 1))
                    b0 = 0 if hf == 0 else HB[0]
                    cols = slice(HOFF[hf], HOFF[hf] + HT[hf])
                    nc.vector.tensor_tensor(w[:, par, e, cols].rearrange("p (b t) -> p b t", t=TB),
                                            gl[:, a % 4, 0:HT[hf]].rearrange("p (b t) -> p b t", t=TB),
                                            gt[:, par, b0:b0 + HB[hf], e, :], ALU.mult).then_inc(s_w, 1)

            def add(s, par, _):
                for n in range(BU):
                    c, hf = n // 2, n % 2
                    cols = slice(HOFF[hf], HOFF[hf] + HT[hf])
                    dve.wait_ge(s_b, s * BU + (n + 1))
                    nc.vector.tensor_tensor(m.acc[:, c, cols], ps_b[:, n % 4, 0:HT[hf]], m.acc[:, c, cols],
                                            ALU.add).then_inc(s_add, 1)

            steps(dve, weights, False, add)


def finish(nc, io, m, sem):
    with nc.psum_tensor("ps_f", [P, 8, 512], F32) as ps, nc.Block() as block:
        s_t = sem("g_t")
        s_y = sem("g_y")
        s_out = sem("g_out")

        @block.tensor
        def _(pe):
            for n in range(2 * NT):
                t, j = n // 2, n % 2
                q = queries_of(t)
                if n >= 8:
                    pe.wait_ge(s_y, n - 7)
                for c in range(4):
                    ins = nc.tensor.transpose(ps[0:q, n % 8, P * c:P * (c + 1)],
                                              m.acc[:, 4 * j + c, P * t:P * t + q], m.ident[:, :])
                ins.then_inc(s_t, 1)

        @block.vector
        def _(dve):
            for n in range(2 * NT):
                t, j = n // 2, n % 2
                q = queries_of(t)
                dve.wait_ge(s_t, n + 1)
                nc.vector.tensor_tensor(m.x[0:q, t, 512 * j:512 * (j + 1)], ps[0:q, n % 8, :],
                                        m.x[0:q, t, 512 * j:512 * (j + 1)], ALU.add).then_inc(s_y, 1)

        @block.sync
        def _(sp):
            for t in range(NT):
                sp.wait_ge(s_y, 2 * t + 2)
                dst = io.y_prompt[P * t:P * (t + 1), :] if t < 4 else io.y_sample[:, :]
                sp.dma_start(dst, m.x[0:queries_of(t), t, :]).then_inc(s_out, 16)
            sp.wait_ge(s_out, 16 * NT)


class Names:
    pass


def hybrid_step(nc, io):
    m = Names()
    m.end = 229344
    pl = Plan(nc, BASE)
    m.ident = pl("ident", [P, P])
    low = pl.at
    m.ht = pl("ht", [P, DC, TOK])
    m.keep = pl.at
    m.kt = pl("kt", [P, H, KEYS])
    m.qt = pl("qt", [P, H, NQ])
    m.biq = pl("biq", [P, H, NQ])
    m.bik = pl("bik", [P, KEYS])
    m.va = pl("va", [P, 7, H, AV])
    m.vb = pl("vb", [P, 7, HD])
    m.iw = pl("iw", [P, NT, H])
    m.temps = pl.at
    sem = nc.alloc_semaphore
    project(nc, io, m, sem)
    attend(nc, io, m, sem)
    merge(nc, io, m, sem)
    m.after_x = m.after_merge - DC * NQ * 4
    retrieve(nc, io, m, sem)
    spread(nc, io, m, sem)
    experts(nc, io, m, sem)
    finish(nc, io, m, sem)


def rotary_tables():
    pos = np.concatenate([META + np.arange(SEQ), PAST + np.arange(DEC), np.arange(META)]).astype(np.float32)
    parts = []
    for rot in (ROPE, BROT):
        half = rot // 2
        inv = np.float32(THETA) ** (-np.arange(half, dtype=np.float32) * np.float32(2.0 / rot))
        ang = pos[:, None] * inv.astype(np.float32)[None, :]
        c, s = np.cos(ang), np.sin(ang)
        parts += [c, c, -s, s]
    flat = np.zeros((NT * P, TABS), np.float32)
    flat[:TOK] = np.concatenate(parts, axis=1)
    return flat.reshape(NT, P, TABS).transpose(1, 0, 2)


def lay_out(x):
    a = {k: np.asarray(v) for k, v in x.items()}
    rows = lambda w: w.reshape(-1, P, w.shape[-1]).transpose(1, 0, 2)
    w_in = a["w_in"][0]
    cut = np.cumsum([QRANK, KVRANK, ROPE, H * HD, HD, HD, H * HD, H, HD, D])
    cq, ckv, kpe, bq, bk, bv, iq, iw, ik, ga, gb = np.split(w_in, cut, axis=1)
    pairs = np.stack([np.concatenate([bq, bk], 1).reshape(D, NPAIR, HD),
                      np.concatenate([iq, ik], 1).reshape(D, NPAIR, HD)], axis=2).reshape(D, -1)
    gate = np.concatenate([ga, gb], 1).reshape(DC, P, 2 * DC, P).transpose(2, 1, 0, 3)
    w_o = np.stack([rows(a["w_o_a"][0]), rows(a["w_o_b"][0])])
    g = a["a_qk_g"][0]
    gains = np.concatenate([a["a_kv_norm_g"][0], g[1, NOPE:], np.tile(a["b_qk_g"][0, 0], H), a["b_qk_g"][0, 1],
                            g[0], g[1, :NOPE]])
    return {
        "x_prompt": a["x_prompt"][0], "x_sample": a["x_sample"][0], "meta_tokens": a["meta_tokens"],
        "w_tok": rows(np.concatenate([cq, ckv, kpe, pairs, bv, iw], 1)),
        "w_gate": gate,
        "tabs": rotary_tables(),
        "gains": np.broadcast_to(gains, (P, GAINS)),
        "ln1": a["ln1_g"][0].reshape(DC, P).T, "ln2": a["ln2_g"][0].reshape(DC, P).T,
        "q_gain": a["a_q_norm_g"][0].reshape(2, P).T,
        "w_uq": rows(a["a_w_uq"][0]), "w_ukv": a["a_w_ukv"][0],
        "lat_t": a["cache_a_latent"][0, 0].T, "cache_kpe": a["cache_a_kpe"][0, 0],
        "bk_t": a["cache_b_k"][0, 0].T, "ik_t": a["cache_b_idx_k"][0, 0].T, "cache_bv": a["cache_b_v"][0, 0],
        "w_o": w_o.reshape(2, P, 4, 2, 512).transpose(3, 0, 1, 2, 4),
        "w_out": rows(a["w_out"][0]).reshape(P, DC, 2, 512).transpose(2, 0, 1, 3),
        "peer_wq": a["peer_wq"][0].reshape(DC, P, PH, P).transpose(2, 1, 0, 3),
        "subkeys": a["peer_subkeys"][0].transpose(1, 3, 0, 2),
        "peer_u": a["peer_u"][0].reshape(NKEY, NKEY, DC, P).transpose(1, 3, 2, 0),
        "peer_v": a["peer_v"][0].reshape(NKEY, NKEY, D),
    }


_OUTS = [("y_prompt", (SEQ, D)), ("y_sample", (DEC, D))]
_OUTS += [(f"new_{s}_{i}", (n, w)) for s, n in (("p", META + SEQ), ("s", DEC))
          for i, w in enumerate((KVRANK, ROPE, HD, HD, HD))]


def kernel(**inputs):
    import concourse.bacc as bacc
    from concourse.bass_utils import run_bass_kernel_spmd

    nc = bacc.Bacc("TRN2", target_bir_lowering=False, num_devices=1)
    io = Names()
    arrays = {}
    for name, a in lay_out(inputs).items():
        a = np.ascontiguousarray(a)
        arrays[f"in_{name}"] = a
        t = nc.dram_tensor(f"in_{name}", a.shape, mybir.dt.from_np(a.dtype), kind="ExternalInput").ap()
        io.__dict__[name] = t
    outs = {}
    for name, shape in _OUTS:
        outs[name] = nc.dram_tensor(f"out_{name}", shape, F32, kind="ExternalOutput").ap()
    io.y_prompt, io.y_sample = outs["y_prompt"], outs["y_sample"]
    io.new_p = [outs[f"new_p_{i}"] for i in range(5)]
    io.new_s = [outs[f"new_s_{i}"] for i in range(5)]
    io.dense = nc.dram_tensor("dense_gates", (NB, P, NKEY, TB), F32, kind="Internal").ap()
    hybrid_step(nc, io)
    got = run_bass_kernel_spmd(nc, [arrays], core_ids=[0]).results[0]
    y = [got["out_y_prompt"][None], got["out_y_sample"][None]]
    return tuple(y + [got[f"out_{name}"][None, None] for name, _ in _OUTS[2:]])
```

```python
import numpy as np
import concourse.bass as bass
from concourse import mybir

F32 = mybir.dt.float32
F32R = mybir.dt.float32r
U32 = mybir.dt.uint32
ALU = mybir.AluOpType
ACT = mybir.ActivationFunctionType
AX_X = mybir.AxisListType.X

P = 128
D = 1024
DC = D // P
SEQ, DEC, META, PAST = 512, 32, 16, 256
TOK = SEQ + DEC + META
NQ = SEQ + DEC
NT = 5
KEYS = META + SEQ + PAST + DEC
KPROMPT = META + SEQ
KCACHE = KPROMPT
KSAMPLE = KPROMPT + PAST
CHUNK = 64
EPS = 1e-6
THETA = 500000.0

H = 8
NOPE, ROPE, AV = 64, 32, 64
AQK = NOPE + ROPE
QRANK, KVRANK = 256, 128
HD = 64
BROT = HD // 4
A_SCALE = AQK ** -0.5
B_SCALE = HD ** -0.5
IDX_SCALE = (H * HD) ** -0.5
TOPK_P = min(256, SEQ // 4)
TOPK_S = min(256, (PAST + DEC) // 4)

C_KV = QRANK
C_KPE = C_KV + KVRANK
C_B = C_KPE + ROPE
NPAIR = H + 1
C_BV = C_B + NPAIR * 2 * HD
C_IW = C_BV + HD
COLS = C_IW + H
PJ = COLS // 4
assert PJ * 4 == COLS and PJ <= 512

NKEY = 128
PH = 8
TOPE = 16
SLOTS = PH * TOPE
HALF = NQ // 2
HIDE = -1e30
NEG = -3.0e38
TAKEN = -3.3e38
SEEN = -3.2e38

GAINS = KVRANK + ROPE + NPAIR * HD + AQK + NOPE
G_KPE = KVRANK
G_B = G_KPE + ROPE
G_Q = G_B + NPAIR * HD
G_KN = G_Q + AQK
TABS = 2 * ROPE + 2 * BROT


def rows_of(t):
    return P if t < 4 else DEC + META


def queries_of(t):
    return P if t < 4 else DEC


def key_columns(t):
    if t < 4:
        return [(0, P, META + P * t)]
    if t == 4:
        return [(0, DEC, KSAMPLE), (DEC, META, 0)]
    return [(0, P, KCACHE + P * (t - 5))]


class Plan:

    def __init__(self, nc, at):
        self.nc, self.at = nc, at

    def __call__(self, name, shape, dt=F32):
        size = int(np.prod(shape[1:])) * 4
        size = (size + 31) // 32 * 32
        t = self.nc.alloc_sbuf_tensor_at(name, shape, dt, offset=self.at)
        self.at += size
        return t


BASE = 16512


class Chain:

    def __init__(self, eng):
        self.eng, self.n = eng, {}

    def __call__(self, ins, sem):
        ins.then_inc(sem, 1)
        self.n[sem.name] = self.n.get(sem.name, 0) + 1
        self.eng.wait_ge(sem, self.n[sem.name])


def mid(ap, n):
    return ap.unsqueeze(1).to_broadcast([ap.shape[0], n, ap.shape[1]])


def last(ap, n):
    return ap.unsqueeze(2).to_broadcast([ap.shape[0], ap.shape[1], n])


def project(nc, io, m, sem):
    pl = Plan(nc, m.temps)
    w_tok = pl("w_tok", [P, DC, COLS])
    x2 = [pl(f"xa{i}", [P, D]) for i in range(2)]
    xs = pl("xs", [P, D])
    pr = [pl(f"pr{i}", [P, COLS]) for i in range(2)]
    qf = pl("qf", [P, H, AQK])
    kf = pl("kf", [P, H, AQK])
    t1 = pl("t1", [P, 18 * BROT])
    t2 = pl("t2", [P, 18 * BROT])
    w_uq = pl("w_uq", [P, 2, H * AQK])
    w_ukv = pl("w_ukv", [P, H * (NOPE + AV)])
    gains = pl("gains", [P, GAINS])
    tabs = pl("tabs", [P, NT, TABS])
    latc = pl("latc", [P, PAST])
    lat = pl("lat", [P, P])
    cq = pl("cq", [P, 2, P])
    kpec = pl("kpec", [P, 2, ROPE])
    ln1 = pl("ln1", [P, DC])
    qg = pl("qg", [P, 2])
    stx = pl("stx", [P, 4])
    stp = pl("stp", [P, 3, 16])
    stq = pl("stq", [P, 3, 24])
    inv_n = pl("inv_n", [P, 16])
    assert pl.at <= m.end
    ident = m.ident

    psum = lambda name, shape: nc.psum_tensor(name, shape, F32)
    with psum("ps_x", [P, DC, P]) as ps_x, psum("ps_pj", [P, 2, 512]) as ps_pj, \
            psum("ps_tr", [P, 2, 4, P]) as ps_tr, psum("ps_mm", [P, 2, 512]) as ps_mm, nc.Block() as block:
        s_x = [sem(f"a_x{t}") for t in range(NT)]
        s_win = sem("a_win")
        s_small = sem("a_small")
        s_kpec = sem("a_kpec")
        s_step = sem("a_step")
        s_ms_x = sem("a_ms_x")
        s_rt_x = sem("a_rt_x")
        s_xs = sem("a_xs")
        s_xT = sem("a_xT")
        s_hT = sem("a_hT")
        s_proj = sem("a_proj")
        s_pr = sem("a_pr")
        s_ms_p = sem("a_ms_p")
        s_rt_p = sem("a_rt_p")
        s_norm = sem("a_norm")
        s_tr = sem("a_tr")
        s_trc = sem("a_trc")
        s_mm = sem("a_mm")
        s_mmc = sem("a_mmc")
        s_ms_q = sem("a_ms_q")
        s_rt_q = sem("a_rt_q")
        s_qk = sem("a_qk")
        s_kv = sem("a_kv")
        s_ident = sem("a_ident")
        s_out = [sem("a_out0"), sem("a_out1")]

        groups = []
        for t in range(NT):
            groups.append((t, "lat", 0))
            groups += [(t, "pair", g) for g in range(3)]
            groups += [(t, "q", 0), (t, "q", 1), (t, "k", 0), (t, "k", 1)]
        for t in (5, 6):
            groups += [(t, "k", 0), (t, "k", 1)]
        index = {g: n for n, g in enumerate(groups)}
        halves = [(t, k, j) for t in range(NT) for k in ("q", "kv") for j in range(2)]
        halves += [(t, "kv", j) for t in (5, 6) for j in range(2)]
        mm_index = {g: n for n, g in enumerate(halves)}

        def pair(buf, g):
            return buf[:, C_B + 2 * HD * g:C_B + 2 * HD * (g + 1)]

        @block.sync
        def _(sp):
            def load_x(t):
                if t < 4:
                    sp.dma_start(x2[t % 2][:, :], io.x_prompt[P * t:P * (t + 1), :]).then_inc(s_x[t], 16)
                else:
                    sp.dma_start(x2[t % 2][0:DEC, :], io.x_sample[:, :]).then_inc(s_x[t], 16)
                    sp.dma_start(x2[t % 2][DEC:DEC + META, :], io.meta_tokens[:, :]).then_inc(s_x[t], 16)

            load_x(0)
            for c in range(DC):
                sp.dma_start(w_tok[:, c, :], io.w_tok[:, c, :]).then_inc(s_win, 16)
            load_x(1)
            for t in range(NT):
                if t + 2 < NT:
                    sp.wait_ge(s_xs, t + 1)
                    load_x(t + 2)
                sp.wait_ge(s_norm, t + 1)
                buf = pr[t % 2]
                for dst, c0, n in ((0, C_KV, KVRANK), (1, C_KPE, ROPE), (2, C_B + 2 * HD * H, HD),
                                   (3, C_BV, HD), (4, C_B + 2 * HD * H + HD, HD)):
                    if t < 4:
                        sp.dma_start(io.new_p[dst][META + P * t:META + P * (t + 1), :],
                                     buf[:, c0:c0 + n]).then_inc(s_out[t % 2], 16)
                    else:
                        sp.dma_start(io.new_s[dst][:, :], buf[0:DEC, c0:c0 + n]).then_inc(s_out[0], 16)
                        sp.dma_start(io.new_p[dst][0:META, :],
                                     buf[DEC:DEC + META, c0:c0 + n]).then_inc(s_out[0], 16)
            sp.wait_ge(s_out[0], 16 * 5 * 4)
            sp.wait_ge(s_out[1], 16 * 5 * 2)

        @block.gpsimd
        def _(pool):
            nc.gpsimd.memset(ident[:, :], 0.0).then_inc(s_ident, 1)
            pool.wait_ge(s_ident, 1)
            nc.gpsimd.affine_select(out=ident[:, :], in_=ident[:, :], compare_op=ALU.not_equal, fill=1.0,
                                    base=0, pattern=[[-1, P]], channel_multiplier=1).then_inc(s_ident, 1)

        @block.scalar
        def _(act):
            act.dma_start(gains[:, :], io.gains[:, :]).then_inc(s_small, 16)
            act.dma_start(tabs[:, :, :], io.tabs[:, :, :]).then_inc(s_small, 16)
            act.dma_start(ln1[:, :], io.ln1[:, :]).then_inc(s_small, 16)
            act.dma_start(qg[:, :], io.q_gain[:, :]).then_inc(s_small, 16)
            act.dma_start(w_uq[:, :, :], io.w_uq[:, :, :]).then_inc(s_small, 16)
            act.dma_start(w_ukv[:, :], io.w_ukv[:, :]).then_inc(s_small, 16)
            act.dma_start(latc[:, :], io.lat_t[:, :]).then_inc(s_small, 16)
            act.dma_start(kpec[:, :, :], io.cache_kpe[:, :].rearrange("(a p) r -> p a r", p=P)).then_inc(s_kpec, 16)
            act.dma_start(m.bik[0:HD, KCACHE:KSAMPLE], io.bk_t[:, :]).then_inc(s_kpec, 16)
            act.dma_start(m.bik[HD:P, KCACHE:KSAMPLE], io.ik_t[:, :]).then_inc(s_kpec, 16)
            for a in range(2):
                act.dma_start(m.vb[:, 5 + a, :], io.cache_bv[P * a:P * (a + 1), :]).then_inc(s_kpec, 16)
            act.wait_ge(s_small, 16 * 7)

            def root(n_sem, r_sem, n, dst, src):
                act.wait_ge(n_sem, n)
                nc.scalar.activation(dst, src, ACT.Sqrt).then_inc(r_sem, 1)

            def proj_out(t):
                r = rows_of(t)
                for c in range(4):
                    act.wait_ge(s_proj, 4 * t + c + 1)
                    if c == 0 and t >= 2:
                        act.wait_ge(s_out[t % 2], 16 * 5 * (t // 2))
                        act.wait_ge(s_tr, index[(t - 2, "pair", 2)] + 1)
                    nc.scalar.copy(pr[t % 2][0:r, PJ * c:PJ * (c + 1)],
                                   ps_pj[0:r, c % 2, 0:PJ]).then_inc(s_pr, 1)

            def tr_out(key):
                t, kind, g = key
                n = index[key]
                r = rows_of(t) if t < NT else P
                bank = ps_tr[:, n % 2, :, :]
                act.wait_ge(s_tr, n + 1)
                if kind == "lat":
                    act.wait_ge(s_mm, mm_index[(t - 1, "kv", 1)] + 1) if t else None
                    for j in range(2):
                        nc.scalar.activation(cq[:, j, 0:r], bank[:, j, 0:r], ACT.Copy, scale=qg[:, j:j + 1])
                    nc.scalar.copy(lat[:, 0:r], bank[:, 2, 0:r]).then_inc(s_trc, 1)
                    return
                moves = []
                for r0, nr, k0 in key_columns(t):
                    if kind == "pair" and g == 2:
                        moves.append((m.bik[:, k0:k0 + nr], bank[:, 0, r0:r0 + nr]))
                    if kind == "k":
                        moves.append((m.kt[0:AQK, 4 * g:4 * g + 4, k0:k0 + nr], bank[0:AQK, :, r0:r0 + nr]))
                nq = queries_of(t)
                if kind == "pair" and g < 2:
                    moves.append((m.biq[:, 4 * g:4 * g + 4, P * t:P * t + nq], bank[:, :, 0:nq]))
                if kind == "q":
                    moves.append((m.qt[0:AQK, 4 * g:4 * g + 4, P * t:P * t + nq], bank[0:AQK, :, 0:nq]))
                for i, (dst, src) in enumerate(moves):
                    ins = nc.scalar.copy(dst, src)
                ins.then_inc(s_trc, 1)

            def mm_out(t, kind):
                r = rows_of(t) if t < NT else P
                for j in range(2):
                    act.wait_ge(s_mm, mm_index[(t, kind, j)] + 1)
                    if kind == "q":
                        if j == 0 and t:
                            act.wait_ge(s_tr, index[(t - 1, "q", 1)] + 1)
                        nc.scalar.copy(qf[0:r, 4 * j:4 * j + 4, :],
                                       ps_mm[0:r, j, 0:4 * AQK].rearrange("p (h c) -> p h c", h=4)
                                       ).then_inc(s_mmc, 1)
                    else:
                        if j == 0 and t:
                            act.wait_ge(s_tr, index[(t - 1, "k", 1)] + 1)
                        kv = ps_mm[0:r, j, :].rearrange("p (h c) -> p h c", h=4)
                        nc.scalar.copy(kf[0:r, 4 * j:4 * j + 4, 0:NOPE], kv[:, :, 0:NOPE])
                        nc.scalar.copy(m.va[0:r, t, 4 * j:4 * j + 4, :], kv[:, :, NOPE:]).then_inc(s_mmc, 1)

            root(s_ms_x, s_rt_x, 1, stx[:, 2:3], stx[:, 1:2])
            proj_out(0)
            for t in range(NT):
                root(s_ms_p, s_rt_p, t + 1, stp[:, 2, 0:12], stp[:, 1, 0:12])
                if t + 1 < NT:
                    root(s_ms_x, s_rt_x, t + 2, stx[:, 2:3], stx[:, 1:2])
                tr_out((t, "lat", 0))
                mm_out(t, "q")
                mm_out(t, "kv")
                root(s_ms_q, s_rt_q, t + 1, stq[:, 2, 0:24], stq[:, 1, 0:24])
                if t + 1 < NT:
                    proj_out(t + 1)
                for g in range(3):
                    tr_out((t, "pair", g))
                for g in range(2):
                    tr_out((t, "q", g))
                for g in range(2):
                    tr_out((t, "k", g))
            for t in (5, 6):
                mm_out(t, "kv")
                root(s_ms_q, s_rt_q, t + 1, stq[:, 2, 16:24], stq[:, 1, 16:24])
                for g in range(2):
                    tr_out((t, "k", g))
            act.wait_ge(s_kpec, 16 * 5)

        @block.vector
        def _(dve):
            step = Chain(dve)
            v = nc.vector
            for j, (n, lo, hi) in enumerate(((QRANK, 0, 1), (KVRANK, 1, 2), (ROPE, 2, 3), (HD, 3, 12))):
                v.memset(inv_n[:, lo:hi], 1.0 / n)
            for buf in (stx, stp, stq):
                step(v.memset(buf[:], 1.0), s_step)

            def x_scale(t):
                r = rows_of(t)
                dve.wait_ge(s_x[t], 16 if t < 4 else 32)
                if t:
                    dve.wait_ge(s_xT, DC * t)
                step(v.tensor_tensor_reduce(out=xs[0:r, :], in0=x2[t % 2][0:r, :], in1=x2[t % 2][0:r, :],
                                            scale=1.0, scalar=0.0, op0=ALU.mult, op1=ALU.add,
                                            accum_out=stx[0:r, 0:1]), s_step)
                v.tensor_scalar(stx[:, 1:2], stx[:, 0:1], 1.0 / D, EPS, ALU.mult, ALU.add).then_inc(s_ms_x, 1)
                dve.wait_ge(s_rt_x, t + 1)
                step(v.reciprocal(stx[:, 3:4], stx[:, 2:3]), s_step)
                step(v.tensor_scalar(xs[0:r, :], x2[t % 2][0:r, :], stx[0:r, 3:4], None, ALU.mult), s_xs)

            def hT_out(t):
                r = rows_of(t)
                for j in range(2):
                    dve.wait_ge(s_xT, DC * t + 4 * (j + 1))
                    v.tensor_tensor(m.ht[:, 4 * j:4 * j + 4, P * t:P * t + r], ps_x[:, 4 * j:4 * j + 4, 0:r],
                                    last(ln1[:, 4 * j:4 * j + 4], r), ALU.mult).then_inc(s_hT, 1)

            def rotate(x, cos, sin, n, half):
                r = x.shape[0]
                a = t1[0:r, 0:2 * n * half].rearrange("p (n k) -> p n k", n=n)
                b = t2[0:r, 0:2 * n * half].rearrange("p (n k) -> p n k", n=n)
                v.tensor_tensor(a, x, mid(cos, n), ALU.mult)
                v.tensor_tensor(b[:, :, 0:half], x[:, :, half:2 * half], mid(sin[:, 0:half], n), ALU.mult)
                step(v.tensor_tensor(b[:, :, half:2 * half], x[:, :, 0:half],
                                     mid(sin[:, half:2 * half], n), ALU.mult), s_step)
                return v.tensor_tensor(x, a, b, ALU.add)

            def p_norm(t):
                r = rows_of(t)
                buf = pr[t % 2][0:r]
                pairs = buf[:, C_B:C_BV].rearrange("p (n k) -> p n k", n=NPAIR)
                dve.wait_ge(s_pr, 4 * t + 4)
                if t == 0:
                    dve.wait_ge(s_small, 16 * 7)
                sq = xs[0:r, :]
                dve.wait_ge(s_xT, DC * (t + 1))
                v.tensor_tensor(sq[:, 0:C_B], buf[:, 0:C_B], buf[:, 0:C_B], ALU.mult)
                sqb = sq[:, C_B:C_B + NPAIR * HD].rearrange("p (n k) -> p n k", n=NPAIR)
                step(v.tensor_tensor(sqb, pairs[:, :, 0:HD], pairs[:, :, 0:HD], ALU.mult), s_step)
                v.tensor_reduce(stp[0:r, 0, 0:1], sq[:, 0:C_KV], AX_X, ALU.add)
                v.tensor_reduce(stp[0:r, 0, 1:2], sq[:, C_KV:C_KPE], AX_X, ALU.add)
                v.tensor_reduce(stp[0:r, 0, 2:3], sq[:, C_KPE:C_B], AX_X, ALU.add)
                step(v.tensor_reduce(stp[0:r, 0, 3:12], sqb, AX_X, ALU.add), s_step)
                step(v.tensor_tensor(stp[:, 1, 0:12], stp[:, 0, 0:12], inv_n[:, 0:12], ALU.mult), s_step)
                v.tensor_scalar(stp[:, 1, 0:12], stp[:, 1, 0:12], EPS, None, ALU.add).then_inc(s_ms_p, 1)
                v.tensor_copy(m.vb[0:r, t, :], buf[:, C_BV:C_IW])
                v.tensor_scalar(m.iw[0:r, t, :], buf[:, C_IW:COLS], IDX_SCALE, None, ALU.mult)
                dve.wait_ge(s_rt_p, t + 1)
                step(v.reciprocal(stp[:, 2, 0:12], stp[:, 2, 0:12]), s_step)
                rs = stp[0:r, 2, :]
                v.tensor_scalar(buf[:, 0:C_KV], buf[:, 0:C_KV], rs[:, 0:1], None, ALU.mult)
                v.scalar_tensor_tensor(out=buf[:, C_KV:C_KPE], in0=buf[:, C_KV:C_KPE], scalar=rs[:, 1:2],
                                       in1=gains[0:r, 0:G_KPE], op0=ALU.mult, op1=ALU.mult)
                v.scalar_tensor_tensor(out=buf[:, C_KPE:C_B], in0=buf[:, C_KPE:C_B], scalar=rs[:, 2:3],
                                       in1=gains[0:r, G_KPE:G_B], op0=ALU.mult, op1=ALU.mult)
                step(v.tensor_tensor(pairs[:, :, 0:HD], pairs[:, :, 0:HD], last(rs[:, 3:12], HD), ALU.mult),
                     s_step)
                step(v.tensor_tensor(pairs[:, :, 0:HD], pairs[:, :, 0:HD],
                                     gains[0:r, G_B:G_Q].rearrange("p (n k) -> p n k", n=NPAIR), ALU.mult),
                     s_step)
                tab = tabs[0:r, t, :]
                step(rotate(buf[:, C_KPE:C_B].unsqueeze(1), tab[:, 0:ROPE], tab[:, ROPE:2 * ROPE], 1, ROPE // 2),
                     s_step)
                heads = buf[:, C_B:C_BV].rearrange("p (n k) -> p n k", n=2 * NPAIR)
                step(rotate(heads[:, :, 0:BROT], tab[:, 2 * ROPE:2 * ROPE + BROT],
                            tab[:, 2 * ROPE + BROT:TABS], 2 * NPAIR, BROT // 2), s_norm)

            def qk_norm(t):
                r = rows_of(t) if t < NT else P
                new = t < NT
                sq = xs[0:r, 0:H * AQK].rearrange("p (h c) -> p h c", h=H)
                lo = 0 if new else 16
                if new:
                    dve.wait_ge(s_mmc, mm_index[(t, "q", 1)] + 1)
                    step(v.tensor_tensor(sq, qf[0:r], qf[0:r], ALU.mult), s_step)
                    v.tensor_reduce(stq[0:r, 0, 0:8], sq[:, :, 0:NOPE], AX_X, ALU.add)
                    step(v.tensor_reduce(stq[0:r, 0, 8:16], sq[:, :, NOPE:], AX_X, ALU.add), s_step)
                dve.wait_ge(s_mmc, mm_index[(t, "kv", 1)] + 1)
                step(v.tensor_tensor(sq[:, :, 0:NOPE], kf[0:r, :, 0:NOPE], kf[0:r, :, 0:NOPE], ALU.mult), s_step)
                step(v.tensor_reduce(stq[0:r, 0, 16:24], sq[:, :, 0:NOPE], AX_X, ALU.add), s_step)
                if new:
                    v.tensor_scalar(stq[:, 1, 8:16], stq[:, 0, 8:16], 1.0 / ROPE, EPS, ALU.mult, ALU.add)
                    v.tensor_scalar(stq[:, 1, 0:8], stq[:, 0, 0:8], 1.0 / NOPE, EPS, ALU.mult, ALU.add)
                step(v.tensor_scalar(stq[:, 1, 16:24], stq[:, 0, 16:24], 1.0 / NOPE, EPS, ALU.mult, ALU.add),
                     s_ms_q)
                dve.wait_ge(s_rt_q, t + 1)
                step(v.reciprocal(stq[:, 2, lo:24], stq[:, 2, lo:24]), s_step)
                rs = stq[0:r, 2, :]
                q, k = qf[0:r], kf[0:r]
                if new:
                    v.tensor_tensor(q[:, :, 0:NOPE], q[:, :, 0:NOPE], last(rs[:, 0:8], NOPE), ALU.mult)
                    v.tensor_tensor(q[:, :, NOPE:], q[:, :, NOPE:], last(rs[:, 8:16], ROPE), ALU.mult)
                step(v.tensor_tensor(k[:, :, 0:NOPE], k[:, :, 0:NOPE], last(rs[:, 16:24], NOPE), ALU.mult), s_step)
                if new:
                    v.tensor_tensor(q, q, mid(gains[0:r, G_Q:G_KN], H), ALU.mult)
                kpe = pr[t % 2][0:r, C_KPE:C_B] if new else kpec[:, t - 5, :]
                if t == 5:
                    dve.wait_ge(s_kpec, 16 * 5)
                v.tensor_copy(k[:, :, NOPE:], mid(kpe, H))
                step(v.tensor_tensor(k[:, :, 0:NOPE], k[:, :, 0:NOPE], mid(gains[0:r, G_KN:GAINS], H), ALU.mult),
                     s_step)
                if new:
                    tab = tabs[0:r, t, :]
                    rotate(q[:, :, NOPE:], tab[:, 0:ROPE], tab[:, ROPE:2 * ROPE], H, ROPE // 2).then_inc(s_qk, 1)
                else:
                    v.tensor_copy(stx[:, 0:1], stx[:, 1:2]).then_inc(s_qk, 1)

            x_scale(0)
            hT_out(0)
            for t in range(NT):
                p_norm(t)
                if t + 1 < NT:
                    x_scale(t + 1)
                    hT_out(t + 1)
                qk_norm(t)
            for t in (5, 6):
                qk_norm(t)

        @block.tensor
        def _(pe):
            def x_transposes(t):
                r = rows_of(t)
                pe.wait_ge(s_xs, t + 1)
                if t:
                    pe.wait_ge(s_hT, 2 * t)
                for c in range(DC):
                    nc.tensor.transpose(ps_x[:, c, 0:r], xs[0:r, P * c:P * (c + 1)],
                                        ident[0:r, 0:r]).then_inc(s_xT, 1)

            def projection(t):
                r = rows_of(t)
                pe.wait_ge(s_hT, 2 * t + 2)
                if t == 0:
                    pe.wait_ge(s_win, 16 * DC)
                for c in range(4):
                    if 4 * t + c >= 2:
                        pe.wait_ge(s_pr, 4 * t + c - 1)
                    for k in range(DC):
                        ins = nc.tensor.matmul(ps_pj[0:r, c % 2, 0:PJ], m.ht[:, k, P * t:P * t + r],
                                               w_tok[:, k, PJ * c:PJ * (c + 1)], start=(k == 0), stop=(k == DC - 1))
                    ins.then_inc(s_proj, 1)

            def turn(key):
                t, kind, g = key
                n = index[key]
                r = rows_of(t) if t < NT else P
                buf = pr[t % 2][0:r]
                if n >= 2:
                    pe.wait_ge(s_trc, n - 1)
                if kind == "lat":
                    pe.wait_ge(s_norm, t + 1)
                    srcs = [buf[:, 0:P], buf[:, P:2 * P], buf[:, C_KV:C_KPE]]
                elif kind == "pair":
                    srcs = [pair(buf, i) for i in (range(4 * g, 4 * g + 4) if g < 2 else [H])]
                else:
                    pe.wait_ge(s_qk, t + 1)
                    src = qf if kind == "q" else kf
                    srcs = [src[0:r, i, :] for i in range(4 * g, 4 * g + 4)]
                for j, s in enumerate(srcs):
                    ins = nc.tensor.transpose(ps_tr[0:s.shape[1], n % 2, j, 0:r], s, ident[0:r, 0:r])
                ins.then_inc(s_tr, 1)

            def up(t, kind):
                r = rows_of(t) if t < NT else P
                for j in range(2):
                    n = mm_index[(t, kind, j)]
                    if n >= 2:
                        pe.wait_ge(s_mmc, n - 1)
                    if kind == "q":
                        for k in range(2):
                            ins = nc.tensor.matmul(ps_mm[0:r, j, 0:4 * AQK], cq[:, k, 0:r],
                                                   w_uq[:, k, 4 * AQK * j:4 * AQK * (j + 1)],
                                                   start=(k == 0), stop=(k == 1))
                    else:
                        left = lat[:, 0:r] if t < NT else latc[:, P * (t - 5):P * (t - 4)]
                        ins = nc.tensor.matmul(ps_mm[0:r, j, :], left, w_ukv[:, 512 * j:512 * (j + 1)],
                                               start=True, stop=True)
                    ins.then_inc(s_mm, 1)

            pe.wait_ge(s_ident, 2)
            x_transposes(0)
            projection(0)
            for t in range(NT):
                turn((t, "lat", 0))
                pe.wait_ge(s_trc, index[(t, "lat", 0)] + 1)
                if t == 0:
                    pe.wait_ge(s_small, 16 * 7)
                up(t, "q")
                up(t, "kv")
                if t + 1 < NT:
                    x_transposes(t + 1)
                    projection(t + 1)
                for g in range(3):
                    turn((t, "pair", g))
                for kind in ("q", "k"):
                    for g in range(2):
                        turn((t, kind, g))
            for t in (5, 6):
                up(t, "kv")
                for g in range(2):
                    turn((t, "k", g))


def attend(nc, io, m, sem):
    pl = Plan(nc, m.temps)
    m.oab = pl("oab", [P, NT, 2, H * AV])
    m.sg = pl("sg", [P, 2, DC, NQ])
    m.after_attend = pl.at
    wg = [pl(f"wg{i}", [P, DC, P]) for i in range(2)]
    vm = pl("vm", [META, H * AV + HD])
    biasA = pl("biasA", [P, KPROMPT])
    biasB = pl("biasB", [P, KPROMPT])
    score = pl("score", [P, KPROMPT])
    rel = [pl(f"rel{i}", [P, KPROMPT]) for i in range(2)]
    logit = [pl(f"logit{i}", [P, KPROMPT]) for i in range(3)]
    prob = [pl(f"prob{i}", [P, KPROMPT]) for i in range(3)]
    probT = [pl(f"probT{i}", [P, NT, P]) for i in range(2)]
    best = pl("best", [P, 8])
    mx = pl("mx", [P, 3, 2])
    total = pl("total", [P, 2, 2, H])
    inv = pl("inv", [P, H])
    assert pl.at <= m.end
    ident = m.ident

    units = [(t, kind, h) for t in range(NT) for kind in ("index", "mla", "dsa") for h in range(H)]
    N = len(units)
    number = {u: n for n, u in enumerate(units)}
    att = [n for n, u in enumerate(units) if u[1] != "index"]
    att_no = {n: i for i, n in enumerate(att)}
    idx_no = {n: i for i, n in enumerate(n for n, u in enumerate(units) if u[1] == "index")}
    TURN, VALUES, LAG = 2, 3, 3
    gates = [(g // 2, g % 2) for g in range(4 * DC)]
    gate_at = {2 * g: g for g in range(len(gates))}
    assert 2 * len(gates) < number[(3, "index", 0)]

    def keys(t):
        return (0, META + P * (t + 1)) if t < 4 else (KPROMPT, PAST + DEC)

    def blocks(t):
        if t < 4:
            return [(META + P * j, P, j) for j in range(t + 1)] + [(0, META, None)]
        return [(0, P, 5), (P, P, 6), (PAST, DEC, 4)]

    def value(kind, h, r, j):
        if kind == "mla":
            return m.va[0:r, j, h, :] if j is not None else vm[0:r, AV * h:AV * (h + 1)]
        return m.vb[0:r, j, :] if j is not None else vm[0:r, H * AV:]

    def halves(buf, t):
        q, nk = queries_of(t), keys(t)[1]
        return buf[0:q, 0:nk].rearrange("p (a k) -> p a k", a=2)

    psum = lambda name, shape: nc.psum_tensor(name, shape, F32)
    with psum("ps_sc", [P, 2, 2, 512]) as ps_sc, psum("ps_pt", [P, 4, P]) as ps_pt, \
            psum("ps_o", [P, 2, 512]) as ps_o, psum("ps_g", [P, 512]) as ps_g, nc.Block() as block:
        s_wg = [sem("b_wg0"), sem("b_wg1")]
        s_gate = sem("b_gate")
        s_gatec = sem("b_gatec")
        s_vm = sem("b_vm")
        s_step = sem("b_step")
        s_score = sem("b_score")
        s_rel = sem("b_rel")
        s_acc = sem("b_acc")
        s_logit = sem("b_logit")
        s_max = sem("b_max")
        s_prob = sem("b_prob")
        s_pt = sem("b_pt")
        s_ptc = sem("b_ptc")
        s_pv = sem("b_pv")
        s_o = sem("b_o")

        @block.sync
        def _(sp):
            sp.dma_start(vm[:, 0:H * AV], m.va[DEC:DEC + META, 4, :, :].rearrange("p h c -> p (h c)")).then_inc(s_vm, 16)
            sp.dma_start(vm[:, H * AV:], m.vb[DEC:DEC + META, 4, :]).then_inc(s_vm, 16)
            for i in range(2 * DC):
                if i >= 2:
                    sp.wait_ge(s_gate, 2 * (i - 1))
                sp.dma_start(wg[i % 2][:, :, :], io.w_gate[i, :, :, :]).then_inc(s_wg[i % 2], 16)

        def turned_at(j, r, q):
            return ps_pt[0:r, j, 0:q] if j < 4 else ps_g[0:r, 0:q]

        def wait_consumed(eng, n):
            if n in idx_no:
                eng.wait_ge(s_rel, idx_no[n] + 1)
            else:
                eng.wait_ge(s_logit, att_no[n] + 1)

        @block.tensor
        def _(pe):
            def scores(n):
                t, kind, h = units[n]
                q = queries_of(t)
                k0, nk = keys(t)
                if n >= 2:
                    wait_consumed(pe, n - 2)
                if kind == "mla":
                    left, right = m.qt[0:AQK, h, P * t:P * t + q], m.kt[0:AQK, h, k0:k0 + nk]
                elif kind == "dsa":
                    left, right = m.biq[0:HD, h, P * t:P * t + q], m.bik[0:HD, k0:k0 + nk]
                else:
                    left, right = m.biq[HD:P, h, P * t:P * t + q], m.bik[HD:P, k0:k0 + nk]
                for a in range(2):
                    ins = nc.tensor.matmul(ps_sc[0:q, n % 2, a, 0:nk // 2], left,
                                           right[:, nk // 2 * a:nk // 2 * (a + 1)], start=True, stop=True)
                ins.then_inc(s_score, 1)

            def turn(n):
                t, kind, h = units[n]
                q, i = queries_of(t), att_no[n]
                pe.wait_ge(s_prob, i + 1)
                if i:
                    pe.wait_ge(s_ptc, i)
                if t == 3 and h == 0:
                    pe.wait_ge(s_gatec, len(gates))
                for j, (c, r, _) in enumerate(blocks(t)):
                    ins = nc.tensor.transpose(turned_at(j, r, q), prob[i % 3][0:q, c:c + r], ident[0:q, 0:q])
                ins.then_inc(s_pt, 1)

            def values(n):
                t, kind, h = units[n]
                q, i = queries_of(t), att_no[n]
                x = 0 if kind == "mla" else 1
                pe.wait_ge(s_ptc, i + 1)
                if h == 0 and t:
                    pe.wait_ge(s_o, 2 * t - 1 + x)
                if i == 0:
                    pe.wait_ge(s_vm, 32)
                bl = blocks(t)
                for j, (c, r, v) in enumerate(bl):
                    ins = nc.tensor.matmul(ps_o[0:q, x, AV * h:AV * (h + 1)], probT[i % 2][0:r, j, 0:q],
                                           value(kind, h, r, v), start=(j == 0), stop=(j == len(bl) - 1))
                ins.then_inc(s_pv, 1)

            def gate(g):
                i, hf = gates[g]
                if hf == 0:
                    pe.wait_ge(s_wg[i % 2], 16 * (i // 2 + 1))
                if g:
                    pe.wait_ge(s_gatec, g)
                for k in range(DC):
                    ins = nc.tensor.matmul(ps_g[:, 0:HALF], wg[i % 2][:, k, :], m.ht[:, k, HALF * hf:HALF * (hf + 1)],
                                           start=(k == 0), stop=(k == DC - 1))
                ins.then_inc(s_gate, 1)

            for n in range(N + VALUES):
                if n < N:
                    scores(n)
                if n - VALUES in att_no:
                    values(n - VALUES)
                if n - TURN in att_no:
                    turn(n - TURN)
                if n in gate_at:
                    gate(gate_at[n])

        @block.scalar
        def _(act):
            def unit(n):
                t, kind, h = units[n]
                q = queries_of(t)
                if kind == "index":
                    i = idx_no[n]
                    act.wait_ge(s_score, n + 1)
                    if i >= 2:
                        act.wait_ge(s_acc, i - 1)
                    nc.scalar.activation(halves(rel[i % 2], t), ps_sc[0:q, n % 2, :, 0:keys(t)[1] // 2],
                                         ACT.Relu).then_inc(s_rel, 1)
                    return
                i, x = att_no[n], 0 if kind == "mla" else 1
                act.wait_ge(s_max, i + 1)
                if i >= 3:
                    act.wait_ge(s_pt, i - 2)
                if h == 0 and t >= 2:
                    act.wait_ge(s_o, 2 * (t - 2) + 1 + x)
                nk = keys(t)[1]
                nc.scalar.activation(prob[i % 3][0:q, 0:nk], logit[i % 3][0:q, 0:nk], ACT.Exp,
                                     bias=mx[0:q, i % 3, 1:2], scale=A_SCALE if x == 0 else B_SCALE,
                                     accum_out=total[0:q, t % 2, x, h:h + 1]).then_inc(s_prob, 1)

            def turned(n):
                t, kind, h = units[n]
                q, i = queries_of(t), att_no[n]
                act.wait_ge(s_pt, i + 1)
                if i >= 2:
                    act.wait_ge(s_pv, i - 1)
                bl = blocks(t)
                full = sum(r == P for _, r, _ in bl)
                nc.scalar.copy(probT[i % 2][:, 0:full, 0:q], ps_pt[:, 0:full, 0:q])
                r = bl[-1][1]
                nc.scalar.copy(probT[i % 2][0:r, full, 0:q], turned_at(full, r, q)).then_inc(s_ptc, 1)

            for n in range(N + TURN):
                if n < N:
                    unit(n)
                if n - TURN in att_no:
                    turned(n - TURN)
                if n - 1 in gate_at:
                    g = gate_at[n - 1]
                    i, hf = gates[g]
                    act.wait_ge(s_gate, g + 1)
                    nc.scalar.copy(m.sg[:, i // DC, i % DC, HALF * hf:HALF * (hf + 1)],
                                   ps_g[:, 0:HALF]).then_inc(s_gatec, 1)

        @block.vector
        def _(dve):
            step = Chain(dve)
            v = nc.vector

            def index_unit(n):
                t, _, h = units[n]
                q, nk = queries_of(t), keys(t)[1]
                i = idx_no[n]
                dve.wait_ge(s_rel, i + 1)
                w = m.iw[0:q, t, h:h + 1]
                if h == 0:
                    step(v.tensor_scalar(score[0:q, 0:nk], rel[i % 2][0:q, 0:nk], w, None, ALU.mult), s_acc)
                else:
                    step(v.scalar_tensor_tensor(out=score[0:q, 0:nk], in0=rel[i % 2][0:q, 0:nk], scalar=w,
                                                in1=score[0:q, 0:nk], op0=ALU.mult, op1=ALU.add), s_acc)

            def hide_ahead(t):
                if t < 4:
                    nk = keys(t)[1]
                    step(v.memset(score[0:CHUNK, nk - CHUNK:nk], NEG), s_step)

            def choose_some(t, h):
                q, nk = queries_of(t), keys(t)[1]
                sc = score[0:q, 0:nk]
                rounds = (TOPK_P if t < 4 else TOPK_S) // 8
                assert rounds <= 2 * H
                for _ in range(2 * h, min(2 * h + 2, rounds)):
                    step(v.max(best[0:q, :], sc), s_step)
                    step(v.match_replace(sc, best[0:q, :], sc, TAKEN), s_step)

            def hide_unchosen(t):
                q, nk = queries_of(t), keys(t)[1]
                sc = score[0:q, 0:nk]
                step(v.tensor_scalar(biasB[0:q, 0:nk], sc, SEEN, HIDE, ALU.is_gt, ALU.mult), s_step)
                if t < 4:
                    step(v.tensor_tensor(biasB[0:q, 0:nk], biasB[0:q, 0:nk], biasA[0:q, KPROMPT - nk:], ALU.add),
                         s_step)

            def logits(n):
                t, kind, h = units[n]
                q, nk = queries_of(t), keys(t)[1]
                i = att_no[n]
                if kind == "dsa":
                    bias = halves(biasB, t)
                elif t < 4:
                    bias = biasA[0:q, KPROMPT - nk:].rearrange("p (a k) -> p a k", a=2)
                else:
                    bias = halves(biasA, t)
                dve.wait_ge(s_score, n + 1)
                if i >= 3:
                    dve.wait_ge(s_prob, i - 2)
                step(v.tensor_tensor_reduce(out=halves(logit[i % 3], t), in0=ps_sc[0:q, n % 2, :, 0:nk // 2],
                                            in1=bias, scale=1.0, scalar=NEG, op0=ALU.add, op1=ALU.max,
                                            accum_out=mx[0:q, i % 3, 0:1]), s_logit)
                v.tensor_scalar(mx[0:q, i % 3, 1:2], mx[0:q, i % 3, 0:1],
                                -(A_SCALE if kind == "mla" else B_SCALE), None, ALU.mult).then_inc(s_max, 1)

            def normalise(n):
                t, kind, _ = units[n]
                q, x = queries_of(t), 0 if kind == "mla" else 1
                dve.wait_ge(s_pv, att_no[n] + 1)
                step(v.reciprocal(inv[0:q, :], total[0:q, t % 2, x, :]), s_step)
                step(v.tensor_tensor(m.oab[0:q, t, x, :].rearrange("p (h c) -> p h c", h=H),
                                     ps_o[0:q, x, :].rearrange("p (h c) -> p h c", h=H),
                                     last(inv[0:q, :], AV), ALU.mult), s_o)

            step(v.memset(biasA[:, :], 0.0), s_step)
            step(v.memset(biasA[0:CHUNK, KPROMPT - CHUNK:], HIDE), s_step)
            for n in range(N + LAG):
                if n < N:
                    t, kind, h = units[n]
                    if kind == "index":
                        index_unit(n)
                        if h == H - 1:
                            hide_ahead(t)
                    else:
                        logits(n)
                        if kind == "mla":
                            choose_some(t, h)
                            if h == H - 1:
                                hide_unchosen(t)
                k = n - LAG
                if k >= 0 and units[k][1] != "index" and units[k][2] == H - 1:
                    normalise(k)


def merge(nc, io, m, sem):
    lo = Plan(nc, m.keep)
    m.x = lo("x", [P, NT, D])
    m.after_x = lo.at
    m.h2t = lo("h2t", [P, DC, NQ])
    mt = lo("mt", [P, DC, NQ])
    pl = Plan(nc, m.after_attend)
    ot = pl("ot", [P, 2, 4, NQ])
    w_out = pl("w_out", [P, 2, DC, 512])
    assert pl.at <= m.end, pl.at
    wo = Plan(nc, m.low)("wo", [P, 2, 4, 512])
    sg = lo("sgm", [P, 2, 2, HALF])
    part = lo("part", [P, 2, HALF])
    xs = lo("xs2", [P, 2, D])
    st = lo("st2", [P, 4])
    ln2 = lo("ln2", [P, DC])
    assert lo.at <= m.temps
    ident = m.ident

    with nc.psum_tensor("ps_m", [P, 8, 512], F32) as ps, nc.Block() as block:
        s_x = sem("c_x")
        s_wo = [sem("c_wo0"), sem("c_wo1")]
        s_wout = [sem("c_wout0"), sem("c_wout1")]
        s_ln = sem("c_ln")
        s_ot = sem("c_ot")
        s_otc = sem("c_otc")
        s_z = sem("c_z")
        s_sig = sem("c_sig")
        s_mt = sem("c_mt")
        s_y = sem("c_y")
        s_step = sem("c_step")
        s_res = sem("c_res")
        s_ms = sem("c_ms")
        s_rt = sem("c_rt")
        s_xs = sem("c_xs")
        s_hT = sem("c_hT")
        s_h2 = sem("c_h2")

        @block.sync
        def _(sp):
            for x in range(2):
                sp.dma_start(wo[:, x, :, :], io.w_o[0, x, :, :, :]).then_inc(s_wo[0], 16)
            sp.dma_start(m.x[:, 0:4, :], io.x_prompt[:, :].rearrange("(t p) d -> p t d", p=P)).then_inc(s_x, 16)
            sp.dma_start(m.x[0:DEC, 4, :], io.x_sample[:, :]).then_inc(s_x, 16)
            sp.dma_start(ln2[:, :], io.ln2[:, :]).then_inc(s_ln, 16)
            for c in range(2):
                sp.dma_start(w_out[:, c, :, :], io.w_out[c, :, :, :]).then_inc(s_wout[c], 16)
            sp.wait_ge(s_z, 2 * 4)
            for x in range(2):
                sp.dma_start(wo[:, x, :, :], io.w_o[1, x, :, :, :]).then_inc(s_wo[1], 16)

        @block.tensor
        def _(pe):
            for t in range(NT):
                q = queries_of(t)
                for x in range(2):
                    n = 2 * t + x
                    if n >= 8:
                        pe.wait_ge(s_otc, n - 7)
                    for c in range(4):
                        ins = nc.tensor.transpose(ps[:, n % 8, P * c:P * c + q], m.oab[0:q, t, x, P * c:P * (c + 1)],
                                                  ident[0:q, 0:q])
                    ins.then_inc(s_ot, 1)
            pe.wait_ge(s_otc, 2 * NT)
            for n in range(2 * DC):
                j, hf = n // 2, n % 2
                b = 2 * (n % 4)
                if n % 8 == 0:
                    pe.wait_ge(s_wo[n // 8], 32)
                if n >= 4:
                    pe.wait_ge(s_mt, n - 3)
                for x in range(2):
                    for k in range(4):
                        ins = nc.tensor.matmul(ps[:, b + x, 0:HALF], wo[:, x, k, P * (j % 4):P * (j % 4 + 1)],
                                               ot[:, x, k, HALF * hf:HALF * (hf + 1)], start=(k == 0), stop=(k == 3))
                ins.then_inc(s_z, 1)
            pe.wait_ge(s_mt, 2 * DC)

            def out(t):
                q = queries_of(t)
                for c in range(2):
                    if t == 0:
                        pe.wait_ge(s_wout[c], 16)
                    n = 2 * t + c
                    if n >= 4:
                        pe.wait_ge(s_res, n - 3)
                    for k in range(DC):
                        ins = nc.tensor.matmul(ps[0:q, n % 4, :], mt[:, k, P * t:P * t + q], w_out[:, c, k, :],
                                               start=(k == 0), stop=(k == DC - 1))
                    ins.then_inc(s_y, 1)

            def turn(t):
                q = queries_of(t)
                pe.wait_ge(s_xs, t + 1)
                for c in range(DC):
                    n = 2 * t + c // 4
                    if c % 4 == 0 and n >= 4:
                        pe.wait_ge(s_h2, n - 3)
                    ins = nc.tensor.transpose(ps[:, 4 + n % 4, P * (c % 4):P * (c % 4) + q],
                                              xs[0:q, t % 2, P * c:P * (c + 1)], ident[0:q, 0:q])
                    if c % 4 == 3:
                        ins.then_inc(s_hT, 1)

            out(0)
            for t in range(NT):
                if t + 1 < NT:
                    out(t + 1)
                turn(t)

        @block.scalar
        def _(act):
            for n in range(2 * NT):
                t, x = n // 2, n % 2
                q = queries_of(t)
                act.wait_ge(s_ot, n + 1)
                nc.scalar.copy(ot[:, x, :, P * t:P * t + q],
                               ps[:, n % 8, :].rearrange("p (c k) -> p c k", c=4)[:, :, 0:q]).then_inc(s_otc, 1)
            for n in range(2 * DC):
                if n >= 2:
                    act.wait_ge(s_mt, n - 1)
                nc.scalar.activation(sg[:, n % 2, :, :], m.sg[:, :, n // 2, HALF * (n % 2):HALF * (n % 2 + 1)],
                                     ACT.Sigmoid).then_inc(s_sig, 1)
            for t in range(NT):
                act.wait_ge(s_ms, t + 1)
                nc.scalar.activation(st[:, 2:3], st[:, 1:2], ACT.Sqrt).then_inc(s_rt, 1)

        @block.vector
        def _(dve):
            step = Chain(dve)
            v = nc.vector
            step(v.memset(st[:, :], 1.0), s_step)
            for n in range(2 * DC):
                j, hf = n // 2, n % 2
                dve.wait_ge(s_sig, n + 1)
                dve.wait_ge(s_z, n + 1)
                step(v.tensor_tensor(part[:, :, :], sg[:, n % 2, :, :], ps[:, 2 * (n % 4):2 * (n % 4) + 2, 0:HALF],
                                     ALU.mult), s_step)
                step(v.tensor_tensor(mt[:, j, HALF * hf:HALF * (hf + 1)], part[:, 0, :], part[:, 1, :], ALU.add),
                     s_mt)
            dve.wait_ge(s_x, 32)
            dve.wait_ge(s_ln, 16)
            def residual(t):
                q = queries_of(t)
                for c in range(2):
                    n = 2 * t + c
                    dve.wait_ge(s_y, n + 1)
                    step(v.tensor_tensor(m.x[0:q, t, 512 * c:512 * (c + 1)], ps[0:q, n % 4, :],
                                         m.x[0:q, t, 512 * c:512 * (c + 1)], ALU.add), s_res)

            def norm(t):
                q = queries_of(t)
                if t >= 2:
                    dve.wait_ge(s_hT, 2 * (t - 1))
                step(v.tensor_tensor_reduce(out=xs[0:q, t % 2, :], in0=m.x[0:q, t, :], in1=m.x[0:q, t, :], scale=1.0,
                                            scalar=0.0, op0=ALU.mult, op1=ALU.add, accum_out=st[0:q, 0:1]), s_step)
                v.tensor_scalar(st[:, 1:2], st[:, 0:1], 1.0 / D, EPS, ALU.mult, ALU.add).then_inc(s_ms, 1)
                dve.wait_ge(s_rt, t + 1)
                step(v.reciprocal(st[:, 3:4], st[:, 2:3]), s_step)
                step(v.tensor_scalar(xs[0:q, t % 2, :], m.x[0:q, t, :], st[0:q, 3:4], None, ALU.mult), s_xs)

            def gain(t):
                q = queries_of(t)
                for j in range(2):
                    n = 2 * t + j
                    dve.wait_ge(s_hT, n + 1)
                    v.tensor_tensor(m.h2t[:, 4 * j:4 * j + 4, P * t:P * t + q],
                                    ps[:, 4 + n % 4, :].rearrange("p (c k) -> p c k", c=4)[:, :, 0:q],
                                    last(ln2[:, 4 * j:4 * j + 4], q), ALU.mult).then_inc(s_h2, 1)

            for t in range(NT):
                residual(t)
                norm(t)
                if t:
                    gain(t - 1)
            gain(NT - 1)


def queries(nc, io, m, sem):
    m.qh = Plan(nc, m.low)("qh", [P, PH, NQ])
    lo = Plan(nc, m.after_x)
    lo.at += DC * NQ * 4
    m.hs = lo("hs", [P, 2, DC, NQ], F32R)
    m.after_hs = lo.at
    wq = [lo(f"wq{i}", [P, DC, P]) for i in range(3)]
    assert lo.at <= m.end, lo.at

    with nc.psum_tensor("ps_q", [P, 2, 2, 512], F32) as ps, nc.Block() as block:
        s_wq = [sem(f"q_wq{i}") for i in range(3)]
        s_q = sem("q_q")
        s_qc = sem("q_qc")
        s_high = sem("q_high")
        s_low = sem("q_low")

        @block.sync
        def _(sp):
            for h in range(PH):
                if h >= 3:
                    sp.wait_ge(s_q, h - 2)
                sp.dma_start(wq[h % 3][:, :, :], io.peer_wq[h, :, :, :]).then_inc(s_wq[h % 3], 16)

        @block.tensor
        def _(pe):
            for h in range(PH):
                pe.wait_ge(s_wq[h % 3], 16 * (h // 3 + 1))
                if h >= 2:
                    pe.wait_ge(s_qc, h - 1)
                for hf in range(2):
                    for k in range(DC):
                        ins = nc.tensor.matmul(ps[:, h % 2, hf, 0:HALF], wq[h % 3][:, k, :],
                                               m.h2t[:, k, HALF * hf:HALF * (hf + 1)],
                                               start=(k == 0), stop=(k == DC - 1))
                ins.then_inc(s_q, 1)

        @block.scalar
        def _(act):
            for h in range(PH):
                act.wait_ge(s_q, h + 1)
                nc.scalar.copy(m.qh[:, h, :].rearrange("p (a k) -> p a k", a=2),
                               ps[:, h % 2, :, 0:HALF]).then_inc(s_qc, 1)

        @block.vector
        def _(dve):
            v = nc.vector
            v.tensor_copy(m.hs[:, 0, :, :], m.h2t[:, :, :]).then_inc(s_high, 1)
            dve.wait_ge(s_high, 1)
            v.tensor_tensor(m.hs[:, 1, :, :], m.h2t[:, :, :], m.hs[:, 0, :, :].bitcast(F32),
                            ALU.subtract).then_inc(s_low, 1)


TB = 32
NB = NQ // TB
GT = 4
GPB = TB // GT
RING = 2
EG = 4
STEPS = NKEY // EG
HB = (NB // 2 + 1, NB // 2)
HT = (HB[0] * TB, HB[1] * TB)
HOFF = (0, HT[0])
BU = 2 * DC
BPT = P // TB
LEAD = 2
SPT = LEAD + BPT
assert NB * TB == NQ and GPB == 2 * EG and BPT % 2 == 0
THREE = ((0, 0), (0, 1), (1, 0))


def retrieve(nc, io, m, sem):
    mid_plan = Plan(nc, m.after_x)
    sc = [mid_plan(f"sc{i}", [P, PH, 2, NKEY]) for i in range(2)]
    work = mid_plan("work", [P, NKEY * 2])
    assert mid_plan.at <= m.after_x + DC * NQ * 4
    pl = Plan(nc, m.after_hs)
    slots = pl("slots", [P, 3, NQ])
    keyb = pl("keyb", [P, PH, 2, NKEY])
    val = pl("val", [P, PH, 2, TOPE])
    ind = pl("ind", [P, PH, 2, TOPE], U32)
    cand = pl("cand", [P, PH, TOPE * TOPE])
    hot = cand[:, :, :].rearrange("p h (i j) -> p (h i) j", i=TOPE)
    top = pl("top", [P, PH, TOPE])
    pos = pl("pos", [P, PH, TOPE], U32)
    posb = pl("posb", [P, 2, SLOTS], U32)
    posf = pl("posf", [P, 2, SLOTS])
    indf = pl("indf", [P, PH, 2, TOPE])
    num = pl("num", [P, TOPE])
    pick = [pl(f"pick{i}", [P, 3, SLOTS]) for i in range(2)]
    ssum = pl("ssum", [P, 2, PH])
    left = pl("left", [P, RING, GT, NKEY])
    right = pl("right", [P, RING, GT, NKEY])
    stage = [pl(f"stage{i}", [P, NKEY, TB]) for i in range(2)]
    number = pl("number", [P, NKEY])
    raw = pl("raw", [P, EG, DC, P])
    us = pl("us", [P, 2, 2, DC, P], F32R)
    gel = pl("gel", [P, EG, NQ])
    assert pl.at <= m.end, pl.at
    ident = m.ident
    first_key, second_key, gate = (slots[:, i, :] for i in range(3))

    with nc.psum_tensor("ps_r", [P, 8, 512], F32) as ps, nc.Block() as block:
        ps_u, ps_s, ps_k, ps_t = ps[:, 0:2, :], ps[:, 2:4, :], ps[:, 4:6, :], ps[:, 6:8, :]
        s_key = sem("d_key")
        s_zero = sem("d_zero")
        s_num = sem("d_num")
        s_s = sem("d_s")
        s_sc = sem("d_sc")
        s_used = sem("d_used")
        s_step = sem("d_step")
        s_shift = sem("d_shift")
        s_exp = sem("d_exp")
        s_pick = sem("d_pick")
        s_turn = sem("d_turn")
        s_slot = sem("d_slot")
        s_left = sem("d_left")
        s_right = sem("d_right")
        s_prod = sem("d_prod")
        s_out = sem("d_out")
        s_store = [sem("d_store0"), sem("d_store1")]
        s_raw = [sem(f"d_raw{e}") for e in range(EG)]
        s_high = sem("d_high")
        s_split = sem("d_split")
        s_u = sem("d_u")
        s_gelu = sem("d_gelu")
        s_kept = [sem(f"d_kept{e}") for e in range(EG)]

        def schedule(eng, step, before_slots, after_blocks):
            step(0, None, 0)
            step(1, None, 0)
            for t in range(4):
                before_slots(t)
                s0, b0 = SPT * t + LEAD, BPT * t
                if t == 0:
                    for j in range(BPT):
                        step(s0 + j, b0 + j, j % 2)
                else:
                    with eng.Fori(0, BPT // 2) as i:
                        step(i * 2 + s0, i * 2 + b0, 0)
                        step(i * 2 + (s0 + 1), i * 2 + (b0 + 1), 1)
                after_blocks(t)
                with eng.Fori(s0 + BPT, s0 + BPT + LEAD) as s:
                    step(s, None, 0)
            before_slots(4)
            step(4 * SPT + LEAD, NB - 1, 0)
            with eng.Fori(4 * SPT + LEAD + 1, STEPS - 1) as s:
                step(s, None, 0)
            step(STEPS - 1, None, 0)

        @block.sync
        def _(sp):
            def load(s, e, dst_only=False):
                src = io.peer_u[s * EG + e] if isinstance(s, int) else io.peer_u[bass.ds(s * EG + e, 1)].squeeze(0)
                sp.dma_start(raw[:, e, :, :], src).then_inc(s_raw[e], 16)

            def store(s, e):
                sp.wait_ge(s_gelu, s * (2 * EG) + 2 * (e + 1))
                dst = io.gelu[s * EG + e] if isinstance(s, int) else io.gelu[bass.ds(s * EG + e, 1)].squeeze(0)
                sp.dma_start(dst, gel[:, e, :]).then_inc(s_kept[e], 16)

            for e in range(EG):
                load(0, e)
            with sp.Fori(0, STEPS - 1) as s:
                for e in range(EG):
                    sp.wait_ge(s_split, s * EG + (e + 1))
                    load(s + 1, e)
                    store(s, e)
            for e in range(EG):
                store(STEPS - 1, e)
            for e in range(EG):
                sp.wait_ge(s_kept[e], 16 * STEPS)
            sp.wait_ge(s_store[0], 16 * (NB // 2 + 1))
            sp.wait_ge(s_store[1], 16 * (NB // 2))

        @block.gpsimd
        def _(pool):
            g = nc.gpsimd
            g.memset(keyb[:, :, :, :], 0.0).then_inc(s_zero, 1)
            g.iota(num[:, :], [[1, TOPE]], base=0, channel_multiplier=0,
                   allow_small_or_imprecise_dtypes=True).then_inc(s_num, 1)
            g.iota(number[:, :], [[1, NKEY]], base=0, channel_multiplier=0,
                   allow_small_or_imprecise_dtypes=True).then_inc(s_num, 1)
            pool.wait_ge(s_zero, 1)
            for a in range(2):
                pool.dma_start(keyb[HD * a:HD * (a + 1), :, a, :], io.subkeys[a, :, :, :]).then_inc(s_key, 16)

            with pool.Fori(0, STEPS) as s:
                for e in range(EG):
                    pool.wait_ge(s_high, s * EG + (e + 1))
                    g.tensor_tensor(us[:, e % 2, 1, :, :], raw[:, e, :, :], us[:, e % 2, 0, :, :].bitcast(F32),
                                    ALU.subtract).then_inc(s_split, 1)

        @block.tensor
        def _(pe):
            def scores(t):
                q = queries_of(t)
                for g in range(4):
                    n = 4 * t + g
                    if n >= 2:
                        pe.wait_ge(s_sc, n - 1)
                    for i in range(2):
                        ins = nc.tensor.matmul(ps_k[0:q, g % 2, 2 * NKEY * i:2 * NKEY * (i + 1)],
                                               m.qh[:, 2 * g + i, P * t:P * t + q],
                                               keyb[:, 2 * g + i, :, :].rearrange("p a k -> p (a k)"),
                                               start=True, stop=True)
                    ins.then_inc(s_s, 1)

            def turn(t):
                q = queries_of(t)
                pe.wait_ge(s_pick, t + 1)
                if t >= 2:
                    pe.wait_ge(s_slot, t - 1)
                for i in range(3):
                    ins = nc.tensor.transpose(ps_t[:, t % 2, P * i:P * i + q], pick[t % 2][0:q, i, :],
                                              ident[0:q, 0:q])
                ins.then_inc(s_turn, 1)

            def group(b, k):
                pe.wait_ge(s_left, b * GPB + (k + 1))
                pe.wait_ge(s_right, b * GPB + (k + 1))
                if not isinstance(b, int) or GPB * b + k >= 2:
                    pe.wait_ge(s_out, b * GPB + (k - 1))
                for j in range(GT):
                    ins = nc.tensor.matmul(ps_s[:, k % 2, NKEY * j:NKEY * (j + 1)], left[:, k % RING, j, :],
                                           right[:, k % RING, j, :], start=True, stop=True)
                ins.then_inc(s_prod, 1)

            def step(s, b, par):
                for e in range(EG):
                    pe.wait_ge(s_split, s * EG + (e + 1))
                    for hf in range(2):
                        if not isinstance(s, int) or EG * s + e:
                            pe.wait_ge(s_gelu, s * (2 * EG) + (2 * e + hf - 1))
                        for k in range(DC):
                            for i, (x, y) in enumerate(THREE):
                                ins = nc.tensor.matmul(ps_u[:, hf, 0:HT[hf]], us[:, e % 2, x, k, :],
                                                       m.hs[:, y, k, HOFF[hf]:HOFF[hf] + HT[hf]],
                                                       start=(k == 0 and i == 0), stop=(k == DC - 1 and i == 2))
                        ins.then_inc(s_u, 1)
                        if b is not None:
                            group(b, 2 * e + hf)

            pe.wait_ge(s_key, 32)
            scores(0)
            scores(1)
            schedule(pe, step, turn, lambda t: scores(t + 2) if t + 2 < NT else None)

        @block.scalar
        def _(act):
            def copy_scores(t):
                q = queries_of(t)
                if t >= 2:
                    act.wait_ge(s_used, t - 1)
                for g in range(4):
                    act.wait_ge(s_s, 4 * t + g + 1)
                    nc.scalar.copy(sc[t % 2][0:q, 2 * g:2 * g + 2, :, :].rearrange("p h a k -> p (h a k)"),
                                   ps_k[0:q, g % 2, :]).then_inc(s_sc, 1)

            def slot(t):
                q = queries_of(t)
                act.wait_ge(s_shift, t + 1)
                nc.scalar.activation(top[0:q, :, :], top[0:q, :, :], ACT.Exp).then_inc(s_exp, 1)
                act.wait_ge(s_turn, t + 1)
                nc.scalar.copy(slots[:, :, P * t:P * t + q],
                               ps_t[:, t % 2, 0:3 * P].rearrange("p (i k) -> p i k", i=3)[:, :, 0:q]
                               ).then_inc(s_slot, 1)

            def high(s, e):
                act.wait_ge(s_raw[e], s * 16 + 16)
                if not isinstance(s, int) or EG * s + e >= 2:
                    act.wait_ge(s_u, s * (2 * EG) + 2 * (e - 1))
                nc.scalar.copy(us[:, e % 2, 0, :, :], raw[:, e, :, :]).then_inc(s_high, 1)

            def step(s, b, par):
                for e in range(EG):
                    if e < EG - 1:
                        high(s, e + 1)
                    elif not isinstance(s, int) or s < STEPS - 1:
                        high(s + 1, 0)
                    if not isinstance(s, int) or s:
                        act.wait_ge(s_kept[e], s * 16)
                    if b is not None and e == 0 and (not isinstance(b, int) or b >= 2):
                        act.wait_ge(s_store[par], (b - par) * 8)
                    for hf in range(2):
                        act.wait_ge(s_u, s * (2 * EG) + (2 * e + hf + 1))
                        nc.scalar.activation(gel[:, e, HOFF[hf]:HOFF[hf] + HT[hf]], ps_u[:, hf, 0:HT[hf]],
                                             ACT.Gelu_apprx_tanh).then_inc(s_gelu, 1)
                        if b is not None:
                            k = 2 * e + hf
                            act.wait_ge(s_prod, b * GPB + (k + 1))
                            nc.scalar.copy(stage[par][:, :, GT * k:GT * (k + 1)],
                                           ps_s[:, k % 2, :].rearrange("p (t i) -> p i t", t=GT)
                                           ).then_inc(s_out, 1)
                if b is not None:
                    act.wait_ge(s_out, b * GPB + GPB)
                    dst = io.dense[b] if isinstance(b, int) else io.dense[bass.ds(b, 1)].squeeze(0)
                    act.dma_start(dst, stage[par][:, :, :]).then_inc(s_store[par], 16)

            high(0, 0)
            copy_scores(0)
            copy_scores(1)
            schedule(act, step, slot, lambda t: copy_scores(t + 2) if t + 2 < NT else None)

        @block.vector
        def _(dve):
            step = Chain(dve)
            v = nc.vector

            def top16(values, where, src, scratch):
                step(v.max(values[:, 0:8], src), s_step)
                v.max_index(where[:, 0:8], values[:, 0:8], src)
                step(v.match_replace(scratch, values[:, 0:8], src, TAKEN), s_step)
                step(v.max(values[:, 8:16], scratch), s_step)
                return v.max_index(where[:, 8:16], values[:, 8:16], scratch)

            def choose(t):
                q = queries_of(t)
                dve.wait_ge(s_sc, 4 * t + 4)
                for h in range(PH):
                    for a in range(2):
                        ins = top16(val[0:q, h, a, :], ind[0:q, h, a, :], sc[t % 2][0:q, h, a, :],
                                    work[0:q, NKEY * a:NKEY * (a + 1)])
                step(ins, s_used)
                c4 = cand[0:q].rearrange("p h (i j) -> p h i j", i=TOPE)
                step(v.tensor_tensor(c4, val[0:q, :, 0, :].unsqueeze(3).to_broadcast([q, PH, TOPE, TOPE]),
                                     val[0:q, :, 1, :].unsqueeze(2).to_broadcast([q, PH, TOPE, TOPE]), ALU.add),
                     s_step)
                for h in range(PH):
                    ins = top16(top[0:q, h, :], pos[0:q, h, :], cand[0:q, h, :], work[0:q, :])
                step(ins, s_step)
                v.tensor_copy(ssum[0:q, 0, :], top[0:q, :, 0])
                step(v.tensor_scalar(posb[0:q, 0, :], pos[0:q].rearrange("p h k -> p (h k)"), 4, None,
                                     ALU.logical_shift_right), s_step)
                v.tensor_tensor(top[0:q], top[0:q], last(ssum[0:q, 0, :], TOPE), ALU.subtract).then_inc(s_shift, 1)
                step(v.tensor_scalar(posb[0:q, 1, :], pos[0:q].rearrange("p h k -> p (h k)"), TOPE - 1, None,
                                     ALU.bitwise_and), s_step)
                v.tensor_copy(posf[0:q], posb[0:q])
                step(v.tensor_copy(indf[0:q], ind[0:q]), s_step)
                if t >= 2:
                    dve.wait_ge(s_turn, t - 1)
                out = pick[t % 2]
                hot4 = hot[0:q].rearrange("p (h i) j -> p h i j", h=PH)
                for a in range(2):
                    step(v.tensor_tensor(hot[0:q], last(posf[0:q, a, :], TOPE), mid(num[0:q, :], SLOTS),
                                         ALU.is_equal), s_step)
                    step(v.tensor_tensor(hot4, hot4, indf[0:q, :, a, :].unsqueeze(2).to_broadcast([q, PH, TOPE, TOPE]),
                                         ALU.mult), s_step)
                    step(v.tensor_reduce(out[0:q, a, :], hot[0:q], AX_X, ALU.add), s_step)
                dve.wait_ge(s_exp, t + 1)
                step(v.tensor_reduce(ssum[0:q, 0, :], top[0:q], AX_X, ALU.add), s_step)
                step(v.reciprocal(ssum[0:q, 1, :], ssum[0:q, 0, :]), s_step)
                step(v.tensor_tensor(out[0:q, 2, :].rearrange("p (h k) -> p h k", h=PH), top[0:q],
                                     last(ssum[0:q, 1, :], TOPE), ALU.mult), s_pick)

            def one_hots(b):
                for k in range(GPB):
                    if not isinstance(b, int) or GPB * b + k >= RING:
                        dve.wait_ge(s_prod, b * GPB + (k - RING + 1))
                    for j in range(GT):
                        tok = bass.ds(b * TB + (GT * k + j), 1)
                        ins = v.tensor_scalar(left[:, k % RING, j, :], number[:, :], first_key[:, tok],
                                              gate[:, tok], ALU.is_equal, ALU.mult)
                    ins.then_inc(s_left, 1)
                    for j in range(GT):
                        tok = bass.ds(b * TB + (GT * k + j), 1)
                        ins = v.tensor_scalar(right[:, k % RING, j, :], number[:, :], second_key[:, tok], None,
                                              ALU.is_equal)
                    ins.then_inc(s_right, 1)

            dve.wait_ge(s_num, 2)
            for t in range(NT):
                choose(t)
                dve.wait_ge(s_slot, t + 1)
                if t == 0:
                    one_hots(0)
                with dve.Fori(max(BPT * t, 1), min(BPT * (t + 1), NB)) as b:
                    one_hots(b)


def experts(nc, io, m, sem):
    m.acc = Plan(nc, m.low)("acc", [P, DC, NQ])
    pl = Plan(nc, m.after_x)
    raw = pl("rawv", [P, EG, D])
    vs = pl("vs", [P, 2, EG, 2, D], F32R)
    gt = pl("gt", [P, 2, NB, EG, TB])
    gel = pl("gelv", [P, 2, EG, NQ])
    wf = pl("wf", [P, 2, NQ])
    ws = pl("ws", [P, 2, EG, 2, NQ], F32R)
    assert pl.at <= m.end, pl.at

    with nc.psum_tensor("ps_b", [P, 8, 512], F32) as ps, nc.Block() as block:
        s_raw = [sem(f"f_raw{e}") for e in range(EG)]
        s_in = [sem("f_in0"), sem("f_in1")]
        s_high = sem("f_high")
        s_split = sem("f_split")
        s_full = sem("f_full")
        s_whigh = sem("f_whigh")
        s_w = sem("f_w")
        s_b = sem("f_b")
        s_add = sem("f_add")

        def pairs(eng, body):
            body(0, 0)
            body(1, 1)
            with eng.Fori(0, STEPS // 2 - 1) as i:
                body(i * 2 + 2, 0)
                body(i * 2 + 3, 1)

        @block.sync
        def _(sp):
            def load(s, par):
                for e in range(EG):
                    if not isinstance(s, int) or s:
                        sp.wait_ge(s_split, s * EG + (e + 1 - EG))
                    src = io.peer_v[:, s * EG + e, :] if isinstance(s, int) else \
                        io.peer_v[:, bass.ds(s * EG + e, 1), :].squeeze(1)
                    sp.dma_start(raw[:, e, :], src).then_inc(s_raw[e], 16)
                if not isinstance(s, int):
                    sp.wait_ge(s_w, s * EG - EG)
                sp.dma_start(gt[:, par, :, :, :].rearrange("p b e t -> p b (e t)"),
                             io.dense[:, :, bass.ds(s * EG, EG), :].rearrange("b p e t -> p b (e t)")
                             ).then_inc(s_in[par], 16)
                sp.dma_start(gel[:, par, :, :], io.gelu[bass.ds(s * EG, EG), :, :].rearrange("e p n -> p e n")
                             ).then_inc(s_in[par], 16)

            pairs(sp, load)

        @block.gpsimd
        def _(pool):
            def split(s, par):
                for e in range(EG):
                    pool.wait_ge(s_high, s * EG + (e + 1))
                    nc.gpsimd.tensor_tensor(vs[:, par, e, 1, :], raw[:, e, :], vs[:, par, e, 0, :].bitcast(F32),
                                            ALU.subtract).then_inc(s_split, 1)

            pairs(pool, split)

        @block.scalar
        def _(act):
            def high(s, par):
                if not isinstance(s, int):
                    act.wait_ge(s_b, s * BU - BU)
                for e in range(EG):
                    act.wait_ge(s_raw[e], s * 16 + 16)
                    nc.scalar.copy(vs[:, par, e, 0, :], raw[:, e, :]).then_inc(s_high, 1)

            pairs(act, high)

        @block.tensor
        def _(pe):
            def products(s, par):
                pe.wait_ge(s_split, s * EG + EG)
                pe.wait_ge(s_w, s * EG + EG)
                for n in range(BU):
                    c, hf = n // 2, n % 2
                    cols = slice(HOFF[hf], HOFF[hf] + HT[hf])
                    pe.wait_ge(s_add, s * BU + (n - 7 + 1) if not isinstance(s, int) or BU * s + n >= 8 else 1)
                    for e in range(EG):
                        for i, (x, y) in enumerate(THREE):
                            ins = nc.tensor.matmul(ps[:, n % 8, 0:HT[hf]], vs[:, par, e, x, P * c:P * (c + 1)],
                                                   ws[:, par, e, y, cols], start=(e == 0 and i == 0),
                                                   stop=(e == EG - 1 and i == 2))
                    ins.then_inc(s_b, 1)

            pairs(pe, products)

        @block.vector
        def _(dve):
            v = nc.vector
            v.memset(m.acc[:, :, :], 0.0).then_inc(s_add, 1)
            dve.wait_ge(s_add, 1)

            def weights(s, par):
                dve.wait_ge(s_in[par], (s - par) * 16 + 32)
                if not isinstance(s, int) or s >= 2:
                    dve.wait_ge(s_b, s * BU - BU)
                for e in range(EG):
                    v.tensor_tensor(wf[:, e % 2, :].rearrange("p (b t) -> p b t", t=TB),
                                    gel[:, par, e, :].rearrange("p (b t) -> p b t", t=TB),
                                    gt[:, par, :, e, :], ALU.mult).then_inc(s_full, 1)
                    dve.wait_ge(s_full, s * EG + (e + 1))
                    v.tensor_copy(ws[:, par, e, 0, :], wf[:, e % 2, :]).then_inc(s_whigh, 1)
                    dve.wait_ge(s_whigh, s * EG + (e + 1))
                    v.tensor_tensor(ws[:, par, e, 1, :], wf[:, e % 2, :], ws[:, par, e, 0, :].bitcast(F32),
                                    ALU.subtract).then_inc(s_w, 1)

            def add(s):
                for n in range(BU):
                    c, hf = n // 2, n % 2
                    cols = slice(HOFF[hf], HOFF[hf] + HT[hf])
                    dve.wait_ge(s_b, s * BU + (n + 1))
                    v.tensor_tensor(m.acc[:, c, cols], ps[:, n % 8, 0:HT[hf]], m.acc[:, c, cols],
                                    ALU.add).then_inc(s_add, 1)

            weights(0, 0)
            weights(1, 1)
            add(0)
            with dve.Fori(0, STEPS // 2 - 1) as i:
                weights(i * 2 + 2, 0)
                add(i * 2 + 1)
                weights(i * 2 + 3, 1)
                add(i * 2 + 2)
            add(STEPS - 1)


def finish(nc, io, m, sem):
    with nc.psum_tensor("ps_f", [P, 8, 512], F32) as ps, nc.Block() as block:
        s_t = sem("g_t")
        s_y = sem("g_y")
        s_out = sem("g_out")

        @block.tensor
        def _(pe):
            for n in range(2 * NT):
                t, j = n // 2, n % 2
                q = queries_of(t)
                if n >= 8:
                    pe.wait_ge(s_y, n - 7)
                for c in range(4):
                    ins = nc.tensor.transpose(ps[0:q, n % 8, P * c:P * (c + 1)],
                                              m.acc[:, 4 * j + c, P * t:P * t + q], m.ident[:, :])
                ins.then_inc(s_t, 1)

        @block.vector
        def _(dve):
            for n in range(2 * NT):
                t, j = n // 2, n % 2
                q = queries_of(t)
                dve.wait_ge(s_t, n + 1)
                nc.vector.tensor_tensor(m.x[0:q, t, 512 * j:512 * (j + 1)], ps[0:q, n % 8, :],
                                        m.x[0:q, t, 512 * j:512 * (j + 1)], ALU.add).then_inc(s_y, 1)

        @block.sync
        def _(sp):
            for t in range(NT):
                sp.wait_ge(s_y, 2 * t + 2)
                dst = io.y_prompt[P * t:P * (t + 1), :] if t < 4 else io.y_sample[:, :]
                sp.dma_start(dst, m.x[0:queries_of(t), t, :]).then_inc(s_out, 16)
            sp.wait_ge(s_out, 16 * NT)


class Names:
    pass


def hybrid_step(nc, io):
    m = Names()
    m.end = 229344
    pl = Plan(nc, BASE)
    m.ident = pl("ident", [P, P])
    m.low = pl.at
    m.ht = pl("ht", [P, DC, TOK])
    m.keep = pl.at
    m.kt = pl("kt", [P, H, KEYS])
    m.qt = pl("qt", [P, H, NQ])
    m.biq = pl("biq", [P, H, NQ])
    m.bik = pl("bik", [P, KEYS])
    m.va = pl("va", [P, 7, H, AV])
    m.vb = pl("vb", [P, 7, HD])
    m.iw = pl("iw", [P, NT, H])
    m.temps = pl.at
    sem = nc.alloc_semaphore
    project(nc, io, m, sem)
    attend(nc, io, m, sem)
    merge(nc, io, m, sem)
    queries(nc, io, m, sem)
    retrieve(nc, io, m, sem)
    experts(nc, io, m, sem)
    finish(nc, io, m, sem)


def rotary_tables():
    pos = np.concatenate([META + np.arange(SEQ), PAST + np.arange(DEC), np.arange(META)]).astype(np.float32)
    parts = []
    for rot in (ROPE, BROT):
        half = rot // 2
        inv = np.float32(THETA) ** (-np.arange(half, dtype=np.float32) * np.float32(2.0 / rot))
        ang = pos[:, None] * inv.astype(np.float32)[None, :]
        c, s = np.cos(ang), np.sin(ang)
        parts += [c, c, -s, s]
    flat = np.zeros((NT * P, TABS), np.float32)
    flat[:TOK] = np.concatenate(parts, axis=1)
    return flat.reshape(NT, P, TABS).transpose(1, 0, 2)


def lay_out(x):
    a = {k: np.asarray(v) for k, v in x.items()}
    rows = lambda w: w.reshape(-1, P, w.shape[-1]).transpose(1, 0, 2)
    w_in = a["w_in"][0]
    cut = np.cumsum([QRANK, KVRANK, ROPE, H * HD, HD, HD, H * HD, H, HD, D])
    cq, ckv, kpe, bq, bk, bv, iq, iw, ik, ga, gb = np.split(w_in, cut, axis=1)
    pairs = np.stack([np.concatenate([bq, bk], 1).reshape(D, NPAIR, HD),
                      np.concatenate([iq, ik], 1).reshape(D, NPAIR, HD)], axis=2).reshape(D, -1)
    gate = np.concatenate([ga, gb], 1).reshape(DC, P, 2 * DC, P).transpose(2, 1, 0, 3)
    w_o = np.stack([rows(a["w_o_a"][0]), rows(a["w_o_b"][0])])
    g = a["a_qk_g"][0]
    gains = np.concatenate([a["a_kv_norm_g"][0], g[1, NOPE:], np.tile(a["b_qk_g"][0, 0], H), a["b_qk_g"][0, 1],
                            g[0], g[1, :NOPE]])
    return {
        "x_prompt": a["x_prompt"][0], "x_sample": a["x_sample"][0], "meta_tokens": a["meta_tokens"],
        "w_tok": rows(np.concatenate([cq, ckv, kpe, pairs, bv, iw], 1)),
        "w_gate": gate,
        "tabs": rotary_tables(),
        "gains": np.broadcast_to(gains, (P, GAINS)),
        "ln1": a["ln1_g"][0].reshape(DC, P).T, "ln2": a["ln2_g"][0].reshape(DC, P).T,
        "q_gain": a["a_q_norm_g"][0].reshape(2, P).T,
        "w_uq": rows(a["a_w_uq"][0]), "w_ukv": a["a_w_ukv"][0],
        "lat_t": a["cache_a_latent"][0, 0].T, "cache_kpe": a["cache_a_kpe"][0, 0],
        "bk_t": a["cache_b_k"][0, 0].T, "ik_t": a["cache_b_idx_k"][0, 0].T, "cache_bv": a["cache_b_v"][0, 0],
        "w_o": w_o.reshape(2, P, 4, 2, 512).transpose(3, 0, 1, 2, 4),
        "w_out": rows(a["w_out"][0]).reshape(P, DC, 2, 512).transpose(2, 0, 1, 3),
        "peer_wq": a["peer_wq"][0].reshape(DC, P, PH, P).transpose(2, 1, 0, 3),
        "subkeys": a["peer_subkeys"][0].transpose(1, 3, 0, 2),
        "peer_u": a["peer_u"][0].reshape(NKEY, NKEY, DC, P).transpose(1, 3, 2, 0),
        "peer_v": a["peer_v"][0].reshape(NKEY, NKEY, D),
    }


_OUTS = [("y_prompt", (SEQ, D)), ("y_sample", (DEC, D))]
_OUTS += [(f"new_{s}_{i}", (n, w)) for s, n in (("p", META + SEQ), ("s", DEC))
          for i, w in enumerate((KVRANK, ROPE, HD, HD, HD))]


def kernel(**inputs):
    import concourse.bacc as bacc
    from concourse.bass_utils import run_bass_kernel_spmd

    nc = bacc.Bacc("TRN2", target_bir_lowering=False, num_devices=1)
    io = Names()
    arrays = {}
    for name, a in lay_out(inputs).items():
        a = np.ascontiguousarray(a)
        arrays[f"in_{name}"] = a
        t = nc.dram_tensor(f"in_{name}", a.shape, mybir.dt.from_np(a.dtype), kind="ExternalInput").ap()
        io.__dict__[name] = t
    outs = {}
    for name, shape in _OUTS:
        outs[name] = nc.dram_tensor(f"out_{name}", shape, F32, kind="ExternalOutput").ap()
    io.y_prompt, io.y_sample = outs["y_prompt"], outs["y_sample"]
    io.new_p = [outs[f"new_p_{i}"] for i in range(5)]
    io.new_s = [outs[f"new_s_{i}"] for i in range(5)]
    io.dense = nc.dram_tensor("dense_gates", (NB, P, NKEY, TB), F32, kind="Internal").ap()
    io.gelu = nc.dram_tensor("gelu", (NKEY, P, NQ), F32, kind="Internal").ap()
    hybrid_step(nc, io)
    got = run_bass_kernel_spmd(nc, [arrays], core_ids=[0]).results[0]
    y = [got["out_y_prompt"][None], got["out_y_sample"][None]]
    return tuple(y + [got[f"out_{name}"][None, None] for name, _ in _OUTS[2:]])
```

```python
import numpy as np
import concourse.bass as bass
from concourse import mybir

F32 = mybir.dt.float32
F32R = mybir.dt.float32r
BF16 = mybir.dt.bfloat16
U32 = mybir.dt.uint32
ALU = mybir.AluOpType
ACT = mybir.ActivationFunctionType
AX_X = mybir.AxisListType.X

P = 128
D = 1024
DC = D // P
SEQ, DEC, META, PAST = 512, 32, 16, 256
TOK = SEQ + DEC + META
NQ = SEQ + DEC
NT = 5
KEYS = META + SEQ + PAST + DEC
KPROMPT = META + SEQ
KCACHE = KPROMPT
KSAMPLE = KPROMPT + PAST
CHUNK = 64
EPS = 1e-6
THETA = 500000.0

H = 8
NOPE, ROPE, AV = 64, 32, 64
AQK = NOPE + ROPE
QRANK, KVRANK = 256, 128
HD = 64
BROT = HD // 4
A_SCALE = AQK ** -0.5
B_SCALE = HD ** -0.5
IDX_SCALE = (H * HD) ** -0.5
TOPK_P = min(256, SEQ // 4)
TOPK_S = min(256, (PAST + DEC) // 4)

C_KV = QRANK
C_KPE = C_KV + KVRANK
C_B = C_KPE + ROPE
NPAIR = H + 1
C_BV = C_B + NPAIR * 2 * HD
C_IW = C_BV + HD
COLS = C_IW + H
PJ = COLS // 4
assert PJ * 4 == COLS and PJ <= 512

NKEY = 128
PH = 8
TOPE = 16
SLOTS = PH * TOPE
HALF = NQ // 2
HIDE = -1e30
NEG = -3.0e38
TAKEN = -3.3e38
SEEN = -3.2e38

GAINS = KVRANK + ROPE + NPAIR * HD + AQK + NOPE
G_KPE = KVRANK
G_B = G_KPE + ROPE
G_Q = G_B + NPAIR * HD
G_KN = G_Q + AQK
TABS = 2 * ROPE + 2 * BROT


def rows_of(t):
    return P if t < 4 else DEC + META


def queries_of(t):
    return P if t < 4 else DEC


def key_columns(t):
    if t < 4:
        return [(0, P, META + P * t)]
    if t == 4:
        return [(0, DEC, KSAMPLE), (DEC, META, 0)]
    return [(0, P, KCACHE + P * (t - 5))]


class Plan:

    def __init__(self, nc, at):
        self.nc, self.at = nc, at

    def __call__(self, name, shape, dt=F32):
        size = int(np.prod(shape[1:])) * (2 if dt == BF16 else 4)
        size = (size + 31) // 32 * 32
        t = self.nc.alloc_sbuf_tensor_at(name, shape, dt, offset=self.at)
        self.at += size
        return t


BASE = 16512


class Chain:

    def __init__(self, eng):
        self.eng, self.n = eng, {}

    def __call__(self, ins, sem):
        ins.then_inc(sem, 1)
        self.n[sem.name] = self.n.get(sem.name, 0) + 1
        self.eng.wait_ge(sem, self.n[sem.name])


def mid(ap, n):
    return ap.unsqueeze(1).to_broadcast([ap.shape[0], n, ap.shape[1]])


def last(ap, n):
    return ap.unsqueeze(2).to_broadcast([ap.shape[0], ap.shape[1], n])


def project(nc, io, m, sem):
    pl = Plan(nc, m.temps)
    w_tok = pl("w_tok", [P, 4, DC, PJ])
    x2 = [pl(f"xa{i}", [P, D]) for i in range(2)]
    xs = pl("xs", [P, D])
    pr = [pl(f"pr{i}", [P, COLS]) for i in range(2)]
    qf = pl("qf", [P, H, AQK])
    kf = pl("kf", [P, H, AQK])
    t1 = pl("t1", [P, 18 * BROT])
    t2 = pl("t2", [P, 18 * BROT])
    w_uq = pl("w_uq", [P, 2, H * AQK])
    w_ukv = pl("w_ukv", [P, H * (NOPE + AV)])
    gains = pl("gains", [P, GAINS])
    tabs = pl("tabs", [P, NT, TABS])
    latc = pl("latc", [P, PAST])
    lat = pl("lat", [P, P])
    cq = pl("cq", [P, 2, P])
    kpec = pl("kpec", [P, 2, ROPE])
    ln1 = pl("ln1", [P, DC])
    qg = pl("qg", [P, 2])
    stx = pl("stx", [P, 4])
    stp = pl("stp", [P, 3, 16])
    stq = pl("stq", [P, 3, 24])
    inv_n = pl("inv_n", [P, 16])
    assert pl.at <= m.end
    ident = m.ident

    psum = lambda name, shape: nc.psum_tensor(name, shape, F32)
    with psum("ps_x", [P, DC, P]) as ps_x, psum("ps_pj", [P, 2, 512]) as ps_pj, \
            psum("ps_tr", [P, 2, 4, P]) as ps_tr, psum("ps_mm", [P, 2, 512]) as ps_mm, nc.Block() as block:
        s_x = [sem(f"a_x{t}") for t in range(NT)]
        s_win = [sem(f"a_win{c}") for c in range(4)]
        s_small = sem("a_small")
        s_early = sem("a_early")
        s_cache = sem("a_cache")
        s_step = sem("a_step")
        s_ms_x = sem("a_ms_x")
        s_rt_x = sem("a_rt_x")
        s_xs = sem("a_xs")
        s_xT = sem("a_xT")
        s_hT = sem("a_hT")
        s_proj = sem("a_proj")
        s_pr = sem("a_pr")
        s_ms_l = sem("a_ms_l")
        s_rt_l = sem("a_rt_l")
        s_lat = sem("a_lat")
        s_ms_p = sem("a_ms_p")
        s_rt_p = sem("a_rt_p")
        s_norm = sem("a_norm")
        s_tr = sem("a_tr")
        s_trc = sem("a_trc")
        s_mm = sem("a_mm")
        s_mmc = sem("a_mmc")
        s_ms_q = sem("a_ms_q")
        s_rt_q = sem("a_rt_q")
        s_qk = sem("a_qk")
        s_kv = sem("a_kv")
        s_ident = sem("a_ident")
        s_out = [sem("a_out0"), sem("a_out1")]

        groups = [(t, "k", g) for t in (5, 6) for g in range(2)]
        for t in range(NT):
            groups.append((t, "lat", 0))
            groups += [(t, "pair", g) for g in range(3)]
            groups += [(t, "q", 0), (t, "q", 1), (t, "k", 0), (t, "k", 1)]
        index = {g: n for n, g in enumerate(groups)}
        halves = [(t, "kv", j) for t in (5, 6) for j in range(2)]
        halves += [(t, k, j) for t in range(NT) for k in ("q", "kv") for j in range(2)]
        mm_index = {g: n for n, g in enumerate(halves)}

        turn_of = {t: n for n, t in enumerate((5, 6, 0, 1, 2, 3, 4))}
        before = {6: 5, 0: 6, 1: 0, 2: 1, 3: 2, 4: 3}

        def pair(buf, g):
            return buf[:, C_B + 2 * HD * g:C_B + 2 * HD * (g + 1)]

        @block.sync
        def _(sp):
            def load_x(t):
                if t < 4:
                    sp.dma_start(x2[t % 2][:, :], io.x_prompt[P * t:P * (t + 1), :]).then_inc(s_x[t], 16)
                else:
                    sp.dma_start(x2[t % 2][0:DEC, :], io.x_sample[:, :]).then_inc(s_x[t], 16)
                    sp.dma_start(x2[t % 2][DEC:DEC + META, :], io.meta_tokens[:, :]).then_inc(s_x[t], 16)

            load_x(0)
            sp.dma_start(latc[:, :], io.lat_t[:, :]).then_inc(s_early, 16)
            sp.dma_start(w_ukv[:, :], io.w_ukv[:, :]).then_inc(s_early, 16)
            sp.dma_start(ln1[:, :], io.ln1[:, :]).then_inc(s_early, 16)
            sp.dma_start(gains[:, :], io.gains[:, :]).then_inc(s_early, 16)
            sp.dma_start(kpec[:, :, :], io.cache_kpe[:, :].rearrange("(a p) r -> p a r", p=P)).then_inc(s_early, 16)
            for c in range(4):
                sp.dma_start(w_tok[:, c, :, :], io.w_tok[c, :, :, :]).then_inc(s_win[c], 16)
            sp.dma_start(tabs[:, :, :], io.tabs[:, :, :]).then_inc(s_small, 16)
            sp.dma_start(qg[:, :], io.q_gain[:, :]).then_inc(s_small, 16)
            sp.dma_start(w_uq[:, :, :], io.w_uq[:, :, :]).then_inc(s_small, 16)
            load_x(1)
            for t in range(NT):
                if t + 2 < NT:
                    sp.wait_ge(s_xs, t + 1)
                    load_x(t + 2)
                sp.wait_ge(s_norm, t + 1)
                buf = pr[t % 2]
                for dst, c0, n in ((0, C_KV, KVRANK), (1, C_KPE, ROPE), (2, C_B + 2 * HD * H, HD),
                                   (3, C_BV, HD), (4, C_B + 2 * HD * H + HD, HD)):
                    if t < 4:
                        sp.dma_start(io.new_p[dst][META + P * t:META + P * (t + 1), :],
                                     buf[:, c0:c0 + n]).then_inc(s_out[t % 2], 16)
                    else:
                        sp.dma_start(io.new_s[dst][:, :], buf[0:DEC, c0:c0 + n]).then_inc(s_out[0], 16)
                        sp.dma_start(io.new_p[dst][0:META, :],
                                     buf[DEC:DEC + META, c0:c0 + n]).then_inc(s_out[0], 16)
            sp.wait_ge(s_out[0], 16 * 5 * 4)
            sp.wait_ge(s_out[1], 16 * 5 * 2)

        @block.gpsimd
        def _(pool):
            nc.gpsimd.memset(ident[:, :], 0.0).then_inc(s_ident, 1)
            pool.wait_ge(s_ident, 1)
            nc.gpsimd.affine_select(out=ident[:, :], in_=ident[:, :], compare_op=ALU.not_equal, fill=1.0,
                                    base=0, pattern=[[-1, P]], channel_multiplier=1).then_inc(s_ident, 1)

        @block.scalar
        def _(act):
            act.dma_start(m.bik[0:HD, KCACHE:KSAMPLE], io.bk_t[:, :]).then_inc(s_cache, 16)
            act.dma_start(m.bik[HD:P, KCACHE:KSAMPLE], io.ik_t[:, :]).then_inc(s_cache, 16)
            for a in range(2):
                act.dma_start(m.vb[:, 5 + a, :], io.cache_bv[P * a:P * (a + 1), :]).then_inc(s_cache, 16)

            def root(n_sem, r_sem, n, dst, src):
                act.wait_ge(n_sem, n)
                nc.scalar.activation(dst, src, ACT.Sqrt).then_inc(r_sem, 1)

            def proj_out(t, quarters):
                r = rows_of(t)
                for c in quarters:
                    act.wait_ge(s_proj, 4 * t + c + 1)
                    if c == 0 and t >= 2:
                        act.wait_ge(s_out[t % 2], 16 * 5 * (t // 2))
                        act.wait_ge(s_tr, index[(t - 2, "pair", 2)] + 1)
                    nc.scalar.copy(pr[t % 2][0:r, PJ * c:PJ * (c + 1)],
                                   ps_pj[0:r, c % 2, 0:PJ]).then_inc(s_pr, 1)

            def tr_out(key):
                t, kind, g = key
                n = index[key]
                r = rows_of(t) if t < NT else P
                bank = ps_tr[:, n % 2, :, :]
                act.wait_ge(s_tr, n + 1)
                if kind == "lat":
                    if t:
                        act.wait_ge(s_mm, mm_index[(t - 1, "kv", 1)] + 1)
                    else:
                        act.wait_ge(s_small, 16 * 3)
                    for j in range(2):
                        nc.scalar.activation(cq[:, j, 0:r], bank[:, j, 0:r], ACT.Copy, scale=qg[:, j:j + 1])
                    nc.scalar.copy(lat[:, 0:r], bank[:, 2, 0:r]).then_inc(s_trc, 1)
                    return
                moves = []
                for r0, nr, k0 in key_columns(t):
                    if kind == "pair" and g == 2:
                        moves.append((m.bik[:, k0:k0 + nr], bank[:, 0, r0:r0 + nr]))
                    if kind == "k":
                        moves.append((m.kt[0:AQK, 4 * g:4 * g + 4, k0:k0 + nr], bank[0:AQK, :, r0:r0 + nr]))
                nq = queries_of(t)
                if kind == "pair" and g < 2:
                    moves.append((m.biq[:, 4 * g:4 * g + 4, P * t:P * t + nq], bank[:, :, 0:nq]))
                if kind == "q":
                    moves.append((m.qt[0:AQK, 4 * g:4 * g + 4, P * t:P * t + nq], bank[0:AQK, :, 0:nq]))
                for i, (dst, src) in enumerate(moves):
                    ins = nc.scalar.copy(dst, src)
                ins.then_inc(s_trc, 1)

            def mm_out(t, kind):
                r = rows_of(t) if t < NT else P
                for j in range(2):
                    act.wait_ge(s_mm, mm_index[(t, kind, j)] + 1)
                    if kind == "q":
                        if j == 0 and t:
                            act.wait_ge(s_tr, index[(t - 1, "q", 1)] + 1)
                        nc.scalar.copy(qf[0:r, 4 * j:4 * j + 4, :],
                                       ps_mm[0:r, j, 0:4 * AQK].rearrange("p (h c) -> p h c", h=4)
                                       ).then_inc(s_mmc, 1)
                    else:
                        if j == 0 and t in before:
                            act.wait_ge(s_tr, index[(before[t], "k", 1)] + 1)
                        kv = ps_mm[0:r, j, :].rearrange("p (h c) -> p h c", h=4)
                        nc.scalar.copy(kf[0:r, 4 * j:4 * j + 4, 0:NOPE], kv[:, :, 0:NOPE])
                        nc.scalar.copy(m.va[0:r, t, 4 * j:4 * j + 4, :], kv[:, :, NOPE:]).then_inc(s_mmc, 1)

            def root_latents(t):
                root(s_ms_l, s_rt_l, t + 1, stp[:, 2, 0:2], stp[:, 1, 0:2])

            def root_rows(t):
                lo = 0 if t < NT else 16
                root(s_ms_q, s_rt_q, turn_of[t] + 1, stq[:, 2, lo:24], stq[:, 1, lo:24])

            root(s_ms_x, s_rt_x, 1, stx[:, 2:3], stx[:, 1:2])
            for t in (5, 6):
                mm_out(t, "kv")
                root_rows(t)
                proj_out(0, (t - 5,))
                for g in range(2):
                    tr_out((t, "k", g))
            root_latents(0)
            proj_out(0, (2, 3))
            for t in range(NT):
                if t + 1 < NT:
                    root(s_ms_x, s_rt_x, t + 2, stx[:, 2:3], stx[:, 1:2])
                tr_out((t, "lat", 0))
                mm_out(t, "q")
                mm_out(t, "kv")
                root(s_ms_p, s_rt_p, t + 1, stp[:, 2, 2:12], stp[:, 1, 2:12])
                if t + 1 < NT:
                    proj_out(t + 1, (0,))
                root_rows(t)
                if t + 1 < NT:
                    proj_out(t + 1, (1,))
                    root_latents(t + 1)
                    proj_out(t + 1, (2, 3))
                for g in range(3):
                    tr_out((t, "pair", g))
                for g in range(2):
                    tr_out((t, "q", g))
                for g in range(2):
                    tr_out((t, "k", g))
            act.wait_ge(s_cache, 16 * 4)

        @block.vector
        def _(dve):
            step = Chain(dve)
            v = nc.vector
            for j, (n, lo, hi) in enumerate(((QRANK, 0, 1), (KVRANK, 1, 2), (ROPE, 2, 3), (HD, 3, 12))):
                v.memset(inv_n[:, lo:hi], 1.0 / n)
            for buf in (stx, stp, stq):
                step(v.memset(buf[:], 1.0), s_step)

            def x_scale(t):
                r = rows_of(t)
                dve.wait_ge(s_x[t], 16 if t < 4 else 32)
                if t:
                    dve.wait_ge(s_xT, DC * t)
                step(v.tensor_tensor_reduce(out=xs[0:r, :], in0=x2[t % 2][0:r, :], in1=x2[t % 2][0:r, :],
                                            scale=1.0, scalar=0.0, op0=ALU.mult, op1=ALU.add,
                                            accum_out=stx[0:r, 0:1]), s_step)
                v.tensor_scalar(stx[:, 1:2], stx[:, 0:1], 1.0 / D, EPS, ALU.mult, ALU.add).then_inc(s_ms_x, 1)
                dve.wait_ge(s_rt_x, t + 1)
                step(v.reciprocal(stx[:, 3:4], stx[:, 2:3]), s_step)
                step(v.tensor_scalar(xs[0:r, :], x2[t % 2][0:r, :], stx[0:r, 3:4], None, ALU.mult), s_xs)

            def hT_out(t):
                r = rows_of(t)
                for j in range(2):
                    dve.wait_ge(s_xT, DC * t + 4 * (j + 1))
                    v.tensor_tensor(m.ht[:, 4 * j:4 * j + 4, P * t:P * t + r], ps_x[:, 4 * j:4 * j + 4, 0:r],
                                    last(ln1[:, 4 * j:4 * j + 4], r), ALU.mult).then_inc(s_hT, 1)

            def rotate(x, cos, sin, n, half):
                r = x.shape[0]
                a = t1[0:r, 0:2 * n * half].rearrange("p (n k) -> p n k", n=n)
                b = t2[0:r, 0:2 * n * half].rearrange("p (n k) -> p n k", n=n)
                v.tensor_tensor(a, x, mid(cos, n), ALU.mult)
                v.tensor_tensor(b[:, :, 0:half], x[:, :, half:2 * half], mid(sin[:, 0:half], n), ALU.mult)
                step(v.tensor_tensor(b[:, :, half:2 * half], x[:, :, 0:half],
                                     mid(sin[:, half:2 * half], n), ALU.mult), s_step)
                return v.tensor_tensor(x, a, b, ALU.add)

            def latent_norm(t):
                r = rows_of(t)
                buf = pr[t % 2][0:r]
                sq = xs[0:r, :]
                dve.wait_ge(s_pr, 4 * t + 1)
                dve.wait_ge(s_xT, DC * (t + 1))
                step(v.tensor_tensor(sq[:, 0:C_KPE], buf[:, 0:C_KPE], buf[:, 0:C_KPE], ALU.mult), s_step)
                v.tensor_reduce(stp[0:r, 0, 0:1], sq[:, 0:C_KV], AX_X, ALU.add)
                step(v.tensor_reduce(stp[0:r, 0, 1:2], sq[:, C_KV:C_KPE], AX_X, ALU.add), s_step)
                step(v.tensor_tensor(stp[:, 1, 0:2], stp[:, 0, 0:2], inv_n[:, 0:2], ALU.mult), s_step)
                v.tensor_scalar(stp[:, 1, 0:2], stp[:, 1, 0:2], EPS, None, ALU.add).then_inc(s_ms_l, 1)
                if t == 0:
                    dve.wait_ge(s_small, 16 * 3)
                dve.wait_ge(s_rt_l, t + 1)
                step(v.reciprocal(stp[:, 2, 0:2], stp[:, 2, 0:2]), s_step)
                v.tensor_scalar(buf[:, 0:C_KV], buf[:, 0:C_KV], stp[0:r, 2, 0:1], None, ALU.mult)
                step(v.scalar_tensor_tensor(out=buf[:, C_KV:C_KPE], in0=buf[:, C_KV:C_KPE],
                                            scalar=stp[0:r, 2, 1:2], in1=gains[0:r, 0:G_KPE], op0=ALU.mult,
                                            op1=ALU.mult), s_lat)

            def head_norm(t):
                r = rows_of(t)
                buf = pr[t % 2][0:r]
                pairs = buf[:, C_B:C_BV].rearrange("p (n k) -> p n k", n=NPAIR)
                sq = xs[0:r, :]
                dve.wait_ge(s_pr, 4 * t + 4)
                v.tensor_tensor(sq[:, C_KPE:C_B], buf[:, C_KPE:C_B], buf[:, C_KPE:C_B], ALU.mult)
                sqb = sq[:, C_B:C_B + NPAIR * HD].rearrange("p (n k) -> p n k", n=NPAIR)
                step(v.tensor_tensor(sqb, pairs[:, :, 0:HD], pairs[:, :, 0:HD], ALU.mult), s_step)
                v.tensor_reduce(stp[0:r, 0, 2:3], sq[:, C_KPE:C_B], AX_X, ALU.add)
                step(v.tensor_reduce(stp[0:r, 0, 3:12], sqb, AX_X, ALU.add), s_step)
                step(v.tensor_tensor(stp[:, 1, 2:12], stp[:, 0, 2:12], inv_n[:, 2:12], ALU.mult), s_step)
                v.tensor_scalar(stp[:, 1, 2:12], stp[:, 1, 2:12], EPS, None, ALU.add).then_inc(s_ms_p, 1)
                v.tensor_copy(m.vb[0:r, t, :], buf[:, C_BV:C_IW])
                v.tensor_scalar(m.iw[0:r, t, :], buf[:, C_IW:COLS], IDX_SCALE, None, ALU.mult)
                dve.wait_ge(s_rt_p, t + 1)
                step(v.reciprocal(stp[:, 2, 2:12], stp[:, 2, 2:12]), s_step)
                rs = stp[0:r, 2, :]
                v.scalar_tensor_tensor(out=buf[:, C_KPE:C_B], in0=buf[:, C_KPE:C_B], scalar=rs[:, 2:3],
                                       in1=gains[0:r, G_KPE:G_B], op0=ALU.mult, op1=ALU.mult)
                step(v.tensor_tensor(pairs[:, :, 0:HD], pairs[:, :, 0:HD], last(rs[:, 3:12], HD), ALU.mult),
                     s_step)
                step(v.tensor_tensor(pairs[:, :, 0:HD], pairs[:, :, 0:HD],
                                     gains[0:r, G_B:G_Q].rearrange("p (n k) -> p n k", n=NPAIR), ALU.mult),
                     s_step)
                tab = tabs[0:r, t, :]
                step(rotate(buf[:, C_KPE:C_B].unsqueeze(1), tab[:, 0:ROPE], tab[:, ROPE:2 * ROPE], 1, ROPE // 2),
                     s_step)
                heads = buf[:, C_B:C_BV].rearrange("p (n k) -> p n k", n=2 * NPAIR)
                step(rotate(heads[:, :, 0:BROT], tab[:, 2 * ROPE:2 * ROPE + BROT],
                            tab[:, 2 * ROPE + BROT:TABS], 2 * NPAIR, BROT // 2), s_norm)

            def qk_norm(t):
                r = rows_of(t) if t < NT else P
                new = t < NT
                sq = xs[0:r, 0:H * AQK].rearrange("p (h c) -> p h c", h=H)
                lo = 0 if new else 16
                if new:
                    dve.wait_ge(s_mmc, mm_index[(t, "q", 1)] + 1)
                    step(v.tensor_tensor(sq, qf[0:r], qf[0:r], ALU.mult), s_step)
                    v.tensor_reduce(stq[0:r, 0, 0:8], sq[:, :, 0:NOPE], AX_X, ALU.add)
                    step(v.tensor_reduce(stq[0:r, 0, 8:16], sq[:, :, NOPE:], AX_X, ALU.add), s_step)
                dve.wait_ge(s_mmc, mm_index[(t, "kv", 1)] + 1)
                step(v.tensor_tensor(sq[:, :, 0:NOPE], kf[0:r, :, 0:NOPE], kf[0:r, :, 0:NOPE], ALU.mult), s_step)
                step(v.tensor_reduce(stq[0:r, 0, 16:24], sq[:, :, 0:NOPE], AX_X, ALU.add), s_step)
                if new:
                    v.tensor_scalar(stq[:, 1, 8:16], stq[:, 0, 8:16], 1.0 / ROPE, EPS, ALU.mult, ALU.add)
                    v.tensor_scalar(stq[:, 1, 0:8], stq[:, 0, 0:8], 1.0 / NOPE, EPS, ALU.mult, ALU.add)
                step(v.tensor_scalar(stq[:, 1, 16:24], stq[:, 0, 16:24], 1.0 / NOPE, EPS, ALU.mult, ALU.add),
                     s_ms_q)
                dve.wait_ge(s_rt_q, turn_of[t] + 1)
                step(v.reciprocal(stq[:, 2, lo:24], stq[:, 2, lo:24]), s_step)
                rs = stq[0:r, 2, :]
                q, k = qf[0:r], kf[0:r]
                if new:
                    v.tensor_tensor(q[:, :, 0:NOPE], q[:, :, 0:NOPE], last(rs[:, 0:8], NOPE), ALU.mult)
                    v.tensor_tensor(q[:, :, NOPE:], q[:, :, NOPE:], last(rs[:, 8:16], ROPE), ALU.mult)
                step(v.tensor_tensor(k[:, :, 0:NOPE], k[:, :, 0:NOPE], last(rs[:, 16:24], NOPE), ALU.mult), s_step)
                if new:
                    v.tensor_tensor(q, q, mid(gains[0:r, G_Q:G_KN], H), ALU.mult)
                kpe = pr[t % 2][0:r, C_KPE:C_B] if new else kpec[:, t - 5, :]
                v.tensor_copy(k[:, :, NOPE:], mid(kpe, H))
                step(v.tensor_tensor(k[:, :, 0:NOPE], k[:, :, 0:NOPE], mid(gains[0:r, G_KN:GAINS], H), ALU.mult),
                     s_step if new else s_qk)
                if new:
                    tab = tabs[0:r, t, :]
                    rotate(q[:, :, NOPE:], tab[:, 0:ROPE], tab[:, ROPE:2 * ROPE], H, ROPE // 2).then_inc(s_qk, 1)

            x_scale(0)
            dve.wait_ge(s_early, 16 * 5)
            hT_out(0)
            for t in (5, 6):
                qk_norm(t)
            latent_norm(0)
            for t in range(NT):
                if t + 1 < NT:
                    x_scale(t + 1)
                    hT_out(t + 1)
                head_norm(t)
                qk_norm(t)
                if t + 1 < NT:
                    latent_norm(t + 1)

        @block.tensor
        def _(pe):
            def x_transposes(t):
                r = rows_of(t)
                pe.wait_ge(s_xs, t + 1)
                if t:
                    pe.wait_ge(s_hT, 2 * t)
                for c in range(DC):
                    nc.tensor.transpose(ps_x[:, c, 0:r], xs[0:r, P * c:P * (c + 1)],
                                        ident[0:r, 0:r]).then_inc(s_xT, 1)

            def projection(t, quarters=range(4)):
                r = rows_of(t)
                pe.wait_ge(s_hT, 2 * t + 2)
                for c in quarters:
                    if t == 0:
                        pe.wait_ge(s_win[c], 16)
                    if 4 * t + c >= 2:
                        pe.wait_ge(s_pr, 4 * t + c - 1)
                    for k in range(DC):
                        ins = nc.tensor.matmul(ps_pj[0:r, c % 2, 0:PJ], m.ht[:, k, P * t:P * t + r],
                                               w_tok[:, c, k, :], start=(k == 0), stop=(k == DC - 1))
                    ins.then_inc(s_proj, 1)

            def turn(key):
                t, kind, g = key
                n = index[key]
                r = rows_of(t) if t < NT else P
                buf = pr[t % 2][0:r]
                if n >= 2:
                    pe.wait_ge(s_trc, n - 1)
                if kind == "lat":
                    pe.wait_ge(s_lat, t + 1)
                    srcs = [buf[:, 0:P], buf[:, P:2 * P], buf[:, C_KV:C_KPE]]
                elif kind == "pair":
                    pe.wait_ge(s_norm, t + 1)
                    srcs = [pair(buf, i) for i in (range(4 * g, 4 * g + 4) if g < 2 else [H])]
                else:
                    pe.wait_ge(s_qk, turn_of[t] + 1)
                    src = qf if kind == "q" else kf
                    srcs = [src[0:r, i, :] for i in range(4 * g, 4 * g + 4)]
                for j, s in enumerate(srcs):
                    ins = nc.tensor.transpose(ps_tr[0:s.shape[1], n % 2, j, 0:r], s, ident[0:r, 0:r])
                ins.then_inc(s_tr, 1)

            def up(t, kind):
                r = rows_of(t) if t < NT else P
                for j in range(2):
                    n = mm_index[(t, kind, j)]
                    if n >= 2:
                        pe.wait_ge(s_mmc, n - 1)
                    if kind == "q":
                        for k in range(2):
                            ins = nc.tensor.matmul(ps_mm[0:r, j, 0:4 * AQK], cq[:, k, 0:r],
                                                   w_uq[:, k, 4 * AQK * j:4 * AQK * (j + 1)],
                                                   start=(k == 0), stop=(k == 1))
                    else:
                        left = lat[:, 0:r] if t < NT else latc[:, P * (t - 5):P * (t - 4)]
                        ins = nc.tensor.matmul(ps_mm[0:r, j, :], left, w_ukv[:, 512 * j:512 * (j + 1)],
                                               start=True, stop=True)
                    ins.then_inc(s_mm, 1)

            pe.wait_ge(s_ident, 2)
            x_transposes(0)
            pe.wait_ge(s_early, 16 * 5)
            for t in (5, 6):
                up(t, "kv")
                projection(0, (t - 5,))
                for g in range(2):
                    turn((t, "k", g))
            projection(0, (2, 3))
            for t in range(NT):
                turn((t, "lat", 0))
                pe.wait_ge(s_trc, index[(t, "lat", 0)] + 1)
                if t == 0:
                    pe.wait_ge(s_small, 16 * 3)
                up(t, "q")
                up(t, "kv")
                if t + 1 < NT:
                    x_transposes(t + 1)
                    projection(t + 1)
                for g in range(3):
                    turn((t, "pair", g))
                for kind in ("q", "k"):
                    for g in range(2):
                        turn((t, kind, g))


def attend(nc, io, m, sem):
    pl = Plan(nc, m.temps)
    m.oab = pl("oab", [P, NT, 2, H * AV])
    m.sg = pl("sg", [P, 2, DC, NQ])
    m.after_attend = pl.at
    wg = [pl(f"wg{i}", [P, DC, P]) for i in range(2)]
    vm = pl("vm", [META, H * AV + HD])
    biasA = pl("biasA", [P, KPROMPT])
    biasB = pl("biasB", [P, KPROMPT])
    score = pl("score", [P, KPROMPT])
    rel = [pl(f"rel{i}", [P, KPROMPT]) for i in range(2)]
    logit = [pl(f"logit{i}", [P, KPROMPT]) for i in range(3)]
    prob = [pl(f"prob{i}", [P, KPROMPT]) for i in range(3)]
    probT = [pl(f"probT{i}", [P, NT, P]) for i in range(2)]
    best = pl("best", [P, 8])
    mx = pl("mx", [P, 3, 2])
    total = pl("total", [P, 2, 2, H])
    inv = pl("inv", [P, H])
    assert pl.at <= m.end
    ident = m.ident

    units = [(t, kind, h) for t in range(NT) for kind in ("index", "mla", "dsa") for h in range(H)]
    N = len(units)
    number = {u: n for n, u in enumerate(units)}
    att = [n for n, u in enumerate(units) if u[1] != "index"]
    att_no = {n: i for i, n in enumerate(att)}
    idx_no = {n: i for i, n in enumerate(n for n, u in enumerate(units) if u[1] == "index")}
    TURN, VALUES, LAG = 2, 3, 3
    gates = [(g // 2, g % 2) for g in range(4 * DC)]
    gate_at = {2 * g + 6: g for g in range(len(gates))}
    assert max(gate_at) + 1 < number[(3, "index", 0)]

    def keys(t):
        return (0, META + P * (t + 1)) if t < 4 else (KPROMPT, PAST + DEC)

    def blocks(t):
        if t < 4:
            return [(META + P * j, P, j) for j in range(t + 1)] + [(0, META, None)]
        return [(0, P, 5), (P, P, 6), (PAST, DEC, 4)]

    def value(kind, h, r, j):
        if kind == "mla":
            return m.va[0:r, j, h, :] if j is not None else vm[0:r, AV * h:AV * (h + 1)]
        return m.vb[0:r, j, :] if j is not None else vm[0:r, H * AV:]

    def halves(buf, t):
        q, nk = queries_of(t), keys(t)[1]
        return buf[0:q, 0:nk].rearrange("p (a k) -> p a k", a=2)

    psum = lambda name, shape: nc.psum_tensor(name, shape, F32)
    with psum("ps_sc", [P, 2, 2, 512]) as ps_sc, psum("ps_pt", [P, 4, P]) as ps_pt, \
            psum("ps_o", [P, 2, 512]) as ps_o, psum("ps_g", [P, 512]) as ps_g, nc.Block() as block:
        s_wg = [sem("b_wg0"), sem("b_wg1")]
        s_gate = sem("b_gate")
        s_gatec = sem("b_gatec")
        s_vm = sem("b_vm")
        s_step = sem("b_step")
        s_score = sem("b_score")
        s_rel = sem("b_rel")
        s_acc = sem("b_acc")
        s_logit = sem("b_logit")
        s_max = sem("b_max")
        s_prob = sem("b_prob")
        s_pt = sem("b_pt")
        s_ptc = sem("b_ptc")
        s_pv = sem("b_pv")
        s_o = sem("b_o")

        @block.sync
        def _(sp):
            sp.dma_start(vm[:, 0:H * AV], m.va[DEC:DEC + META, 4, :, :].rearrange("p h c -> p (h c)")).then_inc(s_vm, 16)
            sp.dma_start(vm[:, H * AV:], m.vb[DEC:DEC + META, 4, :]).then_inc(s_vm, 16)
            for i in range(2 * DC):
                if i >= 2:
                    sp.wait_ge(s_gate, 2 * (i - 1))
                sp.dma_start(wg[i % 2][:, :, :], io.w_gate[i, :, :, :]).then_inc(s_wg[i % 2], 16)

        def turned_at(j, r, q):
            return ps_pt[0:r, j, 0:q] if j < 4 else ps_g[0:r, 0:q]

        def wait_consumed(eng, n):
            if n in idx_no:
                eng.wait_ge(s_rel, idx_no[n] + 1)
            else:
                eng.wait_ge(s_logit, att_no[n] + 1)

        @block.tensor
        def _(pe):
            def scores(n):
                t, kind, h = units[n]
                q = queries_of(t)
                k0, nk = keys(t)
                if n >= 2:
                    wait_consumed(pe, n - 2)
                if kind == "mla":
                    left, right = m.qt[0:AQK, h, P * t:P * t + q], m.kt[0:AQK, h, k0:k0 + nk]
                elif kind == "dsa":
                    left, right = m.biq[0:HD, h, P * t:P * t + q], m.bik[0:HD, k0:k0 + nk]
                else:
                    left, right = m.biq[HD:P, h, P * t:P * t + q], m.bik[HD:P, k0:k0 + nk]
                for a in range(2):
                    ins = nc.tensor.matmul(ps_sc[0:q, n % 2, a, 0:nk // 2], left,
                                           right[:, nk // 2 * a:nk // 2 * (a + 1)], start=True, stop=True)
                ins.then_inc(s_score, 1)

            def turn(n):
                t, kind, h = units[n]
                q, i = queries_of(t), att_no[n]
                pe.wait_ge(s_prob, i + 1)
                if t == 3 and h == 0:
                    pe.wait_ge(s_gatec, len(gates))
                for j, (c, r, _) in enumerate(blocks(t)):
                    ins = nc.tensor.transpose(turned_at(j, r, q), prob[i % 3][0:q, c:c + r], ident[0:q, 0:q])
                ins.then_inc(s_pt, 1)

            def values(n):
                t, kind, h = units[n]
                q, i = queries_of(t), att_no[n]
                x = 0 if kind == "mla" else 1
                pe.wait_ge(s_ptc, i + 1)
                if h == 0 and t:
                    pe.wait_ge(s_o, 2 * t - 1 + x)
                if i == 0:
                    pe.wait_ge(s_vm, 32)
                bl = blocks(t)
                for j, (c, r, v) in enumerate(bl):
                    ins = nc.tensor.matmul(ps_o[0:q, x, AV * h:AV * (h + 1)], probT[i % 2][0:r, j, 0:q],
                                           value(kind, h, r, v), start=(j == 0), stop=(j == len(bl) - 1))
                ins.then_inc(s_pv, 1)

            def gate(g):
                i, hf = gates[g]
                if hf == 0:
                    pe.wait_ge(s_wg[i % 2], 16 * (i // 2 + 1))
                if g:
                    pe.wait_ge(s_gatec, g)
                for k in range(DC):
                    ins = nc.tensor.matmul(ps_g[:, 0:HALF], wg[i % 2][:, k, :], m.ht[:, k, HALF * hf:HALF * (hf + 1)],
                                           start=(k == 0), stop=(k == DC - 1))
                ins.then_inc(s_gate, 1)

            for n in range(N + VALUES):
                if n < N:
                    scores(n)
                if n - VALUES in att_no:
                    values(n - VALUES)
                if n - TURN in att_no:
                    turn(n - TURN)
                if n in gate_at:
                    gate(gate_at[n])

        @block.scalar
        def _(act):
            def unit(n):
                t, kind, h = units[n]
                q = queries_of(t)
                if kind == "index":
                    i = idx_no[n]
                    act.wait_ge(s_score, n + 1)
                    if i >= 2:
                        act.wait_ge(s_acc, i - 1)
                    nc.scalar.activation(halves(rel[i % 2], t), ps_sc[0:q, n % 2, :, 0:keys(t)[1] // 2],
                                         ACT.Relu).then_inc(s_rel, 1)
                    return
                i, x = att_no[n], 0 if kind == "mla" else 1
                act.wait_ge(s_max, i + 1)
                if i >= 3:
                    act.wait_ge(s_pt, i - 2)
                if h == 0 and t >= 2:
                    act.wait_ge(s_o, 2 * (t - 2) + 1 + x)
                nk = keys(t)[1]
                nc.scalar.activation(prob[i % 3][0:q, 0:nk], logit[i % 3][0:q, 0:nk], ACT.Exp,
                                     bias=mx[0:q, i % 3, 1:2], scale=A_SCALE if x == 0 else B_SCALE,
                                     accum_out=total[0:q, t % 2, x, h:h + 1]).then_inc(s_prob, 1)

            def turned(n):
                t, kind, h = units[n]
                q, i = queries_of(t), att_no[n]
                act.wait_ge(s_pt, i + 1)
                if i >= 2:
                    act.wait_ge(s_pv, i - 1)
                bl = blocks(t)
                full = sum(r == P for _, r, _ in bl)
                nc.scalar.copy(probT[i % 2][:, 0:full, 0:q], ps_pt[:, 0:full, 0:q])
                r = bl[-1][1]
                nc.scalar.copy(probT[i % 2][0:r, full, 0:q], turned_at(full, r, q)).then_inc(s_ptc, 1)

            for n in range(N + TURN):
                if n - TURN in att_no:
                    turned(n - TURN)
                if n < N:
                    unit(n)
                if n - 1 in gate_at:
                    g = gate_at[n - 1]
                    i, hf = gates[g]
                    act.wait_ge(s_gate, g + 1)
                    nc.scalar.copy(m.sg[:, i // DC, i % DC, HALF * hf:HALF * (hf + 1)],
                                   ps_g[:, 0:HALF]).then_inc(s_gatec, 1)

        @block.vector
        def _(dve):
            step = Chain(dve)
            v = nc.vector

            def index_unit(n):
                t, _, h = units[n]
                q, nk = queries_of(t), keys(t)[1]
                i = idx_no[n]
                dve.wait_ge(s_rel, i + 1)
                w = m.iw[0:q, t, h:h + 1]
                if h == 0:
                    step(v.tensor_scalar(score[0:q, 0:nk], rel[i % 2][0:q, 0:nk], w, None, ALU.mult), s_acc)
                else:
                    step(v.scalar_tensor_tensor(out=score[0:q, 0:nk], in0=rel[i % 2][0:q, 0:nk], scalar=w,
                                                in1=score[0:q, 0:nk], op0=ALU.mult, op1=ALU.add), s_acc)

            def hide_ahead(t):
                if t < 4:
                    nk = keys(t)[1]
                    step(v.memset(score[0:CHUNK, nk - CHUNK:nk], NEG), s_step)

            def choose_some(t, h):
                q, nk = queries_of(t), keys(t)[1]
                sc = score[0:q, 0:nk]
                rounds = (TOPK_P if t < 4 else TOPK_S) // 8
                assert rounds <= 2 * H
                for _ in range(2 * h, min(2 * h + 2, rounds)):
                    step(v.max(best[0:q, :], sc), s_step)
                    step(v.match_replace(sc, best[0:q, :], sc, TAKEN), s_step)

            def hide_unchosen(t):
                q, nk = queries_of(t), keys(t)[1]
                sc = score[0:q, 0:nk]
                step(v.tensor_scalar(biasB[0:q, 0:nk], sc, SEEN, HIDE, ALU.is_gt, ALU.mult), s_step)
                if t < 4:
                    step(v.tensor_tensor(biasB[0:q, 0:nk], biasB[0:q, 0:nk], biasA[0:q, KPROMPT - nk:], ALU.add),
                         s_step)

            def logits(n):
                t, kind, h = units[n]
                q, nk = queries_of(t), keys(t)[1]
                i = att_no[n]
                if kind == "dsa":
                    bias = halves(biasB, t)
                elif t < 4:
                    bias = biasA[0:q, KPROMPT - nk:].rearrange("p (a k) -> p a k", a=2)
                else:
                    bias = halves(biasA, t)
                dve.wait_ge(s_score, n + 1)
                if i >= 3:
                    dve.wait_ge(s_prob, i - 2)
                step(v.tensor_tensor_reduce(out=halves(logit[i % 3], t), in0=ps_sc[0:q, n % 2, :, 0:nk // 2],
                                            in1=bias, scale=1.0, scalar=NEG, op0=ALU.add, op1=ALU.max,
                                            accum_out=mx[0:q, i % 3, 0:1]), s_logit)
                v.tensor_scalar(mx[0:q, i % 3, 1:2], mx[0:q, i % 3, 0:1],
                                -(A_SCALE if kind == "mla" else B_SCALE), None, ALU.mult).then_inc(s_max, 1)

            def normalise(n):
                t, kind, _ = units[n]
                q, x = queries_of(t), 0 if kind == "mla" else 1
                dve.wait_ge(s_pv, att_no[n] + 1)
                step(v.reciprocal(inv[0:q, :], total[0:q, t % 2, x, :]), s_step)
                step(v.tensor_tensor(m.oab[0:q, t, x, :].rearrange("p (h c) -> p h c", h=H),
                                     ps_o[0:q, x, :].rearrange("p (h c) -> p h c", h=H),
                                     last(inv[0:q, :], AV), ALU.mult), s_o)

            step(v.memset(biasA[:, :], 0.0), s_step)
            step(v.memset(biasA[0:CHUNK, KPROMPT - CHUNK:], HIDE), s_step)
            for n in range(N + LAG):
                if n < N:
                    t, kind, h = units[n]
                    if kind == "index":
                        index_unit(n)
                        if h == H - 1:
                            hide_ahead(t)
                    else:
                        logits(n)
                        if kind == "mla":
                            choose_some(t, h)
                            if h == H - 1:
                                hide_unchosen(t)
                k = n - LAG
                if k >= 0 and units[k][1] != "index" and units[k][2] == H - 1:
                    normalise(k)


def merge(nc, io, m, sem):
    lo = Plan(nc, m.keep)
    m.x = lo("x", [P, NT, D])
    m.after_x = lo.at
    wo2 = Plan(nc, m.after_x)("wo2", [P, 2, 4, 512])
    assert 2 * 4 * 512 <= DC * NQ
    m.h2t = lo("h2t", [P, DC, NQ])
    mt = lo("mt", [P, DC, NQ])
    pl = Plan(nc, m.after_attend)
    ot = pl("ot", [P, 2, 4, NQ])
    w_out = pl("w_out", [P, 2, DC, 512])
    assert pl.at <= m.end, pl.at
    wo = [Plan(nc, m.low)("wo", [P, 2, 4, 512]), wo2]
    sg = lo("sgm", [P, 2, 2, HALF])
    part = lo("part", [P, 2, HALF])
    xs = lo("xs2", [P, 2, D])
    st = lo("st2", [P, 4])
    ln2 = lo("ln2", [P, DC])
    assert lo.at <= m.temps
    m.after_hs = m.after_x + 3 * DC * NQ * 4
    m.wq0 = Plan(nc, m.after_hs)("wq0", [P, DC, P])
    assert lo.at <= m.after_hs and m.after_hs + DC * P * 4 <= m.temps
    m.s_wq0 = sem("q_wq0")
    ident = m.ident

    with nc.psum_tensor("ps_m", [P, 8, 512], F32) as ps, nc.Block() as block:
        s_x = sem("c_x")
        s_wo = [sem("c_wo0"), sem("c_wo1")]
        s_wout = [sem("c_wout0"), sem("c_wout1")]
        s_ln = sem("c_ln")
        s_ot = sem("c_ot")
        s_otc = sem("c_otc")
        s_z = sem("c_z")
        s_sig = sem("c_sig")
        s_mt = sem("c_mt")
        s_y = sem("c_y")
        s_step = sem("c_step")
        s_res = sem("c_res")
        s_ms = sem("c_ms")
        s_rt = sem("c_rt")
        s_xs = sem("c_xs")
        s_hT = sem("c_hT")
        s_h2 = sem("c_h2")

        @block.sync
        def _(sp):
            for x in range(2):
                sp.dma_start(wo[0][:, x, :, :], io.w_o[0, x, :, :, :]).then_inc(s_wo[0], 16)
            for x in range(2):
                sp.dma_start(wo[1][:, x, :, :], io.w_o[1, x, :, :, :]).then_inc(s_wo[1], 16)
            sp.dma_start(m.x[:, 0:4, :], io.x_prompt[:, :].rearrange("(t p) d -> p t d", p=P)).then_inc(s_x, 16)
            sp.dma_start(m.x[0:DEC, 4, :], io.x_sample[:, :]).then_inc(s_x, 16)
            sp.dma_start(ln2[:, :], io.ln2[:, :]).then_inc(s_ln, 16)
            for c in range(2):
                sp.dma_start(w_out[:, c, :, :], io.w_out[c, :, :, :]).then_inc(s_wout[c], 16)
            sp.dma_start(m.wq0[:, :, :], io.peer_wq[0, :, :, :]).then_inc(m.s_wq0, 16)

        @block.tensor
        def _(pe):
            for t in range(NT):
                q = queries_of(t)
                for x in range(2):
                    n = 2 * t + x
                    if n >= 8:
                        pe.wait_ge(s_otc, n - 7)
                    for c in range(4):
                        ins = nc.tensor.transpose(ps[:, n % 8, P * c:P * c + q], m.oab[0:q, t, x, P * c:P * (c + 1)],
                                                  ident[0:q, 0:q])
                    ins.then_inc(s_ot, 1)
            pe.wait_ge(s_otc, 2 * NT)
            for n in range(2 * DC):
                j, hf = n // 2, n % 2
                b = 2 * (n % 4)
                if n % 8 == 0:
                    pe.wait_ge(s_wo[n // 8], 32)
                if n >= 4:
                    pe.wait_ge(s_mt, n - 3)
                for x in range(2):
                    for k in range(4):
                        ins = nc.tensor.matmul(ps[:, b + x, 0:HALF], wo[j // 4][:, x, k, P * (j % 4):P * (j % 4 + 1)],
                                               ot[:, x, k, HALF * hf:HALF * (hf + 1)], start=(k == 0), stop=(k == 3))
                ins.then_inc(s_z, 1)
            pe.wait_ge(s_mt, 2 * DC)

            def out(t):
                q = queries_of(t)
                for c in range(2):
                    if t == 0:
                        pe.wait_ge(s_wout[c], 16)
                    n = 2 * t + c
                    if n >= 4:
                        pe.wait_ge(s_res, n - 3)
                    for k in range(DC):
                        ins = nc.tensor.matmul(ps[0:q, n % 4, :], mt[:, k, P * t:P * t + q], w_out[:, c, k, :],
                                               start=(k == 0), stop=(k == DC - 1))
                    ins.then_inc(s_y, 1)

            def turn(t):
                q = queries_of(t)
                pe.wait_ge(s_xs, t + 1)
                for c in range(DC):
                    n = 2 * t + c // 4
                    if c % 4 == 0 and n >= 4:
                        pe.wait_ge(s_h2, n - 3)
                    ins = nc.tensor.transpose(ps[:, 4 + n % 4, P * (c % 4):P * (c % 4) + q],
                                              xs[0:q, t % 2, P * c:P * (c + 1)], ident[0:q, 0:q])
                    if c % 4 == 3:
                        ins.then_inc(s_hT, 1)

            out(0)
            for t in range(NT):
                if t + 1 < NT:
                    out(t + 1)
                turn(t)

        @block.scalar
        def _(act):
            for n in range(2 * NT):
                t, x = n // 2, n % 2
                q = queries_of(t)
                act.wait_ge(s_ot, n + 1)
                nc.scalar.copy(ot[:, x, :, P * t:P * t + q],
                               ps[:, n % 8, :].rearrange("p (c k) -> p c k", c=4)[:, :, 0:q]).then_inc(s_otc, 1)
            for n in range(2 * DC):
                if n >= 2:
                    act.wait_ge(s_mt, n - 1)
                nc.scalar.activation(sg[:, n % 2, :, :], m.sg[:, :, n // 2, HALF * (n % 2):HALF * (n % 2 + 1)],
                                     ACT.Sigmoid).then_inc(s_sig, 1)
            for t in range(NT):
                act.wait_ge(s_ms, t + 1)
                nc.scalar.activation(st[:, 2:3], st[:, 1:2], ACT.Sqrt).then_inc(s_rt, 1)

        @block.vector
        def _(dve):
            step = Chain(dve)
            v = nc.vector
            step(v.memset(st[:, :], 1.0), s_step)
            for n in range(2 * DC):
                j, hf = n // 2, n % 2
                dve.wait_ge(s_sig, n + 1)
                dve.wait_ge(s_z, n + 1)
                step(v.tensor_tensor(part[:, :, :], sg[:, n % 2, :, :], ps[:, 2 * (n % 4):2 * (n % 4) + 2, 0:HALF],
                                     ALU.mult), s_step)
                step(v.tensor_tensor(mt[:, j, HALF * hf:HALF * (hf + 1)], part[:, 0, :], part[:, 1, :], ALU.add),
                     s_mt)
            dve.wait_ge(s_x, 32)
            dve.wait_ge(s_ln, 16)
            def residual(t):
                q = queries_of(t)
                for c in range(2):
                    n = 2 * t + c
                    dve.wait_ge(s_y, n + 1)
                    step(v.tensor_tensor(m.x[0:q, t, 512 * c:512 * (c + 1)], ps[0:q, n % 4, :],
                                         m.x[0:q, t, 512 * c:512 * (c + 1)], ALU.add), s_res)

            def norm(t):
                q = queries_of(t)
                if t >= 2:
                    dve.wait_ge(s_hT, 2 * (t - 1))
                step(v.tensor_tensor_reduce(out=xs[0:q, t % 2, :], in0=m.x[0:q, t, :], in1=m.x[0:q, t, :], scale=1.0,
                                            scalar=0.0, op0=ALU.mult, op1=ALU.add, accum_out=st[0:q, 0:1]), s_step)
                v.tensor_scalar(st[:, 1:2], st[:, 0:1], 1.0 / D, EPS, ALU.mult, ALU.add).then_inc(s_ms, 1)
                dve.wait_ge(s_rt, t + 1)
                step(v.reciprocal(st[:, 3:4], st[:, 2:3]), s_step)
                step(v.tensor_scalar(xs[0:q, t % 2, :], m.x[0:q, t, :], st[0:q, 3:4], None, ALU.mult), s_xs)

            def gain(t):
                q = queries_of(t)
                for j in range(2):
                    n = 2 * t + j
                    dve.wait_ge(s_hT, n + 1)
                    v.tensor_tensor(m.h2t[:, 4 * j:4 * j + 4, P * t:P * t + q],
                                    ps[:, 4 + n % 4, :].rearrange("p (c k) -> p c k", c=4)[:, :, 0:q],
                                    last(ln2[:, 4 * j:4 * j + 4], q), ALU.mult).then_inc(s_h2, 1)

            for t in range(NT):
                residual(t)
                norm(t)
                if t:
                    gain(t - 1)
            gain(NT - 1)


TB = 32
NB = NQ // TB
GT = 4
GPB = TB // GT
RING = 2
EG = 4
STEPS = NKEY // EG
HB = (NB // 2 + 1, NB // 2)
HT = (HB[0] * TB, HB[1] * TB)
HOFF = (0, HT[0])
BU = 2 * DC
BPT = P // TB
LEAD = 3
SPT = LEAD + BPT
assert 4 * SPT + LEAD + 1 == STEPS
assert NB * TB == NQ and GPB == 2 * EG and BPT % 2 == 0
THREE = ((0, 0), (0, 1), (1, 0))


def queries(nc, io, m, sem):
    m.qh = Plan(nc, m.low)("qh", [P, PH, NQ])
    lo = Plan(nc, m.after_x)
    lo.at += DC * NQ * 4
    m.hs = lo("hs", [P, 2, DC, NQ], F32R)
    assert lo.at == m.after_hs
    lo.at += DC * P * 4
    wq = [m.wq0] + [lo(f"wq{i}", [P, DC, P]) for i in (1, 2)]
    ahead = Plan(nc, m.end - (EG * DC * P + PH * 2 * NKEY) * 4)
    assert lo.at <= ahead.at, lo.at
    m.keyb_at = ahead.at
    m.keyb = ahead("keyb", [P, PH, 2, NKEY])
    m.raw = ahead("raw", [P, EG, DC, P])
    assert ahead.at <= m.end
    m.s_key = sem("q_key")
    m.s_raw = [sem(f"q_raw{e}") for e in range(EG)]

    with nc.psum_tensor("ps_q", [P, 2, 2, 512], F32) as ps, nc.Block() as block:
        s_wq = [m.s_wq0] + [sem(f"q_wq{i}") for i in (1, 2)]
        s_q = sem("q_q")
        s_zero = sem("q_zero")
        s_qc = sem("q_qc")
        s_high = sem("q_high")
        s_low = sem("q_low")

        @block.sync
        def _(sp):
            for h in range(1, PH):
                if h >= 3:
                    sp.wait_ge(s_q, h - 2)
                sp.dma_start(wq[h % 3][:, :, :], io.peer_wq[h, :, :, :]).then_inc(s_wq[h % 3], 16)
            for e in range(EG):
                sp.dma_start(m.raw[:, e, :, :], io.peer_u[e]).then_inc(m.s_raw[e], 16)

        @block.gpsimd
        def _(pool):
            nc.gpsimd.memset(m.keyb[:, :, :, :], 0.0).then_inc(s_zero, 1)
            pool.wait_ge(s_zero, 1)
            for a in range(2):
                pool.dma_start(m.keyb[HD * a:HD * (a + 1), :, a, :], io.subkeys[a, :, :, :]).then_inc(m.s_key, 16)

        @block.tensor
        def _(pe):
            for h in range(PH):
                pe.wait_ge(s_wq[h % 3], 16 * (h // 3 + 1))
                if h >= 2:
                    pe.wait_ge(s_qc, h - 1)
                for hf in range(2):
                    for k in range(DC):
                        ins = nc.tensor.matmul(ps[:, h % 2, hf, 0:HALF], wq[h % 3][:, k, :],
                                               m.h2t[:, k, HALF * hf:HALF * (hf + 1)],
                                               start=(k == 0), stop=(k == DC - 1))
                ins.then_inc(s_q, 1)

        @block.scalar
        def _(act):
            for h in range(PH):
                act.wait_ge(s_q, h + 1)
                nc.scalar.copy(m.qh[:, h, :].rearrange("p (a k) -> p a k", a=2),
                               ps[:, h % 2, :, 0:HALF]).then_inc(s_qc, 1)

        @block.vector
        def _(dve):
            v = nc.vector
            v.tensor_copy(m.hs[:, 0, :, :], m.h2t[:, :, :]).then_inc(s_high, 1)
            dve.wait_ge(s_high, 1)
            v.tensor_tensor(m.hs[:, 1, :, :], m.h2t[:, :, :], m.hs[:, 0, :, :].bitcast(F32),
                            ALU.subtract).then_inc(s_low, 1)


def retrieve(nc, io, m, sem):
    mid_plan = Plan(nc, m.after_x)
    sc = [mid_plan(f"sc{i}", [P, PH, 2, NKEY]) for i in range(2)]
    work = mid_plan("work", [P, NKEY * 2])
    assert mid_plan.at <= m.after_x + DC * NQ * 4
    pl = Plan(nc, m.after_hs)
    slots = pl("slots", [P, 5, NQ])
    stage = [pl("stage0", [P, NKEY, TB])]
    left = pl("left", [P, RING, GT, 3, NKEY], BF16)
    m.cand_at = pl.at
    cand = pl("cand", [P, PH, TOPE * TOPE])
    hot = cand[:, :, :].rearrange("p h (i j) -> p (h i) j", i=TOPE)
    top = pl("top", [P, PH, TOPE])
    val = pl("val", [P, PH, 2, TOPE])
    ind = pl("ind", [P, PH, 2, TOPE], U32)
    pos = pl("pos", [P, PH, TOPE], U32)
    posb = pl("posb", [P, 2, SLOTS], U32)
    posf = pl("posf", [P, 2, SLOTS])
    indf = pl("indf", [P, PH, 2, TOPE])
    num = pl("num", [P, TOPE])
    pick = pl("pick", [P, 3, SLOTS])
    part = pl("part", [P, P], BF16)
    ssum = pl("ssum", [P, 2, PH])
    right = pl("right", [P, RING, GT, NKEY], BF16)
    stage.append(pl("stage1", [P, NKEY, TB]))
    number = pl("number", [P, NKEY], BF16)
    us = pl("us", [P, 2, 2, DC, P], F32R)
    gel = pl("gel", [P, EG, NQ])
    assert pl.at <= m.keyb_at, pl.at
    keyb, raw = m.keyb, m.raw
    rawv = nc.alloc_sbuf_tensor_at("rawv", [P, EG, D], F32, offset=m.keyb_at + PH * 2 * NKEY * 4)
    m.rawv = rawv
    m.gelv = Plan(nc, m.after_x)("gelv", [P, 2, EG, NQ])
    m.gt = Plan(nc, m.cand_at)("gt", [P, 2, NB, EG, TB])
    assert NB * EG * TB == NQ * EG <= PH * TOPE * (TOPE + 1)
    m.s_rawv = [sem(f"f_raw{e}") for e in range(EG)]
    m.s_in = [sem("f_in0"), sem("f_in1")]
    ident = m.ident
    first_key, second_key, gate_parts = slots[:, 0, :], slots[:, 1, :], [slots[:, 2 + x, :] for x in range(3)]

    with nc.psum_tensor("ps_r", [P, 8, 512], F32) as ps, nc.Block() as block:
        ps_u, ps_s, ps_k, ps_t = ps[:, 0:2, :], ps[:, 2:4, :], ps[:, 4:6, :], ps[:, 6:8, :]
        s_num = sem("d_num")
        s_s = sem("d_s")
        s_sc = sem("d_sc")
        s_used = sem("d_used")
        s_step = sem("d_step")
        s_shift = sem("d_shift")
        s_exp = sem("d_exp")
        s_pick = sem("d_pick")
        s_turn = sem("d_turn")
        s_slot = sem("d_slot")
        s_hot = sem("d_hot")
        s_prod = sem("d_prod")
        s_out = sem("d_out")
        s_store = [sem("d_store0"), sem("d_store1")]
        s_raw = m.s_raw
        s_high = sem("d_high")
        s_split = sem("d_split")
        s_u = sem("d_u")
        s_gelu = sem("d_gelu")
        s_kept = [sem(f"d_kept{e}") for e in range(EG)]

        def schedule(eng, step, after_blocks):
            for t in range(NT):
                s0, b0 = SPT * t, BPT * t
                if t == 0:
                    for s in range(LEAD - 1):
                        step(s, None, 0, None)
                else:
                    with eng.Fori(s0, s0 + LEAD - 1) as s:
                        step(s, None, 0, None)
                step(s0 + LEAD - 1, None, 0, t)
                s0 += LEAD
                if t == 0:
                    for j in range(BPT):
                        step(s0 + j, b0 + j, j % 2, None)
                elif t < NT - 1:
                    with eng.Fori(0, BPT // 2) as i:
                        step(i * 2 + s0, i * 2 + b0, 0, None)
                        step(i * 2 + (s0 + 1), i * 2 + (b0 + 1), 1, None)
                else:
                    step(STEPS - 1, NB - 1, 0, None)
                after_blocks(t)

        @block.sync
        def _(sp):
            def load(s, e):
                src = io.peer_u[s * EG + e] if isinstance(s, int) else io.peer_u[bass.ds(s * EG + e, 1)].squeeze(0)
                sp.dma_start(raw[:, e, :, :], src).then_inc(s_raw[e], 16)

            def store(s, e):
                sp.wait_ge(s_gelu, s * (2 * EG) + 2 * (e + 1))
                dst = io.gelu[s * EG + e] if isinstance(s, int) else io.gelu[bass.ds(s * EG + e, 1)].squeeze(0)
                sp.dma_start(dst, gel[:, e, :]).then_inc(s_kept[e], 16)

            with sp.Fori(0, STEPS - 1) as s:
                for e in range(EG):
                    sp.wait_ge(s_split, s * EG + (e + 1))
                    load(s + 1, e)
                    store(s, e)
            sp.wait_ge(s_pick, NT)
            for e in range(EG):
                sp.wait_ge(s_kept[e], 16 * 2)
            sp.wait_ge(s_store[0], 16 * (NB // 2))
            sp.wait_ge(s_store[1], 16 * (NB // 2))
            sp.dma_start(m.gt[:, 0, 0:NB - 1, :, :].rearrange("p b e t -> p b (e t)"),
                         io.dense[0:NB - 1, :, 0:EG, :].rearrange("b p e t -> p b (e t)")).then_inc(m.s_in[0], 16)
            for s in range(2):
                sp.dma_start(m.gelv[:, s, :, :], io.gelu[EG * s:EG * (s + 1), :, :].rearrange("e p n -> p e n")
                             ).then_inc(m.s_in[s], 16)
            for e in range(EG):
                sp.wait_ge(s_split, EG * (STEPS - 1) + e + 1)
                sp.dma_start(rawv[:, e, :], io.peer_v[:, e, :]).then_inc(m.s_rawv[e], 16)
            for e in range(EG):
                store(STEPS - 1, e)
            for e in range(EG):
                sp.wait_ge(s_kept[e], 16 * STEPS)
            for par in range(2):
                sp.wait_ge(s_store[par], 16 * (NB // 2 + 1 - par))

        @block.gpsimd
        def _(pool):
            g = nc.gpsimd
            g.iota(num[:, :], [[1, TOPE]], base=0, channel_multiplier=0,
                   allow_small_or_imprecise_dtypes=True).then_inc(s_num, 1)
            g.iota(number[:, :], [[1, NKEY]], base=0, channel_multiplier=0,
                   allow_small_or_imprecise_dtypes=True).then_inc(s_num, 1)
            with pool.Fori(0, STEPS) as s:
                for e in range(EG):
                    pool.wait_ge(s_high, s * EG + (e + 1))
                    g.tensor_tensor(us[:, e % 2, 1, :, :], raw[:, e, :, :], us[:, e % 2, 0, :, :].bitcast(F32),
                                    ALU.subtract).then_inc(s_split, 1)

        @block.tensor
        def _(pe):
            def scores(t):
                q = queries_of(t)
                for g in range(4):
                    n = 4 * t + g
                    if n >= 2:
                        pe.wait_ge(s_sc, n - 1)
                    for i in range(2):
                        ins = nc.tensor.matmul(ps_k[0:q, g % 2, 2 * NKEY * i:2 * NKEY * (i + 1)],
                                               m.qh[:, 2 * g + i, P * t:P * t + q],
                                               keyb[:, 2 * g + i, :, :].rearrange("p a k -> p (a k)"),
                                               start=True, stop=True)
                    ins.then_inc(s_s, 1)

            def turn(t):
                q = queries_of(t)
                pe.wait_ge(s_pick, t + 1)
                if t >= 2:
                    pe.wait_ge(s_slot, t - 1)
                for i in range(3):
                    ins = nc.tensor.transpose(ps_t[:, t % 2, P * i:P * i + q], pick[0:q, i, :],
                                              ident[0:q, 0:q])
                ins.then_inc(s_turn, 1)

            def group(b, k):
                pe.wait_ge(s_hot, b * GPB + (k + 1))
                for j in range(GT):
                    for x in range(3):
                        ins = nc.tensor.matmul(ps_s[:, k % 2, NKEY * j:NKEY * (j + 1)], left[:, k % RING, j, x, :],
                                               right[:, k % RING, j, :], start=(x == 0), stop=(x == 2))
                ins.then_inc(s_prod, 1)

            def step(s, b, par, t):
                for e in range(EG):
                    pe.wait_ge(s_split, s * EG + (e + 1))
                    for hf in range(2):
                        if not isinstance(s, int) or EG * s + e:
                            pe.wait_ge(s_gelu, s * (2 * EG) + (2 * e + hf - 1))
                        for k in range(DC):
                            for i, (x, y) in enumerate(THREE):
                                ins = nc.tensor.matmul(ps_u[:, hf, 0:HT[hf]], us[:, e % 2, x, k, :],
                                                       m.hs[:, y, k, HOFF[hf]:HOFF[hf] + HT[hf]],
                                                       start=(k == 0 and i == 0), stop=(k == DC - 1 and i == 2))
                        ins.then_inc(s_u, 1)
                        if b is not None:
                            group(b, 2 * e + hf)
                    if t is not None and e == EG - 2:
                        turn(t)

            pe.wait_ge(m.s_key, 32)
            scores(0)
            scores(1)
            schedule(pe, step, lambda t: scores(t + 2) if t + 2 < NT else None)

        @block.scalar
        def _(act):
            def copy_scores(t):
                q = queries_of(t)
                if t >= 2:
                    act.wait_ge(s_used, t - 1)
                for g in range(4):
                    act.wait_ge(s_s, 4 * t + g + 1)
                    nc.scalar.copy(sc[t % 2][0:q, 2 * g:2 * g + 2, :, :].rearrange("p h a k -> p (h a k)"),
                                   ps_k[0:q, g % 2, :]).then_inc(s_sc, 1)

            def exponentials(t):
                q = queries_of(t)
                act.wait_ge(s_shift, t + 1)
                nc.scalar.activation(top[0:q, :, :], top[0:q, :, :], ACT.Exp).then_inc(s_exp, 1)

            def slot(t):
                q = queries_of(t)
                act.wait_ge(s_turn, t + 1)
                nc.scalar.copy(slots[:, 0:3, P * t:P * t + q],
                               ps_t[:, t % 2, :].rearrange("p (i k) -> p i k", i=4)[:, 0:3, 0:q]
                               ).then_inc(s_slot, 1)

            def high(s, e):
                act.wait_ge(s_raw[e], s * 16 + 16)
                if not isinstance(s, int) or EG * s + e >= 2:
                    act.wait_ge(s_u, s * (2 * EG) + 2 * (e - 1))
                nc.scalar.copy(us[:, e % 2, 0, :, :], raw[:, e, :, :]).then_inc(s_high, 1)

            def step(s, b, par, t):
                for e in range(EG):
                    if e < EG - 1:
                        high(s, e + 1)
                    elif not isinstance(s, int) or s < STEPS - 1:
                        high(s + 1, 0)
                    if not isinstance(s, int) or s:
                        act.wait_ge(s_kept[e], s * 16)
                    if b is not None and e == 0 and (not isinstance(b, int) or b >= 2):
                        act.wait_ge(s_store[par], (b - par) * 8)
                    for hf in range(2):
                        act.wait_ge(s_u, s * (2 * EG) + (2 * e + hf + 1))
                        nc.scalar.activation(gel[:, e, HOFF[hf]:HOFF[hf] + HT[hf]], ps_u[:, hf, 0:HT[hf]],
                                             ACT.Gelu_apprx_tanh).then_inc(s_gelu, 1)
                        if b is not None:
                            k = 2 * e + hf
                            act.wait_ge(s_prod, b * GPB + (k + 1))
                            nc.scalar.copy(stage[par][:, :, GT * k:GT * (k + 1)],
                                           ps_s[:, k % 2, :].rearrange("p (t i) -> p i t", t=GT)
                                           ).then_inc(s_out, 1)
                    if t is not None and e == 0:
                        exponentials(t)
                    if t is not None and e == EG - 2:
                        slot(t)
                if b is not None:
                    act.wait_ge(s_out, b * GPB + GPB)
                    dst = io.dense[b] if isinstance(b, int) else io.dense[bass.ds(b, 1)].squeeze(0)
                    act.dma_start(dst, stage[par][:, :, :]).then_inc(s_store[par], 16)

            high(0, 0)
            copy_scores(0)
            copy_scores(1)
            schedule(act, step, lambda t: copy_scores(t + 2) if t + 2 < NT else None)

        @block.vector
        def _(dve):
            step = Chain(dve)
            v = nc.vector

            def top16(values, where, src, scratch):
                step(v.max(values[:, 0:8], src), s_step)
                v.max_index(where[:, 0:8], values[:, 0:8], src)
                step(v.match_replace(scratch, values[:, 0:8], src, TAKEN), s_step)
                step(v.max(values[:, 8:16], scratch), s_step)
                return v.max_index(where[:, 8:16], values[:, 8:16], scratch)

            def choose(t):
                q = queries_of(t)
                dve.wait_ge(s_sc, 4 * t + 4)
                for h in range(PH):
                    for a in range(2):
                        ins = top16(val[0:q, h, a, :], ind[0:q, h, a, :], sc[t % 2][0:q, h, a, :],
                                    work[0:q, NKEY * a:NKEY * (a + 1)])
                step(ins, s_used)
                c4 = cand[0:q].rearrange("p h (i j) -> p h i j", i=TOPE)
                step(v.tensor_tensor(c4, val[0:q, :, 0, :].unsqueeze(3).to_broadcast([q, PH, TOPE, TOPE]),
                                     val[0:q, :, 1, :].unsqueeze(2).to_broadcast([q, PH, TOPE, TOPE]), ALU.add),
                     s_step)
                for h in range(PH):
                    ins = top16(top[0:q, h, :], pos[0:q, h, :], cand[0:q, h, :], work[0:q, :])
                step(ins, s_step)
                v.tensor_copy(ssum[0:q, 0, :], top[0:q, :, 0])
                step(v.tensor_scalar(posb[0:q, 0, :], pos[0:q].rearrange("p h k -> p (h k)"), 4, None,
                                     ALU.logical_shift_right), s_step)
                v.tensor_tensor(top[0:q], top[0:q], last(ssum[0:q, 0, :], TOPE), ALU.subtract).then_inc(s_shift, 1)
                step(v.tensor_scalar(posb[0:q, 1, :], pos[0:q].rearrange("p h k -> p (h k)"), TOPE - 1, None,
                                     ALU.bitwise_and), s_step)
                v.tensor_copy(posf[0:q], posb[0:q])
                step(v.tensor_copy(indf[0:q], ind[0:q]), s_step)
                if t:
                    dve.wait_ge(s_turn, t)
                out = pick
                hot4 = hot[0:q].rearrange("p (h i) j -> p h i j", h=PH)
                for a in range(2):
                    step(v.tensor_tensor(hot[0:q], last(posf[0:q, a, :], TOPE), mid(num[0:q, :], SLOTS),
                                         ALU.is_equal), s_step)
                    step(v.tensor_tensor(hot4, hot4, indf[0:q, :, a, :].unsqueeze(2).to_broadcast([q, PH, TOPE, TOPE]),
                                         ALU.mult), s_step)
                    step(v.tensor_reduce(out[0:q, a, :], hot[0:q], AX_X, ALU.add), s_step)
                dve.wait_ge(s_exp, t + 1)
                step(v.tensor_reduce(ssum[0:q, 0, :], top[0:q], AX_X, ALU.add), s_step)
                step(v.reciprocal(ssum[0:q, 1, :], ssum[0:q, 0, :]), s_step)
                step(v.tensor_tensor(out[0:q, 2, :].rearrange("p (h k) -> p h k", h=PH), top[0:q],
                                     last(ssum[0:q, 1, :], TOPE), ALU.mult), s_pick)

            def gate_in_parts(t):
                q = queries_of(t)
                here = slice(P * t, P * t + q)
                for x in range(2):
                    gate, rest = gate_parts[x][:, here], gate_parts[x + 1][:, here]
                    step(v.tensor_copy(part[:, 0:q], gate), s_step)
                    step(v.tensor_tensor(rest, gate, part[:, 0:q], ALU.subtract), s_step)
                    step(v.tensor_copy(gate, part[:, 0:q]), s_step)

            def one_hots(b):
                for k in range(GPB):
                    if not isinstance(b, int) or GPB * b + k >= RING:
                        dve.wait_ge(s_out, b * GPB + (k - RING + 1))
                    for j in range(GT):
                        tok = bass.ds(b * TB + (GT * k + j), 1)
                        for x in range(3):
                            ins = v.tensor_scalar(left[:, k % RING, j, x, :], number[:, :], first_key[:, tok],
                                                  gate_parts[x][:, tok], ALU.is_equal, ALU.mult)
                    keys = second_key[:, bass.ds(b * TB + GT * k, GT)]
                    v.tensor_tensor(right[:, k % RING, :, :], mid(number[:, :], GT), last(keys, NKEY),
                                    ALU.is_equal).then_inc(s_hot, 1)

            dve.wait_ge(s_num, 2)
            for t in range(NT):
                choose(t)
                dve.wait_ge(s_slot, t + 1)
                gate_in_parts(t)
                if t == 0:
                    one_hots(0)
                with dve.Fori(max(BPT * t, 1), min(BPT * (t + 1), NB)) as b:
                    one_hots(b)
            dve.wait_ge(s_out, NB * GPB)
            step(v.tensor_copy(m.gt[:, 0, NB - 1, :, :], stage[(NB - 1) % 2][:, 0:EG, :]), s_step)


def experts(nc, io, m, sem):
    m.acc = Plan(nc, m.low)("acc", [P, DC, NQ])
    lo = Plan(nc, m.after_x + 2 * EG * NQ * 4)
    vs = lo("vs", [P, 2, EG, 2, D], F32R)
    assert lo.at <= m.cand_at
    pl = Plan(nc, m.cand_at + 2 * EG * NQ * 4)
    ws = pl("ws", [P, 2, EG, 2, NQ], F32R)
    wf = pl("wf", [P, 2, NQ])
    assert pl.at <= m.keyb_at
    raw, gt, gel = m.rawv, m.gt, m.gelv

    with nc.psum_tensor("ps_b", [P, 8, 512], F32) as ps, nc.Block() as block:
        s_raw, s_in = m.s_rawv, m.s_in
        s_high = sem("f_high")
        s_split = sem("f_split")
        s_full = sem("f_full")
        s_whigh = sem("f_whigh")
        s_w = sem("f_w")
        s_b = sem("f_b")
        s_add = sem("f_add")

        def pairs(eng, body):
            body(0, 0)
            body(1, 1)
            with eng.Fori(0, STEPS // 2 - 1) as i:
                body(i * 2 + 2, 0)
                body(i * 2 + 3, 1)

        @block.sync
        def _(sp):
            def gates(s, par):
                sp.dma_start(gt[:, par, :, :, :].rearrange("p b e t -> p b (e t)"),
                             io.dense[:, :, bass.ds(s * EG, EG), :].rearrange("b p e t -> p b (e t)")
                             ).then_inc(s_in[par], 16)

            def load(s, par):
                if isinstance(s, int) and s == 0:
                    gates(1, 1)
                    return
                for e in range(EG):
                    sp.wait_ge(s_split, s * EG + (e + 1 - EG))
                    src = io.peer_v[:, s * EG + e, :] if isinstance(s, int) else \
                        io.peer_v[:, bass.ds(s * EG + e, 1), :].squeeze(1)
                    sp.dma_start(raw[:, e, :], src).then_inc(s_raw[e], 16)
                if not isinstance(s, int):
                    sp.wait_ge(s_w, s * EG - EG)
                    gates(s, par)
                    sp.dma_start(gel[:, par, :, :], io.gelu[bass.ds(s * EG, EG), :, :].rearrange("e p n -> p e n")
                                 ).then_inc(s_in[par], 16)

            pairs(sp, load)

        @block.gpsimd
        def _(pool):
            def split(s, par):
                for e in range(EG):
                    pool.wait_ge(s_high, s * EG + (e + 1))
                    nc.gpsimd.tensor_tensor(vs[:, par, e, 1, :], raw[:, e, :], vs[:, par, e, 0, :].bitcast(F32),
                                            ALU.subtract).then_inc(s_split, 1)

            pairs(pool, split)

        @block.scalar
        def _(act):
            def high(s, par):
                if not isinstance(s, int):
                    act.wait_ge(s_b, s * BU - BU)
                for e in range(EG):
                    act.wait_ge(s_raw[e], s * 16 + 16)
                    nc.scalar.copy(vs[:, par, e, 0, :], raw[:, e, :]).then_inc(s_high, 1)

            pairs(act, high)

        @block.tensor
        def _(pe):
            def products(s, par):
                for n in range(BU):
                    c, hf = n // 2, n % 2
                    cols = slice(HOFF[hf], HOFF[hf] + HT[hf])
                    if not isinstance(s, int) or BU * s + n >= 8:
                        pe.wait_ge(s_add, s * BU + (n - 7 + 1))
                    for e in range(EG):
                        if n == 0:
                            pe.wait_ge(s_split, s * EG + (e + 1))
                            pe.wait_ge(s_w, s * EG + (e + 1))
                        for i, (x, y) in enumerate(THREE):
                            ins = nc.tensor.matmul(ps[:, n % 8, 0:HT[hf]], vs[:, par, e, x, P * c:P * (c + 1)],
                                                   ws[:, par, e, y, cols], start=(e == 0 and i == 0),
                                                   stop=(e == EG - 1 and i == 2))
                    ins.then_inc(s_b, 1)

            pairs(pe, products)

        @block.vector
        def _(dve):
            v = nc.vector
            def weights(s, par):
                dve.wait_ge(s_in[par], (s - par) * 16 + 32)
                if not isinstance(s, int) or s >= 2:
                    dve.wait_ge(s_b, s * BU - BU)
                for e in range(EG):
                    v.tensor_tensor(wf[:, e % 2, :].rearrange("p (b t) -> p b t", t=TB),
                                    gel[:, par, e, :].rearrange("p (b t) -> p b t", t=TB),
                                    gt[:, par, :, e, :], ALU.mult).then_inc(s_full, 1)
                    dve.wait_ge(s_full, s * EG + (e + 1))
                    v.tensor_copy(ws[:, par, e, 0, :], wf[:, e % 2, :]).then_inc(s_whigh, 1)
                    dve.wait_ge(s_whigh, s * EG + (e + 1))
                    v.tensor_tensor(ws[:, par, e, 1, :], wf[:, e % 2, :], ws[:, par, e, 0, :].bitcast(F32),
                                    ALU.subtract).then_inc(s_w, 1)

            def add(s):
                for n in range(BU):
                    c, hf = n // 2, n % 2
                    cols = slice(HOFF[hf], HOFF[hf] + HT[hf])
                    dve.wait_ge(s_b, s * BU + (n + 1))
                    v.tensor_tensor(m.acc[:, c, cols], ps[:, n % 8, 0:HT[hf]], m.acc[:, c, cols],
                                    ALU.add).then_inc(s_add, 1)

            weights(0, 0)
            v.memset(m.acc[:, :, :], 0.0).then_inc(s_add, 1)
            dve.wait_ge(s_add, 1)
            weights(1, 1)
            add(0)
            with dve.Fori(0, STEPS // 2 - 1) as i:
                weights(i * 2 + 2, 0)
                add(i * 2 + 1)
                weights(i * 2 + 3, 1)
                add(i * 2 + 2)
            add(STEPS - 1)


def finish(nc, io, m, sem):
    with nc.psum_tensor("ps_f", [P, 8, 512], F32) as ps, nc.Block() as block:
        s_t = sem("g_t")
        s_y = sem("g_y")
        s_out = sem("g_out")

        @block.tensor
        def _(pe):
            for n in range(2 * NT):
                t, j = n // 2, n % 2
                q = queries_of(t)
                if n >= 8:
                    pe.wait_ge(s_y, n - 7)
                for c in range(4):
                    ins = nc.tensor.transpose(ps[0:q, n % 8, P * c:P * (c + 1)],
                                              m.acc[:, 4 * j + c, P * t:P * t + q], m.ident[:, :])
                ins.then_inc(s_t, 1)

        @block.vector
        def _(dve):
            for n in range(2 * NT):
                t, j = n // 2, n % 2
                q = queries_of(t)
                dve.wait_ge(s_t, n + 1)
                nc.vector.tensor_tensor(m.x[0:q, t, 512 * j:512 * (j + 1)], ps[0:q, n % 8, :],
                                        m.x[0:q, t, 512 * j:512 * (j + 1)], ALU.add).then_inc(s_y, 1)

        @block.sync
        def _(sp):
            for t in range(NT):
                sp.wait_ge(s_y, 2 * t + 2)
                dst = io.y_prompt[P * t:P * (t + 1), :] if t < 4 else io.y_sample[:, :]
                sp.dma_start(dst, m.x[0:queries_of(t), t, :]).then_inc(s_out, 16)
            sp.wait_ge(s_out, 16 * NT)


class Names:
    pass


def hybrid_step(nc, io):
    m = Names()
    m.end = 229344
    pl = Plan(nc, BASE)
    m.ident = pl("ident", [P, P])
    m.low = pl.at
    m.ht = pl("ht", [P, DC, TOK])
    m.keep = pl.at
    m.kt = pl("kt", [P, H, KEYS])
    m.qt = pl("qt", [P, H, NQ])
    m.biq = pl("biq", [P, H, NQ])
    m.bik = pl("bik", [P, KEYS])
    m.va = pl("va", [P, 7, H, AV])
    m.vb = pl("vb", [P, 7, HD])
    m.iw = pl("iw", [P, NT, H])
    m.temps = pl.at
    sem = nc.alloc_semaphore
    project(nc, io, m, sem)
    attend(nc, io, m, sem)
    merge(nc, io, m, sem)
    queries(nc, io, m, sem)
    retrieve(nc, io, m, sem)
    experts(nc, io, m, sem)
    finish(nc, io, m, sem)


def rotary_tables():
    pos = np.concatenate([META + np.arange(SEQ), PAST + np.arange(DEC), np.arange(META)]).astype(np.float32)
    parts = []
    for rot in (ROPE, BROT):
        half = rot // 2
        inv = np.float32(THETA) ** (-np.arange(half, dtype=np.float32) * np.float32(2.0 / rot))
        ang = pos[:, None] * inv.astype(np.float32)[None, :]
        c, s = np.cos(ang), np.sin(ang)
        parts += [c, c, -s, s]
    flat = np.zeros((NT * P, TABS), np.float32)
    flat[:TOK] = np.concatenate(parts, axis=1)
    return flat.reshape(NT, P, TABS).transpose(1, 0, 2)


def lay_out(x):
    a = {k: np.asarray(v) for k, v in x.items()}
    rows = lambda w: w.reshape(-1, P, w.shape[-1]).transpose(1, 0, 2)
    w_in = a["w_in"][0]
    cut = np.cumsum([QRANK, KVRANK, ROPE, H * HD, HD, HD, H * HD, H, HD, D])
    cq, ckv, kpe, bq, bk, bv, iq, iw, ik, ga, gb = np.split(w_in, cut, axis=1)
    pairs = np.stack([np.concatenate([bq, bk], 1).reshape(D, NPAIR, HD),
                      np.concatenate([iq, ik], 1).reshape(D, NPAIR, HD)], axis=2).reshape(D, -1)
    gate = np.concatenate([ga, gb], 1).reshape(DC, P, 2 * DC, P).transpose(2, 1, 0, 3)
    w_o = np.stack([rows(a["w_o_a"][0]), rows(a["w_o_b"][0])])
    g = a["a_qk_g"][0]
    gains = np.concatenate([a["a_kv_norm_g"][0], g[1, NOPE:], np.tile(a["b_qk_g"][0, 0], H), a["b_qk_g"][0, 1],
                            g[0], g[1, :NOPE]])
    return {
        "x_prompt": a["x_prompt"][0], "x_sample": a["x_sample"][0], "meta_tokens": a["meta_tokens"],
        "w_tok": np.concatenate([cq, ckv, kpe, pairs, bv, iw], 1).reshape(DC, P, 4, PJ).transpose(2, 1, 0, 3),
        "w_gate": gate,
        "tabs": rotary_tables(),
        "gains": np.broadcast_to(gains, (P, GAINS)),
        "ln1": a["ln1_g"][0].reshape(DC, P).T, "ln2": a["ln2_g"][0].reshape(DC, P).T,
        "q_gain": a["a_q_norm_g"][0].reshape(2, P).T,
        "w_uq": rows(a["a_w_uq"][0]), "w_ukv": a["a_w_ukv"][0],
        "lat_t": a["cache_a_latent"][0, 0].T, "cache_kpe": a["cache_a_kpe"][0, 0],
        "bk_t": a["cache_b_k"][0, 0].T, "ik_t": a["cache_b_idx_k"][0, 0].T, "cache_bv": a["cache_b_v"][0, 0],
        "w_o": w_o.reshape(2, P, 4, 2, 512).transpose(3, 0, 1, 2, 4),
        "w_out": rows(a["w_out"][0]).reshape(P, DC, 2, 512).transpose(2, 0, 1, 3),
        "peer_wq": a["peer_wq"][0].reshape(DC, P, PH, P).transpose(2, 1, 0, 3),
        "subkeys": a["peer_subkeys"][0].transpose(1, 3, 0, 2),
        "peer_u": a["peer_u"][0].reshape(NKEY, NKEY, DC, P).transpose(1, 3, 2, 0),
        "peer_v": a["peer_v"][0].reshape(NKEY, NKEY, D),
    }


_OUTS = [("y_prompt", (SEQ, D)), ("y_sample", (DEC, D))]
_OUTS += [(f"new_{s}_{i}", (n, w)) for s, n in (("p", META + SEQ), ("s", DEC))
          for i, w in enumerate((KVRANK, ROPE, HD, HD, HD))]


def kernel(**inputs):
    import concourse.bacc as bacc
    from concourse.bass_utils import run_bass_kernel_spmd

    nc = bacc.Bacc("TRN2", target_bir_lowering=False, num_devices=1)
    io = Names()
    arrays = {}
    for name, a in lay_out(inputs).items():
        a = np.ascontiguousarray(a)
        arrays[f"in_{name}"] = a
        t = nc.dram_tensor(f"in_{name}", a.shape, mybir.dt.from_np(a.dtype), kind="ExternalInput").ap()
        io.__dict__[name] = t
    outs = {}
    for name, shape in _OUTS:
        outs[name] = nc.dram_tensor(f"out_{name}", shape, F32, kind="ExternalOutput").ap()
    io.y_prompt, io.y_sample = outs["y_prompt"], outs["y_sample"]
    io.new_p = [outs[f"new_p_{i}"] for i in range(5)]
    io.new_s = [outs[f"new_s_{i}"] for i in range(5)]
    io.dense = nc.dram_tensor("dense_gates", (NB, P, NKEY, TB), F32, kind="Internal").ap()
    io.gelu = nc.dram_tensor("gelu", (NKEY, P, NQ), F32, kind="Internal").ap()
    hybrid_step(nc, io)
    got = run_bass_kernel_spmd(nc, [arrays], core_ids=[0]).results[0]
    y = [got["out_y_prompt"][None], got["out_y_sample"][None]]
    return tuple(y + [got[f"out_{name}"][None, None] for name, _ in _OUTS[2:]])
```
